# Optimizing a Trainium2 kernel written in Bass

```python
import math
import jax, jax.numpy as jnp
from jax import lax
import numpy as np

D_MODEL = 1024
BATCH = 1
SEQ = 512
DEPTH = 2

N_EVEN = (DEPTH + 1) // 2
N_ODD = DEPTH // 2
EPS = 1e-6
ROPE_THETA = 10000.0
NEG_INF = -1e30
TINY = 1e-30
FORCE_SCORE = 1e9
Q_BLOCK = 128

S5_WIDTH = D_MODEL // 2
S5_GROUP = 16
S5_GROUPS = S5_WIDTH // S5_GROUP
S5_STATE = 64
DT_MIN = 1e-3
DT_MAX = 1e-1

MLA_HEADS = 4
MLA_NOPE = 128
MLA_ROPE = 64
MLA_V = 128
MLA_WIDTH = MLA_HEADS * MLA_V
MLA_KV_RANK = D_MODEL // 4
MLA_Q_RANK = 3 * MLA_KV_RANK
EVEN_SPLITS = (S5_WIDTH, S5_WIDTH, MLA_Q_RANK, MLA_KV_RANK, MLA_ROPE, MLA_WIDTH)
EVEN_IN = sum(EVEN_SPLITS)
EVEN_MIX = S5_WIDTH + MLA_WIDTH

NSA_HEADS = 8
NSA_GROUPS = 2
NSA_REP = NSA_HEADS // NSA_GROUPS
NSA_DIM = 128
NSA_WIDTH = NSA_HEADS * NSA_DIM
NSA_KV = NSA_GROUPS * NSA_DIM
CMP_LEN = 32
CMP_STRIDE = 16
CMP_HIDDEN = 256
SEL_BLOCK = 64
SEL_TOP = 16
SEL_Q_CHUNK = 32
WINDOW = 512
ODD_SPLITS = (NSA_WIDTH, NSA_KV, NSA_KV, NSA_KV, NSA_KV, NSA_KV, NSA_KV, 3 * NSA_HEADS, NSA_WIDTH)
ODD_IN = sum(ODD_SPLITS)

kernel_name = 'hybrid_s5_mla_nsa_adaln_trunk'

def _split(x, sizes):
    bounds = [int(v) for v in np.cumsum(sizes)[:-1]]
    return jnp.split(x, bounds, axis=-1)

def rms_norm(x, g):
    xf = x.astype(jnp.float32)
    y = xf * lax.rsqrt(jnp.mean(xf * xf, axis=-1, keepdims=True) + EPS)
    return (y * g.astype(jnp.float32)).astype(x.dtype)

def rope(x, pos):
    half = x.shape[-1] // 2
    inv_freq = ROPE_THETA ** (-jnp.arange(half, dtype=jnp.float32) / half)
    ang = pos.astype(jnp.float32)[..., None] * inv_freq
    ang = ang.reshape(ang.shape[:2] + (1,) * (x.ndim - 3) + (half,))
    cos, sin = jnp.cos(ang), jnp.sin(ang)
    xf = x.astype(jnp.float32)
    x1, x2 = xf[..., :half], xf[..., half:]
    return jnp.concatenate([x1 * cos - x2 * sin, x2 * cos + x1 * sin], axis=-1).astype(x.dtype)

def masked_probs(scores, mask):
    s = jnp.where(mask, scores.astype(jnp.float32), NEG_INF)
    m = jnp.max(s, axis=-1, keepdims=True)
    e = jnp.where(mask, jnp.exp(s - m), 0.0)
    return e / jnp.maximum(jnp.sum(e, axis=-1, keepdims=True), TINY)

def modulation(c, w_ada, b_ada):
    mod = (jax.nn.silu(c) @ w_ada + b_ada)[:, None, :]
    shift, scale, gate = jnp.split(mod, 3, axis=-1)
    return shift, scale, gate

def _diag_combine(left, right):
    a1r, a1i, b1r, b1i = left
    a2r, a2i, b2r, b2i = right
    return (a2r * a1r - a2i * a1i, a2r * a1i + a2i * a1r,
            a2r * b1r - a2i * b1i + b2r, a2r * b1i + a2i * b1r + b2i)

def s5_mixer(u, lam_re, lam_im, log_dt, b_re, b_im, c_re, c_im, d_skip, w_glu, b_glu):
    bsz, seq, _ = u.shape
    f32 = jnp.float32
    lr, li = lam_re.astype(f32), lam_im.astype(f32)
    dt = jnp.exp(log_dt.astype(f32))[:, None]
    decay = jnp.exp(lr * dt)
    ab_re, ab_im = decay * jnp.cos(li * dt), decay * jnp.sin(li * dt)
    den = lr * lr + li * li
    nr, ni = ab_re - 1.0, ab_im
    f_re = (nr * lr + ni * li) / den
    f_im = (ni * lr - nr * li) / den
    br, bi = b_re.astype(f32), b_im.astype(f32)
    bb_re = f_re[..., None] * br - f_im[..., None] * bi
    bb_im = f_re[..., None] * bi + f_im[..., None] * br
    uf = u.astype(f32).reshape(bsz, seq, S5_GROUPS, S5_GROUP)
    bu_re = jnp.einsum('bsgh,gph->sbgp', uf, bb_re)
    bu_im = jnp.einsum('bsgh,gph->sbgp', uf, bb_im)
    a_re = jnp.broadcast_to(ab_re[None, None], (seq, 1, S5_GROUPS, S5_STATE))
    a_im = jnp.broadcast_to(ab_im[None, None], (seq, 1, S5_GROUPS, S5_STATE))
    _, _, xr, xi = lax.associative_scan(_diag_combine, (a_re, a_im, bu_re, bu_im), axis=0)
    y = (jnp.einsum('sbgp,ghp->bsgh', xr, c_re.astype(f32))
         - jnp.einsum('sbgp,ghp->bsgh', xi, c_im.astype(f32)))
    y = (y + d_skip.astype(f32) * uf).reshape(bsz, seq, S5_WIDTH)
    g = jax.nn.gelu(y)
    out = g * jax.nn.sigmoid(g @ w_glu.astype(f32) + b_glu.astype(f32))
    return out.astype(u.dtype)

def mla_mixer(c_q, c_kv, k_pe, pos, q_norm_g, kv_norm_g, w_uq, w_ukv):
    bsz, seq, _ = c_q.shape
    q = (rms_norm(c_q, q_norm_g) @ w_uq).reshape(bsz, seq, MLA_HEADS, MLA_NOPE + MLA_ROPE)
    q_nope, q_pe = q[..., :MLA_NOPE], rope(q[..., MLA_NOPE:], pos)
    kv = (rms_norm(c_kv, kv_norm_g) @ w_ukv).reshape(bsz, seq, MLA_HEADS, MLA_NOPE + MLA_V)
    k_nope, v = kv[..., :MLA_NOPE], kv[..., MLA_NOPE:]
    k_pe = rope(k_pe, pos)
    scale = (MLA_NOPE + MLA_ROPE) ** -0.5
    nb = seq // Q_BLOCK
    qn = q_nope.reshape(bsz, nb, Q_BLOCK, MLA_HEADS, MLA_NOPE).transpose(1, 0, 2, 3, 4)
    qp = q_pe.reshape(bsz, nb, Q_BLOCK, MLA_HEADS, MLA_ROPE).transpose(1, 0, 2, 3, 4)
    k_idx = jnp.arange(seq)

    def block(args):
        qn_b, qp_b, start = args
        s = (jnp.einsum('bqhd,bkhd->bhqk', qn_b, k_nope)
             + jnp.einsum('bqhd,bkd->bhqk', qp_b, k_pe)) * scale
        mask = k_idx[None, :] <= (start + jnp.arange(Q_BLOCK))[:, None]
        p = masked_probs(s, mask)
        return jnp.einsum('bhqk,bkhd->bqhd', p.astype(v.dtype), v)

    o = lax.map(block, (qn, qp, jnp.arange(nb) * Q_BLOCK))
    return o.transpose(1, 0, 2, 3, 4).reshape(bsz, seq, MLA_WIDTH)

def even_mixer(h, pos, w_in, lam_re, lam_im, log_dt, b_re, b_im, c_re, c_im, d_skip,
               w_glu, b_glu, q_norm_g, kv_norm_g, w_uq, w_ukv, w_out):
    u, z_a, c_q, c_kv, k_pe, z_b = _split(h @ w_in, EVEN_SPLITS)
    y_a = s5_mixer(u, lam_re, lam_im, log_dt, b_re, b_im, c_re, c_im, d_skip, w_glu, b_glu) * jax.nn.silu(z_a)
    y_b = mla_mixer(c_q, c_kv, k_pe, pos, q_norm_g, kv_norm_g, w_uq, w_ukv) * jax.nn.silu(z_b)
    return jnp.concatenate([y_a, y_b], axis=-1) @ w_out

def _compress(kv, tok, pe, w1, w2):
    bsz, seq, _ = kv.shape
    n_cmp = tok.shape[0]
    blk = kv.reshape(bsz, seq, NSA_GROUPS, NSA_DIM)[:, tok]
    blk = blk + pe[None, None, :, None, :]
    blk = blk.transpose(0, 1, 3, 2, 4).reshape(bsz, n_cmp, NSA_GROUPS, CMP_LEN * NSA_DIM)
    return jax.nn.gelu(blk @ w1) @ w2

def _to_blocks(t, block):
    b, g, r, s, d = t.shape
    return t.reshape(b, g, r, s // block, block, d).transpose(3, 0, 1, 2, 4, 5)

def _from_blocks(t):
    nb, b, g, r, blk, d = t.shape
    return t.transpose(1, 2, 3, 0, 4, 5).reshape(b, g, r, nb * blk, d)

def nsa_mixer(h, pos, w_in, cmp_k_pe, cmp_k_w1, cmp_k_w2, cmp_v_pe, cmp_v_w1, cmp_v_w2, w_out):
    bsz, seq, _ = h.shape
    G, R, d = NSA_GROUPS, NSA_REP, NSA_DIM
    q, k_c, v_c, k_s, v_s, k_w, v_w, gate_logits, z = _split(h @ w_in, ODD_SPLITS)
    scale = d ** -0.5
    q = rope(q.reshape(bsz, seq, NSA_HEADS, d), pos)
    qg = q.reshape(bsz, seq, G, R, d).transpose(0, 2, 3, 1, 4)
    q_idx = jnp.arange(seq)

    n_cmp = (seq - CMP_LEN) // CMP_STRIDE + 1
    starts = jnp.arange(n_cmp) * CMP_STRIDE
    tok = starts[:, None] + jnp.arange(CMP_LEN)[None, :]
    end_pos = starts + CMP_LEN - 1
    kc = rope(_compress(k_c, tok, cmp_k_pe, cmp_k_w1, cmp_k_w2), pos[:, end_pos])
    vc = _compress(v_c, tok, cmp_v_pe, cmp_v_w1, cmp_v_w2)
    p_cmp = masked_probs(jnp.einsum('bgrqd,bngd->bgrqn', qg, kc) * scale,
                         end_pos[None, :] <= q_idx[:, None])
    o_cmp = jnp.einsum('bgrqn,bngd->bgrqd', p_cmp.astype(vc.dtype), vc)

    n_sel = seq // SEL_BLOCK
    ratio = SEL_BLOCK // CMP_STRIDE
    n_top = min(SEL_TOP, n_sel)
    imp = jnp.pad(p_cmp.sum(axis=2), ((0, 0), (0, 0), (0, 0), (0, n_sel * ratio - n_cmp)))
    imp = imp.reshape(bsz, G, seq, n_sel, ratio).sum(axis=-1)
    blk_id = jnp.arange(n_sel)[None, :]
    cur = (q_idx // SEL_BLOCK)[:, None]
    forced = (blk_id == 0) | (blk_id == cur) | (blk_id == cur - 1)
    imp = jnp.where(forced, FORCE_SCORE, jnp.where(blk_id <= cur, imp, -1.0))
    _, sel_idx = lax.top_k(imp, n_top)
    k_s = rope(k_s.reshape(bsz, seq, G, d), pos)
    ks_blk = k_s.reshape(bsz, n_sel, SEL_BLOCK, G, d).transpose(0, 3, 1, 2, 4)
    vs_blk = v_s.reshape(bsz, n_sel, SEL_BLOCK, G, d).transpose(0, 3, 1, 2, 4)
    n_qc = seq // SEL_Q_CHUNK
    idx_ch = sel_idx.reshape(bsz, G, n_qc, SEL_Q_CHUNK, n_top).transpose(2, 0, 1, 3, 4)
    b_i = jnp.arange(bsz)[:, None, None, None]
    g_i = jnp.arange(G)[None, :, None, None]
    n_key = n_top * SEL_BLOCK

    def sel_chunk(args):
        q_b, idx_b, start = args
        kk = ks_blk[b_i, g_i, idx_b].reshape(bsz, G, SEL_Q_CHUNK, n_key, d)
        vv = vs_blk[b_i, g_i, idx_b].reshape(bsz, G, SEL_Q_CHUNK, n_key, d)
        key_pos = (idx_b[..., None] * SEL_BLOCK + jnp.arange(SEL_BLOCK)).reshape(bsz, G, SEL_Q_CHUNK, n_key)
        mask = key_pos <= (start + jnp.arange(SEL_Q_CHUNK))[None, None, :, None]
        p = masked_probs(jnp.einsum('bgrqd,bgqkd->bgrqk', q_b, kk) * scale, mask[:, :, None])
        return jnp.einsum('bgrqk,bgqkd->bgrqd', p.astype(vv.dtype), vv)

    o_sel = _from_blocks(lax.map(sel_chunk, (_to_blocks(qg, SEL_Q_CHUNK), idx_ch,
                                             jnp.arange(n_qc) * SEL_Q_CHUNK)))

    pad = ((0, 0), (WINDOW, 0), (0, 0), (0, 0))
    kw_p = jnp.pad(rope(k_w.reshape(bsz, seq, G, d), pos), pad)
    vw_p = jnp.pad(v_w.reshape(bsz, seq, G, d), pad)
    span = WINDOW + Q_BLOCK

    def win_block(args):
        q_b, start = args
        kk = lax.dynamic_slice_in_dim(kw_p, start, span, axis=1)
        vv = lax.dynamic_slice_in_dim(vw_p, start, span, axis=1)
        key_pos = start - WINDOW + jnp.arange(span)
        diff = (start + jnp.arange(Q_BLOCK))[:, None] - key_pos[None, :]
        mask = (diff >= 0) & (diff < WINDOW) & (key_pos[None, :] >= 0)
        p = masked_probs(jnp.einsum('bgrqd,bkgd->bgrqk', q_b, kk) * scale, mask)
        return jnp.einsum('bgrqk,bkgd->bgrqd', p.astype(vv.dtype), vv)

    o_win = _from_blocks(lax.map(win_block, (_to_blocks(qg, Q_BLOCK), jnp.arange(seq // Q_BLOCK) * Q_BLOCK)))

    gates = jax.nn.sigmoid(gate_logits.reshape(bsz, seq, G, R, 3)).transpose(0, 2, 3, 1, 4)[..., None]
    o = gates[..., 0, :] * o_cmp + gates[..., 1, :] * o_sel + gates[..., 2, :] * o_win
    o = o.transpose(0, 3, 1, 2, 4).reshape(bsz, seq, NSA_WIDTH)
    return (o * jax.nn.silu(z)) @ w_out

def setup_inputs(seed: int = 0) -> dict:
    key = jax.random.key(seed)
    keys = iter(jax.random.split(key, 64))

    def nrm(shape, std):
        return std * jax.random.normal(next(keys), shape, jnp.float32)

    def gain(shape):
        return 1.0 + nrm(shape, 0.02)

    ne, no = N_EVEN, N_ODD
    G, P, H = S5_GROUPS, S5_STATE, S5_GROUP
    return {
        'x': nrm((BATCH, SEQ, D_MODEL), 1.0),
        'c': nrm((BATCH, D_MODEL), 1.0),
        'positions': jnp.broadcast_to(jnp.arange(SEQ, dtype=jnp.int32), (BATCH, SEQ)),
        'pre_norm_g': gain((DEPTH, D_MODEL)),
        'post_norm_g': gain((DEPTH, D_MODEL)),
        'w_ada': nrm((DEPTH, D_MODEL, 3 * D_MODEL), 0.5 * D_MODEL ** -0.5),
        'b_ada': nrm((DEPTH, 3 * D_MODEL), 0.01),
        'ev_w_in': nrm((ne, D_MODEL, EVEN_IN), D_MODEL ** -0.5),
        'ev_lam_re': -0.5 + nrm((ne, G, P), 0.01),
        'ev_lam_im': math.pi * jnp.arange(P, dtype=jnp.float32) + nrm((ne, G, P), 0.01),
        'ev_log_dt': jax.random.uniform(next(keys), (ne, G), jnp.float32, math.log(DT_MIN), math.log(DT_MAX)),
        'ev_b_re': nrm((ne, G, P, H), (2 * H) ** -0.5),
        'ev_b_im': nrm((ne, G, P, H), (2 * H) ** -0.5),
        'ev_c_re': nrm((ne, G, H, P), P ** -0.5),
        'ev_c_im': nrm((ne, G, H, P), P ** -0.5),
        'ev_d_skip': nrm((ne, G, H), 1.0),
        'ev_w_glu': nrm((ne, S5_WIDTH, S5_WIDTH), S5_WIDTH ** -0.5),
        'ev_b_glu': nrm((ne, S5_WIDTH), 0.01),
        'ev_q_norm_g': gain((ne, MLA_Q_RANK)),
        'ev_kv_norm_g': gain((ne, MLA_KV_RANK)),
        'ev_w_uq': nrm((ne, MLA_Q_RANK, MLA_HEADS * (MLA_NOPE + MLA_ROPE)), MLA_Q_RANK ** -0.5),
        'ev_w_ukv': nrm((ne, MLA_KV_RANK, MLA_HEADS * (MLA_NOPE + MLA_V)), MLA_KV_RANK ** -0.5),
        'ev_w_out': nrm((ne, EVEN_MIX, D_MODEL), EVEN_MIX ** -0.5),
        'od_w_in': nrm((no, D_MODEL, ODD_IN), D_MODEL ** -0.5),
        'od_cmp_k_pe': nrm((no, CMP_LEN, NSA_DIM), 0.02),
        'od_cmp_k_w1': nrm((no, CMP_LEN * NSA_DIM, CMP_HIDDEN), (CMP_LEN * NSA_DIM) ** -0.5),
        'od_cmp_k_w2': nrm((no, CMP_HIDDEN, NSA_DIM), CMP_HIDDEN ** -0.5),
        'od_cmp_v_pe': nrm((no, CMP_LEN, NSA_DIM), 0.02),
        'od_cmp_v_w1': nrm((no, CMP_LEN * NSA_DIM, CMP_HIDDEN), (CMP_LEN * NSA_DIM) ** -0.5),
        'od_cmp_v_w2': nrm((no, CMP_HIDDEN, NSA_DIM), CMP_HIDDEN ** -0.5),
        'od_w_out': nrm((no, NSA_WIDTH, D_MODEL), NSA_WIDTH ** -0.5),
    }

def reference(x, c, positions, pre_norm_g, post_norm_g, w_ada, b_ada,
              ev_w_in, ev_lam_re, ev_lam_im, ev_log_dt, ev_b_re, ev_b_im, ev_c_re, ev_c_im,
              ev_d_skip, ev_w_glu, ev_b_glu, ev_q_norm_g, ev_kv_norm_g, ev_w_uq, ev_w_ukv, ev_w_out,
              od_w_in, od_cmp_k_pe, od_cmp_k_w1, od_cmp_k_w2, od_cmp_v_pe, od_cmp_v_w1, od_cmp_v_w2,
              od_w_out):
    for layer in range(DEPTH):
        shift, scale, gate = modulation(c, w_ada[layer], b_ada[layer])
        h = rms_norm(x, pre_norm_g[layer]) * (1.0 + scale) + shift
        i = layer // 2
        if layer % 2 == 0:
            y = even_mixer(h, positions, ev_w_in[i], ev_lam_re[i], ev_lam_im[i], ev_log_dt[i],
                           ev_b_re[i], ev_b_im[i], ev_c_re[i], ev_c_im[i], ev_d_skip[i],
                           ev_w_glu[i], ev_b_glu[i], ev_q_norm_g[i], ev_kv_norm_g[i],
                           ev_w_uq[i], ev_w_ukv[i], ev_w_out[i])
        else:
            y = nsa_mixer(h, positions, od_w_in[i], od_cmp_k_pe[i], od_cmp_k_w1[i], od_cmp_k_w2[i],
                          od_cmp_v_pe[i], od_cmp_v_w1[i], od_cmp_v_w2[i], od_w_out[i])
        x = x + gate * rms_norm(y, post_norm_g[layer])
    return x


_drawn_inputs = setup_inputs


def setup_inputs(seed=0):
    import zlib

    import numpy as np

    out = dict(_drawn_inputs(seed))
    spreads = {}
    factors = {'pre_norm_g': 5.124,
     'post_norm_g': 6.824,
     'b_ada': 3.222,
     'ev_lam_re': 200.0,
     'ev_lam_im': 2.674,
     'ev_log_dt': 2.993,
     'ev_b_re': 11.66,
     'ev_b_im': 11.753,
     'ev_c_re': 12.437,
     'ev_c_im': 12.002,
     'ev_b_glu': 21.794,
     'ev_q_norm_g': 8.0,
     'ev_kv_norm_g': 8.0,
     'od_cmp_k_pe': 8.0,
     'od_cmp_v_pe': 52.29}
    for name, (base, spread) in spreads.items():
        noise = np.random.default_rng([zlib.crc32(name.encode()), seed]).standard_normal(out[name].shape)
        drawn = base * np.exp(spread * noise) if base else spread * noise
        out[name] = __import__('jax').numpy.asarray(drawn.astype(out[name].dtype))
    for name, factor in factors.items():
        out[name] = (out[name] * factor).astype(out[name].dtype)
    return out
```

```python
import concourse.bass as bass
from concourse import mybir
from contextlib import ExitStack
import math
import numpy as np

F32 = mybir.dt.float32
I32 = mybir.dt.int32
ALU = mybir.AluOpType
ACT = mybir.ActivationFunctionType
AX = mybir.AxisListType

P = 128
S = 512
NT = S // P
D = 1024
KD = D // P
EPS = 1e-6
TINY = 1e-30
NEG = -1e30
W5 = 512
NG, NH, NP_ = 32, 16, 64
L = 8
NC = S // L
TAPS = L + 1
MH, NOPE, RO, MV = 4, 128, 64, 128
QR, KVR = 768, 256
EV_CQ, EV_KPE, EV_ZB = 2 * W5, 2 * W5 + QR + KVR, 2 * W5 + QR + KVR + RO
MSCALE = (NOPE + RO) ** -0.5
HN, GN, REP, DN = 8, 2, 4, 128
NW = HN * DN
OD_KC, OD_VC, OD_KS, OD_VS, OD_KW, OD_VW = (NW + i * GN * DN for i in range(6))
OD_GATE = NW + 6 * GN * DN
OD_Z = OD_GATE + 3 * HN
NSCALE = DN ** -0.5
CL, CS, CH = 32, 16, 256
NCMP = (S - CL) // CS + 1
SLOT = 2048
RING = 4
C_GELU = math.sqrt(2.0 / math.pi)
PI_SAFE = 3.1415925
MAGIC = 12582912.0
TWO_PI = 2 * math.pi
PI_A = 6.28125
PI_B = float(np.float32(TWO_PI - 6.28125))
PI_C = TWO_PI - PI_A - PI_B

V_C, V_PRE, V_BADA, V_POST, V_QN, V_KVN, V_BGLU, V_DSK, V_N = 0, 8, 24, 72, 88, 94, 96, 100, 104

SEMS = """w_loaded0 w_loaded1 w_loaded2 w_loaded3 vec_loaded const_loaded pos_loaded x_loaded lam_loaded
s5_loaded small_w_loaded ident_ready masks_ready pool_chain dve_chain act_chain colT_done col_ready sc_ready
mod_done mod_ready ssq_done msq_done rstd_ready xn_ready xT_done hT_act tab_abs tab_sin tab_cos
lam_exp lam_red lam_sin pw_ready stT_done st_act CT_done C_act BB_done B_ready GT_done GT_act
Kc_done Kc_act T_zero T_stored W1_ready G_ready
pj_done pj_act th_act z_pool u_stored u_back V_done z_dve zero_ready
Xs_ready Y_done Y_act y_stored y_back y_skip y_sq y_arg y_tanh y_gelu glu_done glu_act ya_ready
cq_msq cq_rstd cq_scaled cqT_done cqT_act q_done q_act kv_done kv_act rope_done
s_done s_max s_exp s_scaled pt_done pt_act pt_dve o_dve out_done out_sq out_msq out_rstd out_gpg gpg_done gpg_ready
out_res kc_ready hid_done hid_tanh hid_sq hid_arg hid_ready cmp_done cmp_act cmp_rope cs_done cs_sub cs_exp cs_scaled
cpt_done cpt_act gate_act gate_ready stored v_act rope1 hT_dve pv_done rot_ready r8_ready wo_used w1_used""".split()


def build_trunk(nc, t):
    with ExitStack() as ctx:
        def sb(name, shape, dt=F32):
            return ctx.enter_context(nc.sbuf_tensor(name, shape, dt))

        sem = {n: ctx.enter_context(nc.semaphore(n)) for n in SEMS}
        bank = [ctx.enter_context(nc.psum_tensor(f"bank{i}", [P, 512], F32)) for i in range(8)]

        ident = sb("ident", [P, P])
        swap = sb("swap", [P, P])
        identb = sb("identb", [P, P], mybir.dt.bfloat16)
        cmaskb = sb("cmaskb", [P, P], mybir.dt.bfloat16)
        cmpmask = sb("cmpmask", [P, NT, NCMP])
        valid = sb("valid", [P, NT])
        rows = sb("rows", [P, P])
        perows = sb("perows", [2 * CL, DN])
        peT = sb("peT", [P, 2 * CL])
        col = sb("col", [P, V_N])
        cst = sb("cst", [P, 4])
        mod = sb("mod", [P, 2, 24])
        pre = sb("pre", [P, 2, KD])
        gcol = sb("gcol", [P, 2, KD])
        sc = sb("sc", [P, KD])
        sct = sb("sct", [P, KD])
        hbg = sb("hbg", [P, 4])
        st1 = sb("st1", [P, 64])
        smax, ssum, srec = sb("smax", [P, 4]), sb("ssum", [P, 4]), sb("srec", [P, 4])
        halfpi = sb("halfpi", [P, 1])
        neghalf = sb("neghalf", [P, 8])
        tabM = sb("tabM", [P, 2, S])
        gpg = sb("gpg", [P, D])
        xr = sb("xr", [P, NT, D])
        hT = sb("hT", [P, KD, S])
        ring = sb("ring", [P, RING, SLOT])
        wkpe = sb("wkpe", [P, KD, P])
        wgate = sb("wgate", [P, KD, 3 * HN])
        w2 = sb("w2", [P, 2, 2, DN])
        ARENA = (nc.sbuf_bytes_remaining() if callable(nc.sbuf_bytes_remaining) else nc.sbuf_bytes_remaining) // 4 - 40
        arena = sb("arena", [P, ARENA])
        top = [0]

        def at(off, *shape):
            n = int(np.prod(shape))
            assert off + n <= ARENA, (off + n, ARENA)
            v = arena[:, off:off + n]
            if len(shape) == 2:
                v = v.rearrange("p (a b) -> p a b", a=shape[0])
            if len(shape) == 3:
                v = v.rearrange("p (a b c) -> p a b c", a=shape[0], b=shape[1])
            return v

        oW1, oGT = 0, 4608
        oROT = oGT + 4096
        oD = oROT + 4096
        oT = oD + 3200
        oH = oT + 4608
        oU = oH + 4768
        W1 = at(oW1, NG, TAPS * NH)
        GT = at(oGT, NG, P)
        rotc, rots = at(oROT, NG, NC), at(oROT + 2048, NG, NC)
        Gc = [at(oD, 8, P), at(oD + 1024, 8, P)]
        tmpG = at(oD + 2048, 8, TAPS * NH)
        TP = at(oT, NG, P)
        NPW = 2 * TAPS + 2 * L + 2 * L + 3
        small = at(oT, NPW + 18, NP_)
        iP, iF, iC, iX = 0, 2 * TAPS, 2 * TAPS + 2 * L, 2 * TAPS + 4 * L
        st = at(oH, NPW, NG)
        BA, BB = at(oH + 1696, NG, NH), at(oH + 2208, NG, NH)
        Bb, iBb = at(oH + 2720, NG, NH), at(oH + 3232, NG, NH)
        C1, C2 = at(oH + 3744, NG, NH), at(oH + 4256, NG, NH)
        CN = Gc[0].rearrange("p a b -> p (a b)")[:, 0:512].rearrange("p (a b) -> p a b", a=4)
        U = at(oH, NG, NC)
        zb5, tb5 = at(oH + 2048, 16, NC), at(oH + 3072, 16, NC)
        Xs = at(oD, 16, NC + 1)
        r8b = at(oD + 1040, NG, NC)
        Kh = at(oU + 2048, 16, P)
        uTp = at(oU, 4, S)
        zaT = at(oU + 2048, 4, S)
        th = at(oU + 4096, 2, S)
        kpT = at(oU + 5120, S)
        Yb = at(oGT, NG, NC)
        yT, y2 = at(oGT + 2048, 4, S), at(oROT, 4, S)
        cqt = xr
        cqT, ckvT = at(0, 6, S), at(3072, 2, S)
        qnT = at(oROT + 2048, 4, S)
        qpT = at(oD, 2, S)
        knT, vM = at(oT, 4, S), at(oT + 2048, NT, 4 * MV)
        zbT = at(oH, 4, S)
        mixT = at(oGT, KD, S)
        Pm, PT = at(oD + 1024, 3, S), at(oH + 2048, 2, S)
        rtmp = at(oH + 3072, 2, S)
        ra, rk = at(oU + 2048, S), at(oU + 2560, S)
        posb = at(oU + 3072, S)
        posi = posb.bitcast(I32)
        otmp = at(0, 2, D)
        tabN = at(0, 4, S)
        qT, ksT, kwT = at(2048, HN, S), at(6144, GN, S), at(7168, GN, S)
        vs, vw = at(8192, NT, GN * DN), at(9216, NT, GN * DN)
        R = [at(10240, CL, GN, NCMP), at(10240 + 1984, CL, GN, NCMP)]
        PcT = at(10240, HN, S)
        zT = at(14336, HN, S)
        Pc = [at(18432, 16, NCMP), at(18928, 16, NCMP)]
        hid, hsq = [at(19424, 2, 62), at(19548, 2, 62)], [at(19672, 2, 62), at(19796, 2, 62)]
        kcT, kct = at(19920, GN, NCMP), at(19982, 2, 62)
        vc = at(20106, GN, DN)
        gates = at(20362, NT, 3 * HN)
        cstat = at(20458, 4, 16)
        Pm1, PT1 = at(20592, 3, S), at(22128, 2, S)
        rt1, th1 = at(23152, 2, S), at(24176, 2, S)
        mix1 = at(25200, KD, S)
        xn1 = at(25200, NT, D)
        otmp1 = at(2048, 2, D)
        assert oU + 5632 <= ARENA, (oU + 5632, ARENA)

        def cols(w, r0, nk, c0, c1):
            return w[r0:r0 + nk * P, c0:c1].rearrange("(k p) n -> p k n", p=P)

        ev_in, od_in = t["ev_w_in"][0], t["od_w_in"][0]
        loads = []

        def use(key, pieces, shape):
            loads.append((key, pieces, shape))

        def ada(l):
            for j in range(12):
                use(("ada", l, j), [(slice(0, 256), cols(t["w_ada"][l], 0, KD, 256 * j, 256 * j + 256))], (KD, 256))

        def colchunks(key, w, c0, n, r0=0, nk=KD):
            for j in range(n // 256):
                use((key, j), [(slice(0, 256), cols(w, r0, nk, c0 + 256 * j, c0 + 256 * j + 256))], (nk, 256))

        ada(0)
        colchunks("u", ev_in, 0, 512)
        colchunks("cq", ev_in, EV_CQ, 1024)
        colchunks("za", ev_in, W5, 512)
        ada(1)
        colchunks("zb", ev_in, EV_ZB, 512)
        colchunks("glu", t["ev_w_glu"][0], 0, 512, nk=4)
        uq = t["ev_w_uq"][0]
        for h in range(0, MH, 2):
            for e in range(2):
                use(("uqn", h + e), [(slice(0, P), cols(uq, 0, 6, (h + e) * 192, (h + e) * 192 + P))], (6, P))
            use(("uqp", h // 2), [(slice(64 * e, 64 * e + 64), cols(uq, 0, 6, (h + e) * 192 + P, (h + e) * 192 + 192)) for e in range(2)], (6, P))
        use(("ukv", 0), [(slice(0, 1024), cols(t["ev_w_ukv"][0], 0, 2, 0, 1024))], (2, 1024))
        colchunks("wout0", t["ev_w_out"][0], 0, 1024)
        colchunks("kc", od_in, OD_KC, 256)
        colchunks("vc", od_in, OD_VC, 256)
        colchunks("ks", od_in, OD_KS, 256)
        colchunks("vs", od_in, OD_VS, 256)
        colchunks("kw", od_in, OD_KW, 256)
        colchunks("vw", od_in, OD_VW, 256)
        colchunks("q", od_in, 0, 1024)
        for b in range(2):
            w1 = t[("od_cmp_k_w1", "od_cmp_v_w1")[b]][0]
            for j in range(4):
                use(("w1", b, j), [(slice(0, CH), cols(w1, 1024 * j, 8, 0, CH))], (8, CH))
        colchunks("z", od_in, OD_Z, 1024)
        colchunks("wout1", t["od_w_out"][0], 0, 1024)
        order = {key: n for n, (key, _, _) in enumerate(loads)}
        npieces = [len(p) for _, p, _ in loads]

        def loaded_count(n):
            return 16 * sum(npieces[m] for m in range(n % RING, n + 1, RING))

        def slot(key):
            n = order[key]
            nk, w = loads[n][2]
            return ring[:, n % RING, 0:nk * w].rearrange("p (k n) -> p k n", k=nk)

        def w_ready(eng, key):
            eng.wait_ge(sem[f"w_loaded{order[key] % RING}"], loaded_count(order[key]))

        scr_u = nc.dram_tensor("scr_u", (NG, NH, L, NC), F32, kind="Internal").ap()
        scr_y = nc.dram_tensor("scr_y", (NG, NH, L, NC), F32, kind="Internal").ap()
        SB, TB, OB = [3, 4, 5], [6, 7], [1, 2]
        ssx, msx, rsx = st1[:, 0:4], st1[:, 4:8], st1[:, 8:12]
        ssq_c, msq_c, rst_c = st1[:, 12:28], st1[:, 28:36], st1[:, 36:44]
        sso, mso, rso = st1[:, 44:52], st1[:, 52:56], st1[:, 56:60]
        dtc = st1[0:32, 60:61]
        hT_even = lambda k: (k + 2) // 2
        xin = t["x"][0].rearrange("(i p) d -> p i d", p=P)
        out = t["out"][0].rearrange("(i p) d -> i p d", p=P)
        U0 = [(h, i, 0) for h in range(MH) for i in range(NT)]
        U1 = [(h, i, b) for h in range(HN) for i in range(NT) for b in range(2)]
        N0, N1 = len(U0), len(U1)

        PJ0 = ([("u", f) for f in range(4)] + [("cq", j, i) for j in range(4) for i in range(NT)]
               + [("kpe",)] + [("za", f) for f in range(4)] + [("zb", f) for f in range(4)])

        PJ1 = ([("cmp", kv, g) for kv in range(2) for g in range(GN)]
               + [x for br in range(2) for x in [("k", br, g) for g in range(GN)] + [("v", br, i) for i in range(NT)]]
               + [("q", f) for f in range(HN)] + [("gate",)] + [("z", f) for f in range(HN)])
        NJ0 = len(PJ0)
        QT = [("uqn", 0), ("uqn", 1), ("uqp", 0), ("uqn", 2), ("uqn", 3), ("uqp", 1)]

        def weights1(tile):
            kind = tile[0]
            if kind == "cmp":
                return (("kc", "vc")[tile[1]], 0)
            if kind == "k":
                return (("ks", "kw")[tile[1]], 0)
            if kind == "v":
                return (("vs", "vw")[tile[1]], 0)
            return (kind, tile[1] // 2)

        def last_use(key):
            kind = key[0]
            if kind == "ada":
                return "mod_done", 12 * key[1] + key[2] + 1
            if kind == "cq":
                return "pj_done", 4 + NT * (key[1] + 1)
            if kind in ("u", "za", "zb"):
                return "pj_done", PJ0.index((kind, 2 * key[1] + 1)) + 1
            if kind == "glu":
                return "glu_done", 2 * key[1] + 2
            if kind in ("uqn", "uqp"):
                return "q_done", QT.index(key) + 1
            if kind == "ukv":
                return "kv_done", 8
            if kind in ("wout0", "wout1"):
                l = int(kind[-1])
                return ("wo_used", 3 * l + key[1] + 1) if key[1] < 3 else ("out_done", NT * (l + 1))
            if kind == "w1":
                return ("w1_used", 3 * key[1] + key[2] + 1) if key[2] < 3 else ("hid_done", key[1] + 1)
            return "pj_done", NJ0 + max(n for n, x in enumerate(PJ1) if x != ("gate",) and weights1(x) == key) + 1

        block = ctx.enter_context(nc.Block())

        @block.sync
        def _(sp):
            sp.dma_start(xr[:], xin).then_inc(sem["x_loaded"], 16)
            for n, (key, pieces, (nk, w)) in enumerate(loads):
                if n >= RING:
                    name, count = last_use(loads[n - RING][0])
                    sp.wait_ge(sem[name], count)
                for where, src in pieces:
                    sp.dma_start(slot(key)[:, :, where], src).then_inc(sem[f"w_loaded{n % RING}"], 16)
                if key == ("wout0", 3):
                    sp.wait_ge(sem["cqT_done"], 8)
                    sp.dma_start(xr[:], xin).then_inc(sem["x_loaded"], 16)
            for i in range(NT):
                sp.wait_ge(sem["out_res"], NT + i + 1)
                sp.dma_start(out[i], xr[:, i, :]).then_inc(sem["stored"], 16)
            sp.wait_ge(sem["stored"], 16 * NT)

        @block.gpsimd
        def _(pool):
            g = nc.gpsimd
            chain = [0]

            def link(ins):
                chain[0] += 1
                ins.then_inc(sem["pool_chain"], 1)
                pool.wait_ge(sem["pool_chain"], chain[0])

            link(g.memset(ident[:], 0.0))
            g.affine_select(out=ident[:], in_=ident[:], compare_op=ALU.not_equal, fill=1.0, base=0,
                            pattern=[[-1, P]], channel_multiplier=1).then_inc(sem["ident_ready"], 1)
            link(g.memset(swap[:], 0.0))
            link(g.affine_select(out=swap[:], in_=swap[:], compare_op=ALU.not_equal, fill=-1.0, base=-64,
                                 pattern=[[-1, P]], channel_multiplier=1))
            g.affine_select(out=swap[:], in_=swap[:], compare_op=ALU.not_equal, fill=1.0, base=64,
                            pattern=[[-1, P]], channel_multiplier=1).then_inc(sem["ident_ready"], 1)
            g.memset(neghalf[:], -0.5).then_inc(sem["masks_ready"], 1)
            link(g.memset(cmaskb[:], 0.0))
            g.affine_select(out=cmaskb[:], in_=cmaskb[:], compare_op=ALU.is_ge, fill=NEG, base=0,
                            pattern=[[-1, P]], channel_multiplier=1).then_inc(sem["masks_ready"], 1)
            link(g.memset(cmpmask[:], 0.0))
            g.affine_select(out=cmpmask[:], in_=cmpmask[:], compare_op=ALU.is_ge, fill=NEG, base=-(CL - 1),
                            pattern=[[P, NT], [-CS, NCMP]], channel_multiplier=1).then_inc(sem["masks_ready"], 1)
            link(g.memset(valid[:], 1.0))
            g.affine_select(out=valid[:], in_=valid[:], compare_op=ALU.is_ge, fill=0.0, base=-(CL - 1),
                            pattern=[[P, NT]], channel_multiplier=1).then_inc(sem["masks_ready"], 1)
            pool.wait_ge(sem["ident_ready"], 2)
            g.tensor_copy(identb[:], ident[:]).then_inc(sem["masks_ready"], 1)
            pool.wait_ge(sem["masks_ready"], 1)

            def rstd(l):
                for i in range(NT):
                    pool.wait_ge(sem["msq_done"], NT * l + i + 1)
                    g.tensor_tensor(rsx[:, i:i + 1], msx[:, i:i + 1], neghalf[:, 0:1], ALU.pow).then_inc(sem["rstd_ready"], 1)

            def residual(l):
                for i in range(NT):
                    pool.wait_ge(sem["out_msq"], NT * l + i + 1)
                    g.tensor_tensor(rso[:, i:i + 1], mso[:, i:i + 1], neghalf[:, 0:1], ALU.pow).then_inc(sem["out_rstd"], 1)
                    pool.wait_ge(sem["out_gpg"], NT * l + i + 1)
                    if l == 0 and i == 0:
                        pool.wait_ge(sem["x_loaded"], 32)
                    g.tensor_tensor(xr[:, i, :], xr[:, i, :], (otmp, otmp1)[l][:, i % 2, :], ALU.add).then_inc(sem["out_res"], 1)

            rstd(0)
            pool.wait_ge(sem["stT_done"], 4)
            g.memset(TP, 0.0).then_inc(sem["T_zero"], 1)
            pool.wait_ge(sem["T_zero"], 1)
            for hh in range(2):
                pool.wait_ge(sem["Kc_act"], 4 * (hh + 1))
                for s in range(L):
                    pool.dma_start(TP[NH * s:NH * s + NH, 16 * hh:16 * hh + 16, NH * s:P],
                                   Kh[0:NH, :, 0:P - NH * s]).then_inc(sem["T_stored"], 16)
            pool.wait_ge(sem["u_stored"], 64)
            pool.wait_ge(sem["r8_ready"], 1)
            pool.wait_ge(sem["Kc_done"], 8)
            for s in range(L):
                pool.dma_start(U[NH * s:NH * s + NH, :, :], scr_u[:, :, s, :].rearrange("g h c -> h g c")).then_inc(sem["u_back"], 16)
            pool.wait_ge(sem["cq_msq"], 1)
            g.tensor_tensor(rst_c, msq_c, neghalf[:], ALU.pow).then_inc(sem["cq_rstd"], 1)
            pool.wait_ge(sem["cq_rstd"], 1)
            for i in range(NT):
                g.tensor_scalar(cqt[:, i, 0:QR], cqt[:, i, 0:QR], rst_c[:, i:i + 1], MSCALE, ALU.mult, ALU.mult).then_inc(sem["cq_scaled"], 1)
                g.tensor_scalar(cqt[:, i, QR:D], cqt[:, i, QR:D], rst_c[:, 4 + i:5 + i], None, ALU.mult).then_inc(sem["cq_scaled"], 1)

            def silu2(z, tanh, n, first):
                for f in range(n):
                    pool.wait_ge(sem["th_act"], first + f + 1)
                    link(g.tensor_scalar(tanh[:, f % 2, :], tanh[:, f % 2, :], 1.0, None, ALU.add))
                    g.tensor_tensor(z[:, f, :], z[:, f, :], tanh[:, f % 2, :], ALU.mult).then_inc(sem["z_pool"], 1)

            silu2(zaT, th, 4, 0)
            pool.wait_ge(sem["Y_act"], 4)
            for s in range(L):
                pool.dma_start(scr_y[:, :, s, :].rearrange("g h c -> h g c"), Yb[NH * s:NH * s + NH, :, :]).then_inc(sem["y_stored"], 16)
            pool.wait_ge(sem["y_stored"], 16 * L)
            pool.dma_start(yT, scr_y.rearrange("(f a) h s c -> (a h) f (s c)", f=4)).then_inc(sem["y_back"], 16)
            silu2(zbT, th, 4, 4)
            residual(0)
            rstd(1)
            silu2(zT, th1, 8, 8)
            residual(1)

        @block.scalar
        def _(act):
            a = nc.scalar
            chain = [0]

            def link(ins):
                chain[0] += 1
                ins.then_inc(sem["act_chain"], 1)
                act.wait_ge(sem["act_chain"], chain[0])

            vec = [(V_C, t["c"].rearrange("o (k p) -> (o k) p", p=P)),
                   (V_PRE, t["pre_norm_g"].rearrange("l (k p) -> (l k) p", p=P)),
                   (V_BADA, t["b_ada"].rearrange("l (k p) -> (l k) p", p=P)),
                   (V_POST, t["post_norm_g"].rearrange("l (k p) -> (l k) p", p=P)),
                   (V_QN, t["ev_q_norm_g"].rearrange("l (k p) -> (l k) p", p=P)),
                   (V_KVN, t["ev_kv_norm_g"].rearrange("l (k p) -> (l k) p", p=P)),
                   (V_BGLU, t["ev_b_glu"].rearrange("l (k p) -> (l k) p", p=P)),
                   (V_DSK, t["ev_d_skip"][0].rearrange("(k a) h -> k (a h)", k=4))]
            for r, src in vec:
                act.dma_start(rows[r:r + src.shape[0], :], src).then_inc(sem["vec_loaded"], 16)
            for b in range(2):
                act.dma_start(perows[CL * b:CL * b + CL, :], t[("od_cmp_k_pe", "od_cmp_v_pe")[b]][0]).then_inc(sem["vec_loaded"], 16)
            act.dma_start(small[0:32, NPW, :], t["ev_lam_re"][0]).then_inc(sem["lam_loaded"], 16)
            act.dma_start(small[0:32, NPW + 1, :], t["ev_lam_im"][0]).then_inc(sem["lam_loaded"], 16)
            act.dma_start(dtc, t["ev_log_dt"].rearrange("o g -> g o")).then_inc(sem["lam_loaded"], 16)
            act.dma_start(cst[:], t["cst"]).then_inc(sem["const_loaded"], 16)
            act.dma_start(posi, t["positions"].to_broadcast([P, S])).then_inc(sem["pos_loaded"], 16)
            act.dma_start(BA[0:64], t["ev_b_re"][0].rearrange("g p h -> p g h")).then_inc(sem["s5_loaded"], 16)
            act.dma_start(BA[64:128], t["ev_b_im"][0].rearrange("g p h -> p g h")).then_inc(sem["s5_loaded"], 16)
            act.dma_start(CN[:, :, 0:64], t["ev_c_re"][0].rearrange("(f a) h p -> (a h) f p", f=4)).then_inc(sem["s5_loaded"], 16)
            act.dma_start(CN[:, :, 64:128], t["ev_c_im"][0].rearrange("(f a) h p -> (a h) f p", f=4)).then_inc(sem["s5_loaded"], 16)
            for e in range(2):
                act.dma_start(wkpe[:, :, 64 * e:64 * e + 64], cols(ev_in, 0, KD, EV_KPE, EV_KPE + RO)).then_inc(sem["small_w_loaded"], 16)
            act.dma_start(wgate[:], cols(od_in, 0, KD, OD_GATE, OD_GATE + 3 * HN)).then_inc(sem["small_w_loaded"], 16)
            for b in range(2):
                act.dma_start(w2[:, b], cols(t[("od_cmp_k_w2", "od_cmp_v_w2")[b]][0], 0, 2, 0, DN)).then_inc(sem["small_w_loaded"], 16)

            X = lambda n: small[0:32, NPW + n, :]
            act.wait_ge(sem["lam_loaded"], 48)
            a.activation(dtc, dtc, ACT.Exp).then_inc(sem["lam_exp"], 1)
            act.wait_ge(sem["lam_red"], 1)
            a.activation(X(9), X(2), ACT.Exp).then_inc(sem["lam_exp"], 1)
            a.activation(small[0:32, iX + 2, :], X(2), ACT.Exp, scale=float(L)).then_inc(sem["lam_exp"], 1)
            act.wait_ge(sem["col_ready"], 1)
            a.activation(sct[:], col[:, V_C:V_C + KD], ACT.Tanh, scale=0.5).then_inc(sem["sc_ready"], 1)
            a.mul(hbg[:], col[:, V_BGLU:V_BGLU + 4], 0.5)

            def squares(l):
                for i in range(NT):
                    if l == 0 and i == 0:
                        act.wait_ge(sem["x_loaded"], 16)
                    if l == 1:
                        act.wait_ge(sem["out_res"], i + 1)
                    a.activation(hT[:, 2 * i:2 * i + 2, :].rearrange("p k n -> p (k n)"), xr[:, i, :], ACT.Square, accum_out=ssx[:, i:i + 1]).then_inc(sem["ssq_done"], 1)

            def sines(n, sin_out, cos_out, sgn, r_ap, abs_ap):
                act.wait_ge(sem["tab_abs"], n + 1)
                a.activation(sin_out, r_ap, ACT.Sin, scale=sgn).then_inc(sem["tab_sin"], 1)
                a.activation(cos_out, abs_ap, ACT.Sin, scale=-1.0, bias=cst_half_pi()).then_inc(sem["tab_cos"], 1)

            def cst_half_pi(rows_=P):
                return halfpi[0:rows_, :]

            squares(0)
            act.wait_ge(sem["const_loaded"], 16)
            act.wait_ge(sem["masks_ready"], 6)
            act.wait_ge(sem["lam_red"], 2)
            a.activation(X(7), X(5), ACT.Sin).then_inc(sem["lam_sin"], 1)
            a.activation(X(8), X(6), ACT.Sin, scale=-1.0, bias=cst_half_pi(32)).then_inc(sem["lam_sin"], 1)
            sines(0, tabM[:, 1, :], tabM[:, 0, :], cst[:, 3:4], ra, rk)

            for b in range(4):
                n = min(16, NPW - 16 * b)
                act.wait_ge(sem["stT_done"], b + 1)
                src = bank[2 + b][0:64, 0:32 * n].rearrange("p (a g) -> p a g", g=NG)
                a.copy(st[0:64, 16 * b:16 * b + n, :], src).then_inc(sem["st_act"], 1)
                a.copy(st[64:128, 16 * b:16 * b + n, :], src).then_inc(sem["st_act"], 1)
            act.wait_ge(sem["CT_done"], 1)
            c1 = C1.rearrange("p g h -> p (g h)")
            a.copy(c1[0:64, :], bank[6][0:64, :]).then_inc(sem["C_act"], 1)
            a.mul(c1[64:128, :], bank[6][64:128, :], -1.0).then_inc(sem["C_act"], 1)
            act.wait_ge(sem["CT_done"], 2)
            a.mul(C2.rearrange("p g h -> p (g h)"), bank[7][:, :], -1.0).then_inc(sem["C_act"], 1)
            act.wait_ge(sem["BB_done"], 1)
            a.copy(BB.rearrange("p g h -> p (g h)"), bank[0][:, :]).then_inc(sem["B_ready"], 1)
            for j in range(2):
                act.wait_ge(sem["gpg_done"], j + 1)
                a.copy(gpg[:, 512 * j:512 * j + 512], bank[6 + j][:, :]).then_inc(sem["gpg_ready"], 1)

            def hT_tiles(l):
                act.wait_ge(sem["mod_ready"], 3 * (l + 1))
                for k in range(0, KD, 2):
                    act.wait_ge(sem["xT_done"], KD * l + k + 1)
                    a.activation(hT[:, k, :], bank[k % 4][:, :], ACT.Identity, bias=mod[:, l, k:k + 1],
                                 scale=pre[:, l, k:k + 1]).then_inc(sem["hT_act"], 1)

            hT_tiles(0)

            def pj_wait(n):
                act.wait_ge(sem["pj_done"], n + 1)

            def z_tile(n, b, z, tanh, f, zn):
                pj_wait(n)
                if zn >= 2:
                    act.wait_ge(sem["z_pool"], zn - 1)
                link(a.copy(z[:, f, :], b[:, :]))
                a.activation(tanh[:, zn % 2, :], b[:, :], ACT.Tanh, scale=0.5).then_inc(sem["th_act"], 1)

            thj = th[:, 0, 0:256]
            for n, tile in enumerate(PJ0):
                if tile[0] == "u":
                    pj_wait(n)
                    f = tile[1]
                    a.copy(uTp[:, f, :].rearrange("p (s c) -> p c s", s=L),
                           bank[n % 4][:, :].rearrange("p (c s) -> p c s", s=L)).then_inc(sem["pj_act"], 1)
                    act.wait_ge(sem["pj_act"], n + 1)
                    act.dma_start(scr_u[8 * f:8 * f + 8].rearrange("g h s c -> (g h) (s c)"), uTp[:, f, :]).then_inc(sem["u_stored"], 16)
                elif tile[0] == "cq":
                    pj_wait(n)
                    if n == 4:
                        act.wait_ge(sem["xT_done"], KD)
                    j, i = tile[1:]
                    link(a.activation(thj, bank[n % 4][:, 0:256], ACT.Square, accum_out=ssq_c[:, 4 * j + i:4 * j + i + 1]))
                    a.copy(cqt[:, i, 256 * j:256 * j + 256], bank[n % 4][:, 0:256]).then_inc(sem["pj_act"], 1)
                elif tile[0] == "kpe":
                    pj_wait(n)
                    a.copy(kpT, bank[n % 4][:, :]).then_inc(sem["pj_act"], 1)
                    for b in range(8):
                        act.wait_ge(sem["GT_done"], b + 1)
                        a.copy(GT[:, 4 * b:4 * b + 4, :].rearrange("p g n -> p (g n)"), bank[4 + b % 4][:, :]).then_inc(sem["GT_act"], 1)
                    for b in range(8):
                        act.wait_ge(sem["Kc_done"], b + 1)
                        if b == 0:
                            act.wait_ge(sem["tab_cos"], 1)
                        if b == 4:
                            act.wait_ge(sem["T_stored"], 16 * L)
                        a.copy(Kh[0:NH, 4 * (b % 4):4 * (b % 4) + 4, :].rearrange("p g n -> p (g n)"),
                               bank[4 + b % 4][0:NH, :]).then_inc(sem["Kc_act"], 1)
                elif tile[0] == "za":
                    if tile[1] == 0:
                        act.wait_ge(sem["T_stored"], 32 * L)
                    z_tile(n, bank[n % 4], zaT, th, tile[1], tile[1])
                    if tile[1] == 3:
                        for b in range(4):
                            act.wait_ge(sem["Y_done"], b + 1)
                            a.copy(Yb[:, 8 * b:8 * b + 8, :].rearrange("p g n -> p (g n)"), bank[4 + b][:, :]).then_inc(sem["Y_act"], 1)
                else:
                    z_tile(n, bank[n % 4], zbT, th, tile[1], 4 + tile[1])

            act.wait_ge(sem["y_skip"], 4)
            a.activation(y2.rearrange("p f n -> p (f n)"), yT.rearrange("p f n -> p (f n)"), ACT.Square).then_inc(sem["y_sq"], 1)
            act.wait_ge(sem["y_arg"], 1)
            a.activation(y2.rearrange("p f n -> p (f n)"), y2.rearrange("p f n -> p (f n)"), ACT.Tanh, scale=C_GELU).then_inc(sem["y_tanh"], 1)
            for f in range(4):
                act.wait_ge(sem["glu_done"], f + 1)
                a.activation(y2[:, f, :], bank[f][:, :], ACT.Tanh, scale=0.25, bias=hbg[:, f:f + 1]).then_inc(sem["glu_act"], 1)
            for f in range(8):
                act.wait_ge(sem["cqT_done"], f + 1)
                dst = cqT[:, f, :] if f < 6 else ckvT[:, f - 6, :]
                a.activation(dst, bank[4 + f % 4][:, :], ACT.Copy, scale=col[:, V_QN + f:V_QN + f + 1]).then_inc(sem["cqT_act"], 1)
            for n in range(6):
                if n % 3 < 2:
                    act.wait_ge(sem["q_done"], n + 1)
                    a.copy(qnT[:, 2 * (n // 3) + n % 3, :], bank[n % 4][:, :]).then_inc(sem["q_act"], 1)
            for n in range(8):
                act.wait_ge(sem["kv_done"], n + 1)
                dst = knT[:, n, :] if n < 4 else vM[:, n - 4, :]
                a.copy(dst, bank[4 + n % 4][:, :]).then_inc(sem["kv_act"], 1)

            def attend(units, n0, Pb, PTb, nP):
                N = len(units)
                for n in range(N + 2):
                    if n < N:
                        h, i, b = units[n]
                        w = P * (i + 1)
                        act.wait_ge(sem["s_max"], n0 + n + 1)
                        if n >= nP:
                            act.wait_ge(sem["pt_done"], n0 + n - nP + 1)
                        a.activation(Pb[:, n % nP, 0:w], bank[SB[n % 3]][:, 0:w], ACT.Exp, bias=smax[:, n % 4:n % 4 + 1],
                                     accum_out=ssum[:, n % 4:n % 4 + 1]).then_inc(sem["s_exp"], 1)
                    m = n - 2
                    if m >= 0 and m % 2 == 0:
                        w = P * (units[m][1] + 1)
                        act.wait_ge(sem["pt_done"], n0 + m + 1)
                        if m >= 2:
                            act.wait_ge(sem["pv_done"], n0 + m - 1)
                        a.copy(PTb[:, m % 2, 0:w], bank[TB[m % 2]][:, 0:w]).then_inc(sem["pt_act"], 1)

            attend(U0, 0, Pm, PT, 3)

            def y_squares(l):
                for i in range(NT):
                    act.wait_ge(sem["out_done"], NT * l + i + 1)
                    for e in range(2):
                        ins = a.activation(hT[:, 2 * i + e, :], bank[2 * i + e][:, :], ACT.Square, accum_out=sso[:, 2 * i + e:2 * i + e + 1])
                        ins.then_inc(sem["out_sq"], 1)

            y_squares(0)

            squares(1)
            for j in range(2):
                act.wait_ge(sem["gpg_done"], 3 + j)
                a.copy(gpg[:, 512 * j:512 * j + 512], bank[6 + j][:, :]).then_inc(sem["gpg_ready"], 1)
            act.wait_ge(sem["xn_ready"], 2 * NT)
            act.dma_start(th1[:, 0, :].bitcast(I32), t["positions"].to_broadcast([P, S])).then_inc(sem["pos_loaded"], 16)
            hT_tiles(1)
            sines(1, tabN[:, 1, :], tabN[:, 0, :], cst[:, 2:3], rt1[:, 0, :], rt1[:, 1, :])
            n0 = NJ0

            def hidden():
                for b in range(2):
                    act.wait_ge(sem["hid_done"], b + 1)
                    for e in range(2):
                        src = bank[4 + 2 * b + e][:, 0:62]
                        a.copy(hid[b][:, e, :], src).then_inc(sem["hid_sq"], 1)
                        a.activation(hsq[b][:, e, :], src, ACT.Square).then_inc(sem["hid_sq"], 1)
                for b in range(2):
                    act.wait_ge(sem["hid_arg"], b + 1)
                    hq = hsq[b].rearrange("p m n -> p (m n)")
                    a.activation(hq, hq, ACT.Tanh, scale=C_GELU).then_inc(sem["hid_tanh"], 1)

            for n, tile in enumerate(PJ1):
                kind, b = tile[0], bank[n % 4]
                if tile == ("z", 0):
                    hidden()
                if tile == ("z", 4):
                    act.wait_ge(sem["cmp_done"], 2)
                    a.mul(vc[0:NCMP].rearrange("p g n -> p (g n)"), bank[5][0:NCMP, 0:GN * DN], 0.5).then_inc(sem["cmp_act"], 1)
                if tile == ("z", 6):
                    for g in range(GN):
                        act.wait_ge(sem["cs_sub"], g + 1)
                        pc = Pc[g].rearrange("p a n -> p (a n)")
                        a.activation(pc, pc, ACT.Exp).then_inc(sem["cs_exp"], 1)
                if kind in ("v", "gate", "z"):
                    pj_wait(n0 + n)
                if kind == "v":
                    a.copy((vs, vw)[tile[1]][:, tile[2], :], b[:, 0:256]).then_inc(sem["v_act"], 1)
                elif kind == "gate":
                    a.activation(gates[:, :, :].rearrange("p i n -> p (i n)"), b[:, 0:NT * 3 * HN], ACT.Tanh, scale=0.5).then_inc(sem["gate_act"], 1)
                elif kind == "z":
                    z_tile(n0 + n, b, zT, th1, tile[1], 8 + tile[1])
            for h in range(HN):
                act.wait_ge(sem["cpt_done"], h + 1)
                a.copy(PcT[0:NCMP, h, :], bank[h % 2][0:NCMP, :]).then_inc(sem["cpt_act"], 1)
            attend(U1, N0, Pm1, PT1, 3)
            y_squares(1)

        @block.vector
        def _(dve):
            v = nc.vector
            chain = [0]

            def link(ins):
                chain[0] += 1
                ins.then_inc(sem["dve_chain"], 1)
                dve.wait_ge(sem["dve_chain"], chain[0])

            X = lambda n: small[0:32, NPW + n, :]
            v.memset(halfpi[:], math.pi / 2).then_inc(sem["masks_ready"], 1)
            v.memset(small[0:32, iP, :], 1.0).then_inc(sem["dve_chain"], 1)
            for r in (iP + TAPS, iF + L, iC + L):
                v.memset(small[0:32, r, :], 0.0).then_inc(sem["dve_chain"], 1)
            for r in (iF, iC):
                v.memset(small[0:32, r, :], 1.0).then_inc(sem["dve_chain"], 1)
            chain[0] += 6

            def reduce_angle(k, r, ang, absr):
                link(v.tensor_scalar(k, ang, 1.0 / TWO_PI, MAGIC, ALU.mult, ALU.add))
                link(v.tensor_scalar(k, k, MAGIC, None, ALU.subtract))
                link(v.scalar_tensor_tensor(r, k, -PI_A, ang, ALU.mult, ALU.add))
                link(v.scalar_tensor_tensor(r, k, -PI_B, r, ALU.mult, ALU.add))
                link(v.scalar_tensor_tensor(r, k, -PI_C, r, ALU.mult, ALU.add))
                link(v.tensor_scalar(r, r, PI_SAFE, -PI_SAFE, ALU.min, ALU.max))
                return v.scalar_tensor_tensor(absr, r, -1.0, r, ALU.mult, ALU.max)

            dve.wait_ge(sem["lam_exp"], 1)
            v.tensor_scalar(X(2), X(0), dtc, None, ALU.mult).then_inc(sem["lam_red"], 1)
            link(v.tensor_scalar(X(3), X(1), dtc, None, ALU.mult))
            reduce_angle(X(4), X(5), X(3), X(6)).then_inc(sem["lam_red"], 1)
            dve.wait_ge(sem["colT_done"], 2)
            v.tensor_copy(col[:], bank[0][:, 0:V_N]).then_inc(sem["col_ready"], 1)
            v.tensor_copy(peT[:], bank[0][:, 128:192]).then_inc(sem["col_ready"], 1)
            dve.wait_ge(sem["pos_loaded"], 16)
            dve.wait_ge(sem["const_loaded"], 16)
            link(v.tensor_copy(rk, posi))
            link(v.tensor_scalar(posb, rk, cst[:, 1:2], None, ALU.mult))
            reduce_angle(rk, ra, posb, rk).then_inc(sem["tab_abs"], 1)
            dve.wait_ge(sem["sc_ready"], 1)
            dve.wait_ge(sem["col_ready"], 2)
            link(v.scalar_tensor_tensor(sc[:], sct[:], 1.0, col[:, V_C:V_C + KD], ALU.add, ALU.mult))
            v.tensor_scalar(sc[:], sc[:], 0.5, None, ALU.mult).then_inc(sem["sc_ready"], 1)

            def mean_squares(l):
                for i in range(NT):
                    dve.wait_ge(sem["ssq_done"], NT * l + i + 1)
                    v.tensor_scalar(msx[:, i:i + 1], ssx[:, i:i + 1], 1.0 / D, EPS, ALU.mult, ALU.add).then_inc(sem["msq_done"], 1)

            def normalise(l, dst):
                for i in range(NT):
                    dve.wait_ge(sem["rstd_ready"], NT * l + i + 1)
                    v.tensor_scalar(dst[:, i, :], xr[:, i, :], rsx[:, i:i + 1], None, ALU.mult).then_inc(sem["xn_ready"], 1)

            mean_squares(0)
            normalise(0, xr)

            tt = [at(oD + 2048 + 256 * q, 4, NP_) for q in range(4)]
            RE, IM = lambda b, n: slice(b, b + n), None

            def cmul(o_re, o_im, a_re, a_im, b_re, b_im, n, last=False):
                T0, T1, T2, T3 = (q[0:32, 0:n, :] for q in tt)
                v.tensor_tensor(T0, a_re, b_re, ALU.mult).then_inc(sem["dve_chain"], 1)
                v.tensor_tensor(T1, a_im, b_im, ALU.mult).then_inc(sem["dve_chain"], 1)
                v.tensor_tensor(T2, a_re, b_im, ALU.mult).then_inc(sem["dve_chain"], 1)
                chain[0] += 3
                link(v.tensor_tensor(T3, a_im, b_re, ALU.mult))
                v.tensor_tensor(o_re, T0, T1, ALU.subtract).then_inc(sem["dve_chain"], 1)
                chain[0] += 1
                ins = v.tensor_tensor(o_im, T2, T3, ALU.add)
                if last:
                    ins.then_inc(sem["pw_ready"], 1)
                else:
                    link(ins)

            def sm(a0, n):
                return small[0:32, a0:a0 + n, :]

            def one(a0, n):
                return small[0:32, a0:a0 + 1, :].to_broadcast([32, n, NP_])

            dve.wait_ge(sem["lam_exp"], 3)
            dve.wait_ge(sem["lam_sin"], 2)
            v.tensor_tensor(sm(iP + 1, 1), sm(NPW + 9, 1), sm(NPW + 8, 1), ALU.mult).then_inc(sem["dve_chain"], 1)
            chain[0] += 1
            link(v.tensor_tensor(sm(iP + TAPS + 1, 1), sm(NPW + 9, 1), sm(NPW + 7, 1), ALU.mult))
            link(v.tensor_tensor(X(10), X(0), X(0), ALU.mult))
            link(v.tensor_tensor(X(11), X(1), X(1), ALU.mult))
            link(v.tensor_tensor(X(10), X(10), X(11), ALU.add))
            link(v.reciprocal(X(10), X(10)))
            link(v.tensor_scalar(X(11), small[0:32, iP + 1, :], 1.0, None, ALU.subtract))
            ni = small[0:32, iP + TAPS + 1, :]
            link(v.tensor_tensor(X(12), X(11), X(0), ALU.mult))
            link(v.tensor_tensor(X(13), ni, X(1), ALU.mult))
            link(v.tensor_tensor(X(12), X(12), X(13), ALU.add))
            link(v.tensor_tensor(small[0:32, iX, :], X(12), X(10), ALU.mult))
            link(v.tensor_tensor(X(12), ni, X(0), ALU.mult))
            link(v.tensor_tensor(X(13), X(11), X(1), ALU.mult))
            link(v.tensor_tensor(X(12), X(12), X(13), ALU.subtract))
            link(v.tensor_tensor(small[0:32, iX + 1, :], X(12), X(10), ALU.mult))
            p, q = iP, iP + TAPS
            cmul(sm(p + 2, 1), sm(q + 2, 1), sm(p + 1, 1), sm(q + 1, 1), sm(p + 1, 1), sm(q + 1, 1), 1)
            cmul(sm(p + 3, 2), sm(q + 3, 2), sm(p + 1, 2), sm(q + 1, 2), one(p + 2, 2), one(q + 2, 2), 2)
            cmul(sm(p + 5, 4), sm(q + 5, 4), sm(p + 1, 4), sm(q + 1, 4), one(p + 4, 4), one(q + 4, 4), 4)
            cmul(sm(NPW + 14, 1), sm(NPW + 15, 1), sm(NPW + 8, 1), sm(NPW + 7, 1), sm(NPW + 8, 1), sm(NPW + 7, 1), 1)
            w_re, w_im = NPW + 14, NPW + 15

            def square():
                cmul(sm(w_re, 1), sm(w_im, 1), sm(w_re, 1), sm(w_im, 1), sm(w_re, 1), sm(w_im, 1), 1)

            square()
            square()
            for base in (iF, iC):
                p, q = base, base + L
                for n in (1, 2, 4):
                    end = base == iC and n == 4
                    cmul(sm(p + n, n), sm(q + n, n), sm(p, n), sm(q, n), one(w_re, n), one(w_im, n), n, last=end)
                    if not end:
                        square()

            def modulation(l):
                dve.wait_ge(sem["mod_done"], 12 * (l + 1))
                v.tensor_tensor(mod[:, l, :], bank[1 - l][:, 0:24], col[:, V_BADA + 24 * l:V_BADA + 24 * l + 24], ALU.add).then_inc(sem["mod_ready"], 1)
                dve.wait_ge(sem["mod_ready"], 3 * l + 1)
                v.scalar_tensor_tensor(pre[:, l, :], mod[:, l, KD:2 * KD], 1.0, col[:, V_PRE + KD * l:V_PRE + KD * l + KD], ALU.add, ALU.mult).then_inc(sem["mod_ready"], 1)
                v.tensor_tensor(gcol[:, l, :], mod[:, l, 2 * KD:], col[:, V_POST + KD * l:V_POST + KD * l + KD], ALU.mult).then_inc(sem["mod_ready"], 1)

            modulation(0)

            def hT_tiles(l):
                dve.wait_ge(sem["mod_ready"], 3 * (l + 1))
                for k in range(1, KD, 2):
                    dve.wait_ge(sem["xT_done"], KD * l + k + 1)
                    v.tensor_scalar(hT[:, k, :], bank[k % 4][:, :], pre[:, l, k:k + 1], mod[:, l, k:k + 1], ALU.mult, ALU.add).then_inc(sem["hT_dve"], 1)

            hT_tiles(0)

            dve.wait_ge(sem["st_act"], 8)
            dve.wait_ge(sem["B_ready"], 1)
            fr = st[:, iX, :].unsqueeze(2).to_broadcast([P, NG, NH])
            fi = st[:, iX + 1, :].unsqueeze(2).to_broadcast([P, NG, NH])
            tb = at(oD + 2048, NG, NH)
            link(v.tensor_tensor(Bb, BA, fr, ALU.mult))
            link(v.tensor_tensor(tb, BB, fi, ALU.mult))
            link(v.tensor_tensor(Bb, Bb, tb, ALU.add))
            link(v.tensor_tensor(iBb, BB, fr, ALU.mult))
            link(v.tensor_tensor(tb, BA, fi, ALU.mult))
            link(v.tensor_tensor(iBb, iBb, tb, ALU.subtract))
            dve.wait_ge(sem["CT_done"], 1)
            def powers(base, n, qq, rev):
                a_ = st[:, base:base + n, 8 * qq:8 * qq + 8]
                if rev:
                    a_ = a_[:, ::-1, :]
                return a_.rearrange("p t g -> p g t").unsqueeze(3).to_broadcast([P, 8, n, NH])

            def per_tap(m, n, qq):
                return m[:, 8 * qq:8 * qq + 8, :].unsqueeze(2).to_broadcast([P, 8, n, NH])

            for qq in range(4):
                if qq >= 2:
                    dve.wait_ge(sem["GT_done"], 2 * (qq - 1))
                G4 = Gc[qq % 2].rearrange("p g (s h) -> p g s h", s=L)
                T4 = tmpG[:, :, 0:L * NH].rearrange("p g (s h) -> p g s h", s=L)
                link(v.tensor_tensor(G4, powers(iP, L, qq, True), per_tap(Bb, L, qq), ALU.mult))
                link(v.tensor_tensor(T4, powers(iP + TAPS, L, qq, True), per_tap(iBb, L, qq), ALU.mult))
                v.tensor_tensor(G4, G4, T4, ALU.add).then_inc(sem["G_ready"], 1)
            dve.wait_ge(sem["C_act"], 3)
            for qq in range(4):
                W4 = W1[:, 8 * qq:8 * qq + 8, :].rearrange("p g (s h) -> p g s h", s=TAPS)
                T4 = tmpG.rearrange("p g (s h) -> p g s h", s=TAPS)
                dve.wait_ge(sem["G_ready"], 4)
                link(v.tensor_tensor(W4, powers(iP, TAPS, qq, False), per_tap(C1, TAPS, qq), ALU.mult))
                link(v.tensor_tensor(T4, powers(iP + TAPS, TAPS, qq, False), per_tap(C2, TAPS, qq), ALU.mult))
                v.tensor_tensor(W4, W4, T4, ALU.add).then_inc(sem["W1_ready"], 1)
            for qq in range(2):
                gs = slice(16 * qq, 16 * qq + 16)

                def co(base):
                    return st[:, base:base + L, gs].rearrange("p a g -> p g a").unsqueeze(3).to_broadcast([P, 16, L, L])

                def fi_(base):
                    return st[:, base:base + L, gs].rearrange("p b g -> p g b").unsqueeze(2).to_broadcast([P, 16, L, L])

                c4 = rotc[:, gs, :].rearrange("p g (a b) -> p g a b", a=L)
                s4 = rots[:, gs, :].rearrange("p g (a b) -> p g a b", a=L)
                t4 = at(oD + 2048, 16, L, L)
                link(v.tensor_tensor(c4, co(iC), fi_(iF), ALU.mult))
                link(v.tensor_tensor(t4, co(iC + L), fi_(iF + L), ALU.mult))
                link(v.tensor_tensor(c4, c4, t4, ALU.subtract))
                link(v.tensor_tensor(s4, co(iC), fi_(iF + L), ALU.mult))
                link(v.tensor_tensor(t4, co(iC + L), fi_(iF), ALU.mult))
                link(v.tensor_tensor(s4, s4, t4, ALU.add))
            v.tensor_scalar(rots[0:64], rots[0:64], -1.0, None, ALU.mult).then_inc(sem["rot_ready"], 1)
            dve.wait_ge(sem["GT_done"], 8)
            link(v.tensor_copy(r8b, st[:, iX + 2, :].unsqueeze(2).to_broadcast([P, NG, NC])))
            v.memset(Xs[:, :, 0:1], 0.0).then_inc(sem["zero_ready"], 1)
            v.memset(r8b[:, :, 0:1], 0.0).then_inc(sem["r8_ready"], 1)
            dve.wait_ge(sem["r8_ready"], 1)
            dve.wait_ge(sem["rot_ready"], 1)

            dve.wait_ge(sem["pj_act"], 20)
            link(v.tensor_tensor(msq_c[:, 0:4], ssq_c[:, 0:4], ssq_c[:, 4:8], ALU.add))
            link(v.tensor_tensor(msq_c[:, 0:4], msq_c[:, 0:4], ssq_c[:, 8:12], ALU.add))
            link(v.tensor_scalar(msq_c[:, 4:8], ssq_c[:, 12:16], 1.0 / KVR, EPS, ALU.mult, ALU.add))
            v.tensor_scalar(msq_c[:, 0:4], msq_c[:, 0:4], 1.0 / QR, EPS, ALU.mult, ALU.add).then_inc(sem["cq_msq"], 1)

            for hh in range(2):
                if hh == 1:
                    dve.wait_ge(sem["Xs_ready"], 1)
                zv, tv = zb5.rearrange("p g c -> p (g c)"), tb5.rearrange("p g c -> p (g c)")
                rc = rotc[:, 16 * hh:16 * hh + 16, :].rearrange("p g c -> p (g c)")
                rs = rots[:, 16 * hh:16 * hh + 16, :].rearrange("p g c -> p (g c)")
                for b in range(2):
                    dve.wait_ge(sem["V_done"], 2 * hh + b + 1)
                    vb, cs = bank[4 + 2 * hh + b], slice(512 * b, 512 * b + 512)
                    v.tensor_tensor(tv[0:64, cs], vb[64:128, :], rs[64:128, cs], ALU.mult).then_inc(sem["dve_chain"], 1)
                    v.tensor_tensor(tv[64:128, cs], vb[0:64, :], rs[0:64, cs], ALU.mult).then_inc(sem["dve_chain"], 1)
                    v.tensor_tensor(zv[:, cs], vb[:, :], rc[:, cs], ALU.mult).then_inc(sem["z_dve"], 1)
                    chain[0] += 2
                dve.wait_ge(sem["dve_chain"], chain[0])
                dve.wait_ge(sem["z_dve"], 2 * hh + 2)
                link(v.tensor_tensor(zv, zv, tv, ALU.add))
                link(v.tensor_tensor_scan(tv, r8b[:, 16 * hh:16 * hh + 16, :].rearrange("p g c -> p (g c)"), zv, 0.0, ALU.mult, ALU.add))
                link(v.tensor_tensor(zv[0:64], tv[64:128], rs[64:128], ALU.mult))
                link(v.tensor_tensor(zv[64:128], tv[0:64], rs[0:64], ALU.mult))
                link(v.tensor_tensor(tv, tv, rc, ALU.mult))
                if hh == 1:
                    dve.wait_ge(sem["Y_done"], 2)
                v.tensor_tensor(Xs[:, :, 1:], tb5, zb5, ALU.subtract).then_inc(sem["Xs_ready"], 1)

            modulation(1)

            dve.wait_ge(sem["y_back"], 16)
            for f in range(4):
                v.scalar_tensor_tensor(yT[:, f, :], uTp[:, f, :], col[:, V_DSK + f:V_DSK + f + 1], yT[:, f, :], ALU.mult, ALU.add).then_inc(sem["y_skip"], 1)
            dve.wait_ge(sem["y_sq"], 1)
            yv, sv = yT.rearrange("p f n -> p (f n)"), y2.rearrange("p f n -> p (f n)")
            link(v.tensor_scalar(sv, sv, 0.044715, 1.0, ALU.mult, ALU.add))
            v.tensor_tensor(sv, sv, yv, ALU.mult).then_inc(sem["y_arg"], 1)
            dve.wait_ge(sem["y_tanh"], 1)
            v.scalar_tensor_tensor(yv, sv, 1.0, yv, ALU.add, ALU.mult).then_inc(sem["y_gelu"], 1)
            dve.wait_ge(sem["y_gelu"], 1)
            dve.wait_ge(sem["z_pool"], 4)
            for f in range(4):
                dve.wait_ge(sem["glu_act"], f + 1)
                link(v.scalar_tensor_tensor(y2[:, f, :], y2[:, f, :], 1.0, yT[:, f, :], ALU.add, ALU.mult))
                v.scalar_tensor_tensor(mixT[:, f, :].rearrange("p (c s) -> p s c", s=L), y2[:, f, :].rearrange("p (s c) -> p s c", s=L),
                                       0.125, zaT[:, f, :].rearrange("p (c s) -> p s c", s=L), ALU.mult, ALU.mult).then_inc(sem["ya_ready"], 1)

            def rope(dst, x, cos, sin, q, tmp, scalar=1.0):
                A, B = tmp
                link(v.scalar_tensor_tensor(A, x, scalar, cos, ALU.mult, ALU.mult))
                for b0 in range(0, P, 2 * q):
                    lo, hi = slice(b0, b0 + q), slice(b0 + q, b0 + 2 * q)
                    link(v.scalar_tensor_tensor(B[lo], x[hi], scalar, sin[hi], ALU.mult, ALU.mult))
                    link(v.scalar_tensor_tensor(B[hi], x[lo], scalar, sin[lo], ALU.mult, ALU.mult))
                return v.tensor_tensor(dst, A, B, ALU.add)

            dve.wait_ge(sem["tab_cos"], 1)
            rt = (rtmp[:, 0, :], rtmp[:, 1, :])
            rope(kpT, kpT, tabM[:, 0, :], tabM[:, 1, :], 32, rt).then_inc(sem["rope_done"], 1)
            for j in range(2):
                dve.wait_ge(sem["q_done"], 3 * j + 3)
                dve.wait_ge(sem["rope_done"], j + 1)
                rope(qpT[:, j, :], bank[(3 * j + 2) % 4][:, :], tabM[:, 0, :], tabM[:, 1, :], 32, rt).then_inc(sem["rope_done"], 1)

            def attend(units, n0, Pb, PTb, nP, heads, mix, z, gated):
                N, per = len(units), len(units) // heads
                for n in range(N + 4):
                    if n < N:
                        w = P * (units[n][1] + 1)
                        dve.wait_ge(sem["s_done"], n0 + n + 1)
                        v.reduce_max(smax[:, n % 4:n % 4 + 1], bank[SB[n % 3]][:, 0:w], AX.X, negate=True).then_inc(sem["s_max"], 1)
                    m = n - 1
                    if 0 <= m < N:
                        h, i, b = units[m]
                        w = P * (i + 1)
                        dve.wait_ge(sem["s_exp"], n0 + m + 1)
                        link(v.reciprocal(srec[:, m % 4:m % 4 + 1], ssum[:, m % 4:m % 4 + 1]))
                        pb = Pb[:, m % nP, 0:w]
                        if gated:
                            v.tensor_scalar(pb, pb, srec[:, m % 4:m % 4 + 1], gates[:, i, 3 * h + b + 1:3 * h + b + 2], ALU.mult, ALU.mult).then_inc(sem["s_scaled"], 1)
                        else:
                            v.tensor_scalar(pb, pb, srec[:, m % 4:m % 4 + 1], None, ALU.mult).then_inc(sem["s_scaled"], 1)
                    m = n - 2
                    if 0 <= m < N and m % 2 == 1:
                        w = P * (units[m][1] + 1)
                        dve.wait_ge(sem["pt_done"], n0 + m + 1)
                        if m >= 2:
                            dve.wait_ge(sem["pv_done"], n0 + m - 1)
                        v.tensor_copy(PTb[:, m % 2, 0:w], bank[TB[m % 2]][:, 0:w]).then_inc(sem["pt_dve"], 1)
                    m = n - 4
                    if m >= 0 and (m + 1) % per == 0:
                        h = m // per
                        dve.wait_ge(sem["pv_done"], n0 + m + 1)
                        v.scalar_tensor_tensor(mix[:, h, :], bank[OB[h % 2]][:, :], 0.5, z[:, h, :], ALU.mult, ALU.mult).then_inc(sem["o_dve"], 1)

            dve.wait_ge(sem["z_pool"], 8)
            attend(U0, 0, Pm, PT, 3, MH, mixT[:, 4:8, :], zbT, False)

            def output(l, tmp):
                for i in range(NT):
                    dve.wait_ge(sem["out_sq"], 2 * (NT * l + i + 1))
                    link(v.tensor_tensor(mso[:, i:i + 1], sso[:, 2 * i:2 * i + 1], sso[:, 2 * i + 1:2 * i + 2], ALU.add))
                    v.tensor_scalar(mso[:, i:i + 1], mso[:, i:i + 1], 1.0 / D, EPS, ALU.mult, ALU.add).then_inc(sem["out_msq"], 1)
                    dve.wait_ge(sem["gpg_ready"], 2 * (l + 1))
                    dve.wait_ge(sem["out_rstd"], NT * l + i + 1)
                    if i >= 2:
                        dve.wait_ge(sem["out_res"], NT * l + i - 1)
                    link(v.scalar_tensor_tensor(tmp[:, i % 2, 0:512], bank[2 * i][:, :], rso[:, i:i + 1], gpg[:, 0:512], ALU.mult, ALU.mult))
                    v.scalar_tensor_tensor(tmp[:, i % 2, 512:], bank[2 * i + 1][:, :], rso[:, i:i + 1], gpg[:, 512:], ALU.mult, ALU.mult).then_inc(sem["out_gpg"], 1)

            output(0, otmp)
            mean_squares(1)
            normalise(1, xn1)
            hT_tiles(1)
            dve.wait_ge(sem["pos_loaded"], 32)
            ang = th1[:, 0, :]
            link(v.tensor_copy(rt1[:, 1, :], ang.bitcast(I32)))
            link(v.tensor_scalar(ang, rt1[:, 1, :], cst[:, 0:1], None, ALU.mult))
            reduce_angle(rt1[:, 1, :], rt1[:, 0, :], ang, rt1[:, 1, :]).then_inc(sem["tab_abs"], 1)
            dve.wait_ge(sem["tab_cos"], 2)
            link(v.tensor_scalar(tabN[:, 2:4, :].rearrange("p a n -> p (a n)"), tabN[:, 0:2, :].rearrange("p a n -> p (a n)"), NSCALE, None, ALU.mult))
            n0 = len(PJ0)
            rt = (rt1[:, 0, :], rt1[:, 1, :])
            for n, tile in enumerate(PJ1):
                kind, b = tile[0], bank[n % 4]
                if kind in ("cmp", "k", "q"):
                    dve.wait_ge(sem["pj_done"], n0 + n + 1)
                if kind == "cmp":
                    kv, gg = tile[1:]
                    for e in range(2):
                        ins = v.tensor_tensor(R[kv][:, CS * e:CS * e + CS, gg, :],
                                              b[:, CS * e:CS * e + CS * NCMP].rearrange("p (n l) -> p l n", l=CS),
                                              peT[:, CL * kv + CS * e:CL * kv + CS * e + CS].unsqueeze(2).to_broadcast([P, CS, NCMP]), ALU.add)
                        ins.then_inc(sem["kc_ready"], 1)
                elif kind == "k":
                    rope((ksT, kwT)[tile[1]][:, tile[2], :], b[:, :], tabN[:, 2, :], tabN[:, 3, :], 64, rt).then_inc(sem["rope1"], 1)
                    dve.wait_ge(sem["rope1"], sum(x[0] in ("k", "q") for x in PJ1[:n + 1]))
                elif kind == "q":
                    rope(qT[:, tile[1], :], b[:, :], tabN[:, 0, :], tabN[:, 1, :], 64, rt).then_inc(sem["rope1"], 1)
                    dve.wait_ge(sem["rope1"], sum(x[0] in ("k", "q") for x in PJ1[:n + 1]))
            dve.wait_ge(sem["gate_act"], 1)
            gf = gates.rearrange("p i n -> p (i n)")
            v.tensor_scalar(gf, gf, 0.5, 0.5, ALU.mult, ALU.add).then_inc(sem["gate_ready"], 1)
            for b in range(2):
                dve.wait_ge(sem["hid_sq"], 4 * (b + 1))
                hv, qv = hid[b].rearrange("p m n -> p (m n)"), hsq[b].rearrange("p m n -> p (m n)")
                link(v.tensor_scalar(qv, qv, 0.044715, 1.0, ALU.mult, ALU.add))
                v.tensor_tensor(qv, qv, hv, ALU.mult).then_inc(sem["hid_arg"], 1)
            for b in range(2):
                hv, qv = hid[b].rearrange("p m n -> p (m n)"), hsq[b].rearrange("p m n -> p (m n)")
                dve.wait_ge(sem["hid_tanh"], b + 1)
                v.scalar_tensor_tensor(hv, qv, 1.0, hv, ALU.add, ALU.mult).then_inc(sem["hid_ready"], 1)
            dve.wait_ge(sem["cmp_done"], 1)
            ends = lambda j: tabN[:, j, CL - 1:CL - 1 + CS * (NCMP - 1) + 1:CS].unsqueeze(1).to_broadcast([P, GN, NCMP])
            kx = bank[4][:, 0:62].rearrange("p (g n) -> p g n", g=GN)
            rope(kcT, kx, ends(2), ends(3), 64, tuple(kct[:, j, :].rearrange("p (g n) -> p g n", g=GN) for j in range(2)), 0.5).then_inc(sem["cmp_rope"], 1)
            dve.wait_ge(sem["gate_ready"], 1)
            for b in range(GN):
                pc4 = Pc[b].rearrange("p (r i) n -> p r i n", r=REP)
                ng, sm_, rr = cstat[:, 0, :], cstat[:, 1, :], cstat[:, 2, :]
                dve.wait_ge(sem["cs_done"], b + 1)
                link(v.tensor_tensor(pc4, bank[6 + b][:, 0:496].rearrange("p (r i n) -> p r i n", r=REP, i=NT),
                                     cmpmask[:].unsqueeze(1).to_broadcast([P, REP, NT, NCMP]), ALU.add))
                link(v.reduce_max(ng, Pc[b], AX.X, negate=True))
                v.tensor_tensor(Pc[b], Pc[b], ng.unsqueeze(2).to_broadcast([P, 16, NCMP]), ALU.add).then_inc(sem["cs_sub"], 1)
                dve.wait_ge(sem["cs_exp"], b + 1)
                link(v.reduce_sum(sm_, Pc[b], AX.X))
                link(v.tensor_scalar(sm_, sm_, TINY, None, ALU.max))
                link(v.reciprocal(rr, sm_))
                r4 = rr.rearrange("p (r i) -> p r i", r=REP)
                link(v.tensor_tensor(r4, r4, valid[:].unsqueeze(1).to_broadcast([P, REP, NT]), ALU.mult))
                gt = gates[:, :, 3 * REP * b:3 * REP * (b + 1):3].rearrange("p i r -> p r i")
                link(v.tensor_tensor(r4, r4, gt, ALU.mult))
                v.tensor_tensor(Pc[b], Pc[b], rr.unsqueeze(2).to_broadcast([P, 16, NCMP]), ALU.mult).then_inc(sem["cs_scaled"], 1)
            dve.wait_ge(sem["z_pool"], 16)
            attend(U1, N0, Pm1, PT1, 3, HN, mix1, zT, True)
            output(1, otmp1)

        @block.tensor
        def _(pe):
            m = nc.tensor
            pe.wait_ge(sem["ident_ready"], 2)
            pe.wait_ge(sem["vec_loaded"], 160)
            m.transpose(bank[0][:, 0:V_N], rows[0:V_N, :], ident[0:V_N, 0:V_N]).then_inc(sem["colT_done"], 1)
            m.transpose(bank[0][:, 128:192], perows[:, :], ident[0:64, 0:64]).then_inc(sem["colT_done"], 1)

            def mod_chunk(l, j):
                key = ("ada", l, j)
                w_ready(pe, key)
                for f in range(2):
                    for k in range(KD):
                        ins = m.matmul(bank[1 - l][:, 2 * j + f:2 * j + f + 1], slot(key)[:, k, P * f:P * f + P],
                                       sc[:, k:k + 1], start=k == 0, stop=k == KD - 1)
                ins.then_inc(sem["mod_done"], 1)

            pe.wait_ge(sem["sc_ready"], 2)
            for j in range(4):
                mod_chunk(0, j)
            pe.wait_ge(sem["pw_ready"], 1)
            for j in range(NPW):
                ins = m.transpose(bank[2 + j // 16][0:64, 32 * (j % 16):32 * (j % 16) + 32], small[0:32, j, :], ident[0:32, 0:32])
                if j % 16 == 15 or j == NPW - 1:
                    ins.then_inc(sem["stT_done"], 1)
            pe.wait_ge(sem["s5_loaded"], 64)
            for f in range(4):
                ins = m.transpose(bank[6][:, P * f:P * f + P], CN[:, f, :], ident[:])
            ins.then_inc(sem["CT_done"], 1)
            pe.wait_ge(sem["col_ready"], 2)
            m.matmul(bank[0][:, :], swap[:], BA.rearrange("p g h -> p (g h)"), start=True, stop=True).then_inc(sem["BB_done"], 1)
            pe.wait_ge(sem["C_act"], 2)
            m.matmul(bank[7][:, :], swap[:], C1.rearrange("p g h -> p (g h)"), start=True, stop=True).then_inc(sem["CT_done"], 1)
            for j in range(4, 12):
                mod_chunk(0, j)

            def gate_rows(l):
                pe.wait_ge(sem["mod_ready"], 3 * (l + 1))
                if l == 0:
                    pe.wait_ge(sem["C_act"], 3)
                else:
                    pe.wait_ge(sem["out_gpg"], NT)
                for k in range(KD):
                    ins = m.matmul(bank[6 + k // 4][:, P * (k % 4):P * (k % 4) + P], gcol[:, l, k:k + 1].to_broadcast([P, P]), ident[:], start=True, stop=True)
                    if k % 4 == 3:
                        ins.then_inc(sem["gpg_done"], 1)

            def x_transposes(l, src):
                for k in range(KD):
                    if l == 0 and k == 0:
                        pe.wait_ge(sem["B_ready"], 1)
                        pe.wait_ge(sem["st_act"], 4)
                    if l == 0 and k == 1:
                        pe.wait_ge(sem["mod_ready"], 1)
                    if l == 1 and k == 0:
                        pe.wait_ge(sem["out_gpg"], 2)
                    if k >= 4 and k % 2 == 0:
                        pe.wait_ge(sem["hT_act"], 4 * l + (k - 4) // 2 + 1)
                    if k >= 4 and k % 2 == 1:
                        pe.wait_ge(sem["hT_dve"], 4 * l + (k - 5) // 2 + 1)
                    for i in range(NT):
                        if k == 0:
                            pe.wait_ge(sem["xn_ready"], NT * l + i + 1)
                        ins = m.transpose(bank[k % 4][:, P * i:P * i + P], src[:, i, P * k:P * k + P], ident[:])
                    ins.then_inc(sem["xT_done"], 1)

            def h_ready(l):
                pe.wait_ge(sem["hT_act"], 4 * (l + 1))
                pe.wait_ge(sem["hT_dve"], 4 * (l + 1))

            gate_rows(0)
            x_transposes(0, xr)
            h_ready(0)

            def f_tile(b, w, c0, rhs=hT, nk=KD):
                for k in range(nk):
                    ins = m.matmul(b[:, :], w[:, k, c0:c0 + P], rhs[:, k, :], start=k == 0, stop=k == nk - 1)
                return ins

            def t_tile(b, w, i, n):
                for k in range(KD):
                    ins = m.matmul(b, hT[:, k, P * i:P * i + P], w[:, k, 0:n], start=k == 0, stop=k == KD - 1)
                return ins

            def s5_transposes():
                for b in range(8):
                    if b % 2 == 0:
                        pe.wait_ge(sem["G_ready"], b // 2 + 1)
                    if b == 0:
                        pe.wait_ge(sem["st_act"], 8)
                        pe.wait_ge(sem["gpg_ready"], 2)
                    if b >= 4:
                        pe.wait_ge(sem["GT_act"], b - 3)
                    for g in range(4):
                        ins = m.transpose(bank[4 + b % 4][:, P * g:P * g + P], Gc[(b // 2) % 2][:, 4 * (b % 2) + g, :], ident[:])
                    ins.then_inc(sem["GT_done"], 1)
                for b in range(8):
                    pe.wait_ge(sem["W1_ready"], b // 2 + 1)
                    pe.wait_ge(sem["GT_act"], min(8, b + 5))
                    if b >= 4:
                        pe.wait_ge(sem["Kc_act"], b - 3)
                    for g in range(4):
                        ins = m.matmul(bank[4 + b % 4][0:NH, P * g:P * g + P], Bb[:, 4 * b + g, :], W1[:, 4 * b + g, 0:L * NH], start=True, stop=True)
                    ins.then_inc(sem["Kc_done"], 1)

            def s5_states():
                pe.wait_ge(sem["u_back"], 16 * L)
                pe.wait_ge(sem["GT_act"], 8)
                pe.wait_ge(sem["Kc_act"], 8)
                for b in range(4):
                    for g in range(8):
                        ins = m.matmul(bank[4 + b][:, NC * g:NC * g + NC], GT[:, 8 * b + g, :], U[:, 8 * b + g, :], start=True, stop=True)
                    ins.then_inc(sem["V_done"], 1)

            def s5_outputs():
                pe.wait_ge(sem["T_stored"], 32 * L)
                pe.wait_ge(sem["zero_ready"], 1)
                for b in range(4):
                    pe.wait_ge(sem["Xs_ready"], b // 2 + 1)
                    for g in range(8):
                        gg = 8 * b + g
                        dst = bank[4 + b][:, NC * g:NC * g + NC]
                        m.matmul(dst, W1[:, gg, NH:], Xs[:, gg % 16, 0:NC], start=True, stop=False)
                        ins = m.matmul(dst, TP[:, gg, :], U[:, gg, :], start=False, stop=True)
                    ins.then_inc(sem["Y_done"], 1)

            def pj_free(n):
                if n >= 4:
                    kinds = [x[0] for x in PJ0[:n - 3]]
                    nz = sum(x in ("za", "zb") for x in kinds)
                    last = PJ0[n - 4][0]
                    if last in ("za", "zb"):
                        pe.wait_ge(sem["th_act"], nz)
                    else:
                        pe.wait_ge(sem["pj_act"], n - 3 - nz)

            for n, tile in enumerate(PJ0):
                pj_free(n)
                if tile == ("zb", 3):
                    pe.wait_ge(sem["mod_ready"], 4)
                b = bank[n % 4]
                if tile[0] == "u":
                    f = tile[1]
                    w_ready(pe, ("u", f // 2))
                    ins = f_tile(b, slot(("u", f // 2)), P * (f % 2))
                elif tile[0] == "cq":
                    j, i = tile[1:]
                    w_ready(pe, ("cq", j))
                    ins = t_tile(b[:, 0:256], slot(("cq", j)), i, 256)
                elif tile[0] == "kpe":
                    pe.wait_ge(sem["small_w_loaded"], 80)
                    ins = f_tile(b, wkpe, 0)
                else:
                    f = tile[1]
                    w_ready(pe, (tile[0], f // 2))
                    ins = f_tile(b, slot((tile[0], f // 2)), P * (f % 2))
                ins.then_inc(sem["pj_done"], 1)
                if tile[0] == "kpe":
                    s5_transposes()
                if tile == ("za", 3):
                    s5_states()
                    pe.wait_ge(sem["th_act"], 4)
                    for j in range(12):
                        mod_chunk(1, j)
                    s5_outputs()

            pe.wait_ge(sem["th_act"], 8)
            pe.wait_ge(sem["y_gelu"], 1)
            for f in range(4):
                w_ready(pe, ("glu", f // 2))
                f_tile(bank[f], slot(("glu", f // 2)), P * (f % 2), yT, 4).then_inc(sem["glu_done"], 1)
            pe.wait_ge(sem["cq_scaled"], 2 * NT)
            pe.wait_ge(sem["Y_act"], 4)
            for f in range(8):
                if f >= 4:
                    pe.wait_ge(sem["cqT_act"], f - 3)
                for i in range(NT):
                    ins = m.transpose(bank[4 + f % 4][:, P * i:P * i + P], cqt[:, i, P * f:P * f + P], ident[:])
                ins.then_inc(sem["cqT_done"], 1)
            pe.wait_ge(sem["glu_act"], 4)
            pe.wait_ge(sem["cqT_act"], 8)
            for n, key in enumerate(QT):
                if n >= 4:
                    pe.wait_ge(sem["q_act"], n - 3)
                w_ready(pe, key)
                f_tile(bank[n % 4], slot(key), 0, cqT, 6).then_inc(sem["q_done"], 1)
            key = ("ukv", 0)
            w_ready(pe, key)
            for n in range(8):
                if n >= 4:
                    pe.wait_ge(sem["kv_act"], n - 3)
                for k in range(2):
                    if n < 4:
                        ins = m.matmul(bank[4 + n % 4][:, :], slot(key)[:, k, 256 * n:256 * n + P], ckvT[:, k, :], start=k == 0, stop=k == 1)
                    else:
                        wv = slot(key)[:, k, :].rearrange("p (h x) -> p h x", h=MH)[:, :, NOPE:]
                        ins = m.matmul(bank[4 + n % 4][:, :], ckvT[:, k, P * (n - 4):P * (n - 4) + P], wv, start=k == 0, stop=k == 1)
                ins.then_inc(sem["kv_done"], 1)

            def attend(units, n0, scores, Pb, PTb, heads, h0, values, extra):
                N, per = len(units), len(units) // heads

                def evacuated(m_):
                    pe.wait_ge(sem[("pt_act", "pt_dve")[m_ % 2]], n0 // 2 + m_ // 2 + 1)

                for n in range(N + 3):
                    if n < N:
                        h, i, b = units[n]
                        if n >= 3:
                            pe.wait_ge(sem["s_exp"], n0 + n - 2)
                        w = P * (i + 1)
                        sb_ = bank[SB[n % 3]]
                        scores(sb_, h, i, b, w)
                        m.matmul(sb_[:, P * i:w], identb[:], cmaskb[:], start=False, stop=True).then_inc(sem["s_done"], 1)
                    u = n - 2
                    if 0 <= u < N:
                        pe.wait_ge(sem["s_scaled"], n0 + u + 1)
                        if u >= 2:
                            evacuated(u - 2)
                        for j in range(units[u][1] + 1):
                            ins = m.transpose(bank[TB[u % 2]][:, P * j:P * j + P], Pb[:, u % 3, P * j:P * j + P], ident[:])
                        ins.then_inc(sem["pt_done"], 1)
                    u = n - 3
                    if u >= 0:
                        h, i, b = units[u]
                        evacuated(u)
                        if u % per == 0 and h >= 2:
                            pe.wait_ge(sem["o_dve"], h0 + h - 1)
                        dst = bank[OB[h % 2]][:, P * i:P * i + P]
                        first = b == 0
                        if extra is not None and b == 0:
                            extra(dst, h, i)
                            first = False
                        last_b = extra is None or b == 1
                        for j in range(i + 1):
                            ins = m.matmul(dst, values(h, b, j), PTb[:, u % 2, P * j:P * j + P], start=first and j == 0, stop=last_b and j == i)
                        ins.then_inc(sem["pv_done"], 1)

            def scores0(dst, h, i, b, w):
                m.matmul(dst[:, 0:w], qnT[:, h, P * i:P * i + P], knT[:, h, 0:w], start=True, stop=False)
                r = slice(64 * (h % 2), 64 * (h % 2) + 64)
                m.matmul(dst[:, 0:w], qpT[r, h // 2, P * i:P * i + P], kpT[r, 0:w], start=False, stop=False)

            pe.wait_ge(sem["masks_ready"], 6)
            pe.wait_ge(sem["q_act"], 4)
            pe.wait_ge(sem["kv_act"], 8)
            pe.wait_ge(sem["rope_done"], 3)
            attend(U0, 0, scores0, Pm, PT, MH, 0, lambda h, b, j: vM[:, j, P * h:P * h + P], None)

            def output(l, mix, heads):
                pe.wait_ge(sem["o_dve"], heads)
                for j in range(4):
                    key = (f"wout{l}", j)
                    w_ready(pe, key)
                    for i in range(NT):
                        for k in range(KD):
                            ins = m.matmul(bank[2 * i + j // 2][:, 256 * (j % 2):256 * (j % 2) + 256], mix[:, k, P * i:P * i + P],
                                           slot(key)[:, k, :], start=k == 0, stop=k == KD - 1)
                        if j == 3:
                            ins.then_inc(sem["out_done"], 1)
                    if j < 3:
                        ins.then_inc(sem["wo_used"], 1)

            pe.wait_ge(sem["ya_ready"], 4)
            output(0, mixT, MH)

            gate_rows(1)
            x_transposes(1, xn1)
            h_ready(1)

            def pj1_free(n):
                if n < 4:
                    return
                done = PJ1[:n - 3]
                kind = PJ1[n - 4][0]
                count = sum(x[0] == kind for x in done)
                if kind == "cmp":
                    pe.wait_ge(sem["kc_ready"], 2 * count)
                elif kind in ("k", "q"):
                    pe.wait_ge(sem["rope1"], sum(x[0] in ("k", "q") for x in done))
                elif kind == "v":
                    pe.wait_ge(sem["v_act"], count)
                elif kind == "gate":
                    pe.wait_ge(sem["gate_act"], 1)
                else:
                    pe.wait_ge(sem["th_act"], 8 + count)

            def hidden():
                pe.wait_ge(sem["kc_ready"], 8)
                for b in range(2):
                    for j in range(4):
                        key = ("w1", b, j)
                        w_ready(pe, key)
                        for l in range(8):
                            for e in range(2):
                                ins = m.matmul(bank[4 + 2 * b + e][:, 0:62], slot(key)[:, l, P * e:P * e + P],
                                               R[b][:, 8 * j + l, :, :], start=j + l == 0, stop=j == 3 and l == 7)
                        if j < 3:
                            ins.then_inc(sem["w1_used"], 1)
                    ins.then_inc(sem["hid_done"], 1)

            def compressed():
                pe.wait_ge(sem["small_w_loaded"], 80)
                pe.wait_ge(sem["hid_ready"], 2)
                for e in range(2):
                    ins = m.matmul(bank[4][:, 0:62], w2[:, 0, e, :], hid[0][:, e, :], start=e == 0, stop=e == 1)
                ins.then_inc(sem["cmp_done"], 1)
                for g in range(GN):
                    for e in range(2):
                        ins = m.matmul(bank[5][0:NCMP, DN * g:DN * g + DN], hid[1][:, e, NCMP * g:NCMP * g + NCMP], w2[:, 1, e, :],
                                       start=e == 0, stop=e == 1)
                ins.then_inc(sem["cmp_done"], 1)

            def compressed_scores():
                pe.wait_ge(sem["cmp_rope"], 1)
                pe.wait_ge(sem["rope1"], 12)
                for g in range(GN):
                    for r in range(REP):
                        for i in range(NT):
                            c0 = NCMP * (NT * r + i)
                            ins = m.matmul(bank[6 + g][:, c0:c0 + NCMP], qT[:, REP * g + r, P * i:P * i + P], kcT[:, g, :], start=True, stop=True)
                    ins.then_inc(sem["cs_done"], 1)

            for n, tile in enumerate(PJ1):
                if tile == ("z", 0):
                    hidden()
                if tile == ("z", 4):
                    compressed()
                if tile == ("z", 6):
                    compressed_scores()
                pj1_free(n)
                kind, b = tile[0], bank[n % 4]
                if kind == "gate":
                    for i in range(NT):
                        ins = t_tile(b[:, 24 * i:24 * i + 24], wgate, i, 24)
                else:
                    key = weights1(tile)
                    w_ready(pe, key)
                    if kind == "v":
                        ins = t_tile(b[:, 0:256], slot(key), tile[2], 256)
                    else:
                        ins = f_tile(b, slot(key), P * (tile[-1] % 2))
                ins.then_inc(sem["pj_done"], 1)
            pe.wait_ge(sem["th_act"], 16)
            for h in range(HN):
                if h % REP == 0:
                    pe.wait_ge(sem["cs_scaled"], h // REP + 1)
                if h >= 2:
                    pe.wait_ge(sem["cpt_act"], h - 1)
                for i in range(NT):
                    ins = m.transpose(bank[h % 2][0:NCMP, P * i:P * i + P], Pc[h // REP][:, NT * (h % REP) + i, :], ident[:])
                ins.then_inc(sem["cpt_done"], 1)

            def scores1(dst, h, i, b, w):
                m.matmul(dst[:, 0:w], qT[:, h, P * i:P * i + P], (ksT, kwT)[b][:, h // REP, 0:w], start=True, stop=False)

            def extra(dst, h, i):
                m.matmul(dst, vc[0:NCMP, h // REP, :], PcT[0:NCMP, h, P * i:P * i + P], start=True, stop=False)

            pe.wait_ge(sem["v_act"], 8)
            pe.wait_ge(sem["cmp_act"], 1)
            pe.wait_ge(sem["cpt_act"], HN)
            attend(U1, N0, scores1, Pm1, PT1, HN, MH, lambda h, b, j: (vs, vw)[b][:, j, DN * (h // REP):DN * (h // REP) + DN], extra)
            output(1, mix1, MH + HN)


_INS = ['x', 'c', 'positions', 'pre_norm_g', 'post_norm_g', 'w_ada', 'b_ada', 'ev_w_in', 'ev_lam_re', 'ev_lam_im', 'ev_log_dt',
        'ev_b_re', 'ev_b_im', 'ev_c_re', 'ev_c_im', 'ev_d_skip', 'ev_w_glu', 'ev_b_glu', 'ev_q_norm_g', 'ev_kv_norm_g', 'ev_w_uq',
        'ev_w_ukv', 'ev_w_out', 'od_w_in', 'od_cmp_k_pe', 'od_cmp_k_w1', 'od_cmp_k_w2', 'od_cmp_v_pe', 'od_cmp_v_w1', 'od_cmp_v_w2',
        'od_w_out']


def _constants():
    f = np.float32
    half_n, half_m = DN // 2, RO // 2
    inv = lambda half: (f(10000.0) ** (-np.arange(half, dtype=f) / f(half))).astype(f)
    p = np.arange(P)
    return np.stack([inv(half_n)[p % half_n], inv(half_m)[p % half_m], np.where(p < half_n, f(1), f(-1)),
                     np.where(p % RO < half_m, f(1), f(-1))], axis=1).astype(f)


def kernel(**inputs):
    import numpy as _np
    import concourse.bacc as _bacc
    from concourse import mybir as _mybir
    from concourse.bass_utils import run_bass_kernel_spmd as _run

    nc = _bacc.Bacc("TRN2", target_bir_lowering=False, num_devices=1)
    arrays, t = {}, {}
    for name in _INS:
        a = _np.ascontiguousarray(inputs[name])
        arrays[f"in_{name}"] = a
        t[name] = nc.dram_tensor(f"in_{name}", a.shape, _mybir.dt.from_np(a.dtype), kind="ExternalInput").ap()
    arrays["in_cst"] = _constants()
    t["cst"] = nc.dram_tensor("in_cst", (P, 4), F32, kind="ExternalInput").ap()
    t["out"] = nc.dram_tensor("out_0", (1, S, D), F32, kind="ExternalOutput").ap()
    build_trunk(nc, t)
    r = _run(nc, [arrays], core_ids=[0])
    return r.results[0]["out_0"]
```

```python
import concourse.bass as bass
from concourse import mybir
from contextlib import ExitStack
import math
import numpy as np

F32 = mybir.dt.float32
F32R = mybir.dt.float32r
I32 = mybir.dt.int32
ALU = mybir.AluOpType
ACT = mybir.ActivationFunctionType
AX = mybir.AxisListType

P = 128
S = 512
NT = S // P
D = 1024
KD = D // P
EPS = 1e-6
TINY = 1e-30
NEG = -1e30
W5 = 512
NG, NH, NP_ = 32, 16, 64
L = 8
NC = S // L
TAPS = L + 1
MH, NOPE, RO, MV = 4, 128, 64, 128
QR, KVR = 768, 256
EV_CQ, EV_KPE, EV_ZB = 2 * W5, 2 * W5 + QR + KVR, 2 * W5 + QR + KVR + RO
MSCALE = (NOPE + RO) ** -0.5
HN, GN, REP, DN = 8, 2, 4, 128
NW = HN * DN
OD_KC, OD_VC, OD_KS, OD_VS, OD_KW, OD_VW = (NW + i * GN * DN for i in range(6))
OD_GATE = NW + 6 * GN * DN
OD_Z = OD_GATE + 3 * HN
NSCALE = DN ** -0.5
CL, CS, CH = 32, 16, 256
NCMP = (S - CL) // CS + 1
SLOT = 2048
RING = 4
C_GELU = math.sqrt(2.0 / math.pi)
PI_SAFE = 3.1415925
MAGIC = 12582912.0
TWO_PI = 2 * math.pi
PI_A = 6.28125
PI_B = float(np.float32(TWO_PI - 6.28125))
PI_C = TWO_PI - PI_A - PI_B

V_C, V_PRE, V_BADA, V_POST, V_QN, V_KVN, V_BGLU, V_DSK, V_N = 0, 8, 24, 72, 88, 94, 96, 100, 104

SEMS = """w_loaded0 w_loaded1 w_loaded2 w_loaded3 vec_loaded const_loaded pos_loaded x_loaded lam_loaded
s5_loaded small_w_loaded ident_ready masks_ready pool_chain dve_chain act_chain colT_done col_ready sc_ready
mod_done mod_ready ssq_done msq_done rstd_ready xn_ready xT_done hT_act tab_abs tab_sin tab_cos
lam_exp lam_red lam_sin pw_ready stT_done st_act CT_done C_act BB_done B_ready GT_done GT_act
Kc_done Kc_act T_zero T_stored W1_ready G_ready
pj_done pj_act th_act z_pool u_stored u_back V_done z_dve zero_ready
Xs_ready Y_done Y_act y_stored y_back y_skip y_sq y_arg y_tanh y_gelu glu_done glu_act ya_ready
cq_msq cq_rstd cq_scaled cqT_done cqT_act q_done q_act kv_done kv_act rope_done
s_done s_max s_exp s_scaled pt_done pt_act pt_dve o_dve out_done out_sq out_msq out_rstd out_gpg gpg_done gpg_ready
out_res kc_ready hid_done hid_tanh hid_sq hid_arg hid_ready cmp_done cmp_act cmp_rope cs_done cs_sub cs_exp cs_scaled
cpt_done cpt_act gate_act gate_ready stored v_act rope1 hT_dve pv_done mrow_act mcol_done macc_done msum_done mod1_ready kz_ready hidT_done hidT_act gT_done pad_ready rot_ready r8_ready wo_used w1_used w_hi w_lo mix_hi mix_lo h_full h_hi h_lo gate_w""".split()


def build_trunk(nc, t):
    with ExitStack() as ctx:
        def sb(name, shape, dt=F32):
            return ctx.enter_context(nc.sbuf_tensor(name, shape, dt))

        sem = {n: ctx.enter_context(nc.semaphore(n)) for n in SEMS}
        bank = [ctx.enter_context(nc.psum_tensor(f"bank{i}", [P, 512], F32)) for i in range(8)]

        ident = sb("ident", [P, P])
        swap = sb("swap", [P, P])
        identb = sb("identb", [P, P], mybir.dt.bfloat16)
        cmaskb = sb("cmaskb", [P, P], mybir.dt.bfloat16)
        cmpmask = sb("cmpmask", [P, NT, NCMP])
        valid = sb("valid", [P, NT])
        rows = sb("rows", [P, P])
        perows = sb("perows", [2 * CL, DN])
        peT = sb("peT", [P, 2 * CL])
        col = sb("col", [P, V_N])
        cst = sb("cst", [P, 4])
        mod = sb("mod", [P, 2, 24])
        pre = sb("pre", [P, 2, KD])
        gcol = sb("gcol", [P, 2, KD])
        sc = sb("sc", [P, KD])
        sct = sb("sct", [P, KD])
        hbg = sb("hbg", [P, 4])
        st1 = sb("st1", [P, 64])
        smax, ssum, srec = sb("smax", [P, 4]), sb("ssum", [P, 4]), sb("srec", [P, 4])
        halfpi = sb("halfpi", [P, 1])
        ones = sb("ones", [P, P])
        neghalf = sb("neghalf", [P, 8])
        gpg = sb("gpg", [P, D])
        xr = sb("xr", [P, NT, D])
        def sb_split(name, shape):
            full = sb(name, shape)
            return full, nc.alloc_sbuf_tensor_at(name + "_r", shape, F32R, offset=nc.sbuf_base - 4 * int(np.prod(shape[1:])))

        hT, hTr = sb_split("hT", [P, KD, S])
        ring, ringr = sb_split("ring", [P, RING, SLOT])
        wgate, wgater = sb_split("wgate", [P, KD, 3 * HN])
        wgate_hi = sb("wgate_hi", [P, KD, 3 * HN], F32R)
        l0s, l0sr = sb_split("l0s", [P, SLOT])
        wkpe = l0s[:, 0:KD * P].rearrange("p (k n) -> p k n", k=KD)
        tabM = l0s[:, KD * P:].rearrange("p (a n) -> p a n", a=2)
        w2 = sb("w2", [P, 2, 2, DN])
        ARENA = (nc.sbuf_bytes_remaining() if callable(nc.sbuf_bytes_remaining) else nc.sbuf_bytes_remaining) // 4 - 40
        ARENA -= ARENA % 8
        arena = sb("arena", [P, ARENA])
        arena0 = nc.sbuf_base - 4 * ARENA

        def at_r(name, off, *shape):
            return nc.alloc_sbuf_tensor_at(name, [P, *shape], F32R, offset=arena0 + 4 * off)

        def at(off, *shape):
            n = int(np.prod(shape))
            assert off + n <= ARENA, (off + n, ARENA)
            v = arena[:, off:off + n]
            if len(shape) == 2:
                v = v.rearrange("p (a b) -> p a b", a=shape[0])
            if len(shape) == 3:
                v = v.rearrange("p (a b c) -> p a b c", a=shape[0], b=shape[1])
            return v

        oW1, oGT = 0, 4608
        oROT = oGT + 4096
        oD = oROT + 4096
        oT = oD + 3200
        oH = oT + 4608
        oU = oH + 4768
        W1 = at(oW1, NG, TAPS * NH)
        GT = at(oGT, NG, P)
        rotc, rots = at(oROT, NG, NC), at(oROT + 2048, NG, NC)
        Gc = [at(oD, 8, P), at(oD + 1024, 8, P)]
        tmpG = at(oD + 2048, 8, TAPS * NH)
        TP = at(oT, NG, P)
        NPW = 2 * TAPS + 2 * L + 2 * L + 3
        small = at(oT, NPW + 18, NP_)
        iP, iF, iC, iX = 0, 2 * TAPS, 2 * TAPS + 2 * L, 2 * TAPS + 4 * L
        st = at(oH, NPW, NG)
        BA, BB = at(oH + 1696, NG, NH), at(oH + 2208, NG, NH)
        Bb, iBb = at(oH + 2720, NG, NH), at(oH + 3232, NG, NH)
        C1, C2 = at(oH + 3744, NG, NH), at(oH + 4256, NG, NH)
        CN = Gc[0].rearrange("p a b -> p (a b)")[:, 0:512].rearrange("p (a b) -> p a b", a=4)
        U = at(oH, NG, NC)
        zb5, tb5 = at(oH + 2048, 16, NC), at(oH + 3072, 16, NC)
        Xs = at(oD, 16, NC + 1)
        r8b = at(oD + 1040, NG, NC)
        Kh = at(oU + 2048, 16, P)
        uTp = at(oU, 4, S)
        zaT = at(oU + 2048, 4, S)
        th = at(oU + 4096, 2, S)
        mrow = th
        macc = [at(oT, 6, 256)[:, j, :] for j in range(6)] + [hT[:, j // 2, 256 * (j % 2):256 * (j % 2) + 256] for j in range(6)]
        kz = at(oD + 1024 + 1536, S)
        kpT = at(oU + 5120, S)
        Yb = at(oGT, NG, NC)
        yT, y2 = at(oGT + 2048, 4, S), at(oROT, 4, S)
        cqt = xr
        cqT, ckvT = at(0, 6, S), at(3072, 2, S)
        qnT = at(oROT + 2048, 4, S)
        qpT = at(oD, 2, S)
        knT, vM = at(oT, 4, S), at(oT + 2048, NT, 4 * MV)
        zbT = at(oH, 4, S)
        mixT = at(oGT, KD, S)
        Pm, PT = at(oD + 1024, 3, S), at(oH + 2048, 2, S)
        rtmp = at(oH + 3072, 2, S)
        ra, rk = at(oU + 2048, S), at(oU + 2560, S)
        posb = at(oU + 3072, S)
        posi = posb.bitcast(I32)
        otmp = at(0, 2, D)
        tabN = at(0, 4, S)
        qT, ksT, kwT = at(2048, HN, S), at(6144, GN, S), at(7168, GN, S)
        vs, vw = at(8192, NT, GN * DN), at(9216, NT, GN * DN)
        R = [at(10240, CL, GN, NCMP), at(10240 + 1984, CL, GN, NCMP)]
        PcT = at(10240, HN, S)
        zT = at(14336, HN, S)
        Pc = [at(18432, 16, NCMP), at(18928, 16, NCMP)]
        NB = GN * NCMP
        hidT = [at(19424, 2, NB), at(19548, 2, NB)]
        kcT, kct = at(19920, GN, NCMP), at(19982, 2, NB)
        hid, hsq = [at(20592 + 256 * b, 2, P) for b in range(2)], [at(21104 + 256 * b, 2, P) for b in range(2)]
        vc = at(20106, GN, DN)
        gates = at(20362, NT, 3 * HN)
        cstat = at(20458, 4, 16)
        gT = at(21616, S)
        Pm1, PT1 = at(20592, 3, S), at(22128, 2, S)
        rt1, th1 = at(23152, 2, S), at(24176, 2, S)
        mix1 = at(25200, KD, S)
        xn1 = at(14336, NT, D)
        hlo1, hlo1r = mix1, at_r("hlo1_r", 25200, KD, S)
        mixr = [at_r("mix0_r", oGT, KD, S), hlo1r]
        w_high = [l0sr, at_r("w_high_r", 29296, SLOT)]
        sqj = at(oROT, 2, S)
        otmp1 = at(2048, 2, D)
        assert oU + 5632 <= ARENA, (oU + 5632, ARENA)

        def cols(w, r0, nk, c0, c1):
            return w[r0:r0 + nk * P, c0:c1].rearrange("(k p) n -> p k n", p=P)

        ev_in, od_in = t["ev_w_in"][0], t["od_w_in"][0]
        loads = []

        def use(key, pieces, shape):
            loads.append((key, pieces, shape))

        def ada(l, j0, j1):
            for j in range(j0, j1):
                use(("ada", l, j), [(slice(0, 256), cols(t["w_ada"][l], 0, KD, 256 * j, 256 * j + 256))], (KD, 256))

        def colchunks(key, w, c0, n, r0=0, nk=KD):
            for j in range(n // 256):
                use((key, j), [(slice(0, 256), cols(w, r0, nk, c0 + 256 * j, c0 + 256 * j + 256))], (nk, 256))

        ada(0, 0, 12)
        colchunks("u", ev_in, 0, 512)
        colchunks("cq", ev_in, EV_CQ, 1024)
        colchunks("za", ev_in, W5, 512)
        colchunks("zb", ev_in, EV_ZB, 512)
        ada(1, 0, 6)
        uq = t["ev_w_uq"][0]
        for h in range(0, MH, 2):
            for e in range(2):
                use(("uqn", h + e), [(slice(0, P), cols(uq, 0, 6, (h + e) * 192, (h + e) * 192 + P))], (6, P))
            if h == 2:
                ada(1, 6, 8)
            use(("uqp", h // 2), [(slice(64 * e, 64 * e + 64), cols(uq, 0, 6, (h + e) * 192 + P, (h + e) * 192 + 192)) for e in range(2)], (6, P))
        use(("ukv", 0), [(slice(0, 1024), cols(t["ev_w_ukv"][0], 0, 2, 0, 1024))], (2, 1024))
        ada(1, 8, 12)
        colchunks("glu", t["ev_w_glu"][0], 0, 512, nk=4)
        colchunks("wout0", t["ev_w_out"][0], 0, 1024)
        colchunks("kc", od_in, OD_KC, 256)
        colchunks("vc", od_in, OD_VC, 256)
        colchunks("ks", od_in, OD_KS, 256)
        colchunks("vs", od_in, OD_VS, 256)
        colchunks("kw", od_in, OD_KW, 256)
        colchunks("vw", od_in, OD_VW, 256)
        colchunks("q", od_in, 0, 1024)
        for b in range(2):
            w1 = t[("od_cmp_k_w1", "od_cmp_v_w1")[b]][0]
            for j in range(4):
                use(("w1", b, j), [(slice(0, CH), cols(w1, 1024 * j, 8, 0, CH))], (8, CH))
        colchunks("z", od_in, OD_Z, 1024)
        colchunks("wout1", t["od_w_out"][0], 0, 1024)
        order = {key: n for n, (key, _, _) in enumerate(loads)}
        npieces = [len(p) for _, p, _ in loads]

        def loaded_count(n):
            return 16 * sum(npieces[m] for m in range(n % RING, n + 1, RING))

        def slot(key):
            n = order[key]
            nk, w = loads[n][2]
            return ring[:, n % RING, 0:nk * w].rearrange("p (k n) -> p k n", k=nk)

        SPLIT = [key for key, _, _ in loads if key[0] in ("wout0", "kc", "vc", "ks", "vs", "kw", "vw", "q", "z", "wout1")]
        sorder = {key: n for n, key in enumerate(SPLIT)}

        def hi(key):
            nk, w = loads[order[key]][2]
            return w_high[sorder[key] % 2][:, 0:nk * w].rearrange("p (k n) -> p k n", k=nk)

        def lo(key):
            nk, w = loads[order[key]][2]
            return ringr[:, order[key] % RING, 0:nk * w].rearrange("p (k n) -> p k n", k=nk)

        def split_high(act, a, key):
            n = sorder[key]
            w_ready(act, key)
            if n >= 2:
                name, count = last_use(SPLIT[n - 2])
                act.wait_ge(sem[name], count)
            a.copy(hi(key), slot(key)).then_inc(sem["w_hi"], 1)

        def split_low(dve, v, key):
            dve.wait_ge(sem["w_hi"], sorder[key] + 1)
            v.tensor_tensor(lo(key), slot(key), hi(key).bitcast(F32), ALU.subtract).then_inc(sem["w_lo"], 1)

        def next_split(n):
            if n == 0 or PJ1[n] == ("gate",) or PJ1[n][-1] % 2:
                return None
            key = weights1(PJ1[n])
            if PJ1[n - 1] != ("gate",) and weights1(PJ1[n - 1]) == key or key in (("q", 3), ("z", 0)):
                return None
            return SPLIT[sorder[key] + 1]

        def w_ready(eng, key):
            eng.wait_ge(sem[f"w_loaded{order[key] % RING}"], loaded_count(order[key]))

        scr_u = nc.dram_tensor("scr_u", (NG, NH, L, NC), F32, kind="Internal").ap()
        scr_y = nc.dram_tensor("scr_y", (NG, NH, L, NC), F32, kind="Internal").ap()
        MB = [[4, 5, 6], [0, 1, 2]]
        SB, TB, OB = [3, 4, 5], [6, 7], [1, 2]
        ssx, msx, rsx = st1[:, 0:4], st1[:, 4:8], st1[:, 8:12]
        ssq_c, msq_c, rst_c = st1[:, 12:28], st1[:, 28:36], st1[:, 36:44]
        sso, mso, rso = st1[:, 44:52], st1[:, 52:56], st1[:, 56:60]
        dtc = st1[0:32, 60:61]
        xin = t["x"][0].rearrange("(i p) d -> p i d", p=P)
        out = t["out"][0].rearrange("(i p) d -> i p d", p=P)
        U0 = [(h, i, 0) for h in range(MH) for i in range(NT)]
        U1 = [(h, i, b) for h in range(HN) for i in range(NT) for b in range(2)]
        N0, N1 = len(U0), len(U1)

        PJ0 = ([("u", f) for f in range(4)] + [("cq", j, i) for j in range(4) for i in range(NT)]
               + [("kpe",)] + [("za", f) for f in range(4)] + [("zb", f) for f in range(4)])

        PJ1 = ([("cmp", kv, g) for kv in range(2) for g in range(GN)]
               + [x for br in range(2) for x in [("k", br, g) for g in range(GN)] + [("v", br, i) for i in range(NT)]]
               + [("q", f) for f in range(HN)] + [("gate",)] + [("z", f) for f in range(HN)])
        NJ0 = len(PJ0)
        QT = [("uqn", 0), ("uqn", 1), ("uqp", 0), ("uqn", 2), ("uqn", 3), ("uqp", 1)]

        def weights1(tile):
            kind = tile[0]
            if kind == "cmp":
                return (("kc", "vc")[tile[1]], 0)
            if kind == "k":
                return (("ks", "kw")[tile[1]], 0)
            if kind == "v":
                return (("vs", "vw")[tile[1]], 0)
            return (kind, tile[1] // 2)

        def last_use(key):
            kind = key[0]
            if kind == "ada":
                return ("mod_done", "macc_done")[key[1]], key[2] + 1
            if kind == "cq":
                return "pj_done", 4 + NT * (key[1] + 1)
            if kind in ("u", "za", "zb"):
                return "pj_done", PJ0.index((kind, 2 * key[1] + 1)) + 1
            if kind == "glu":
                return "glu_done", 2 * key[1] + 2
            if kind in ("uqn", "uqp"):
                return "q_done", QT.index(key) + 1
            if kind == "ukv":
                return "kv_done", 8
            if kind in ("wout0", "wout1"):
                l = int(kind[-1])
                return ("wo_used", 3 * l + key[1] + 1) if key[1] < 3 else ("out_done", NT * (l + 1))
            if kind == "w1":
                return ("w1_used", 3 * key[1] + key[2] + 1) if key[2] < 3 else ("hid_done", key[1] + 1)
            return "pj_done", NJ0 + max(n for n, x in enumerate(PJ1) if x != ("gate",) and weights1(x) == key) + 1

        block = ctx.enter_context(nc.Block())

        @block.sync
        def _(sp):
            sp.dma_start(xr[:], xin).then_inc(sem["x_loaded"], 16)
            for n, (key, pieces, (nk, w)) in enumerate(loads):
                if n >= RING:
                    name, count = last_use(loads[n - RING][0])
                    sp.wait_ge(sem[name], count)
                for where, src in pieces:
                    sp.dma_start(slot(key)[:, :, where], src).then_inc(sem[f"w_loaded{n % RING}"], 16)
                if key == ("wout0", 3):
                    sp.wait_ge(sem["cqT_done"], 8)
                    sp.dma_start(xr[:], xin).then_inc(sem["x_loaded"], 16)
            for i in range(NT):
                sp.wait_ge(sem["out_res"], NT + i + 1)
                sp.dma_start(out[i], xr[:, i, :]).then_inc(sem["stored"], 16)
            sp.wait_ge(sem["stored"], 16 * NT)

        @block.gpsimd
        def _(pool):
            g = nc.gpsimd
            chain = [0]

            def link(ins):
                chain[0] += 1
                ins.then_inc(sem["pool_chain"], 1)
                pool.wait_ge(sem["pool_chain"], chain[0])

            link(g.memset(ident[:], 0.0))
            g.affine_select(out=ident[:], in_=ident[:], compare_op=ALU.not_equal, fill=1.0, base=0,
                            pattern=[[-1, P]], channel_multiplier=1).then_inc(sem["ident_ready"], 1)
            link(g.memset(swap[:], 0.0))
            link(g.affine_select(out=swap[:], in_=swap[:], compare_op=ALU.not_equal, fill=-1.0, base=-64,
                                 pattern=[[-1, P]], channel_multiplier=1))
            g.affine_select(out=swap[:], in_=swap[:], compare_op=ALU.not_equal, fill=1.0, base=64,
                            pattern=[[-1, P]], channel_multiplier=1).then_inc(sem["ident_ready"], 1)
            g.memset(ones[:], 1.0).then_inc(sem["masks_ready"], 1)
            g.memset(neghalf[:], -0.5).then_inc(sem["masks_ready"], 1)
            link(g.memset(cmaskb[:], 0.0))
            g.affine_select(out=cmaskb[:], in_=cmaskb[:], compare_op=ALU.is_ge, fill=NEG, base=0,
                            pattern=[[-1, P]], channel_multiplier=1).then_inc(sem["masks_ready"], 1)
            link(g.memset(cmpmask[:], 0.0))
            g.affine_select(out=cmpmask[:], in_=cmpmask[:], compare_op=ALU.is_ge, fill=NEG, base=-(CL - 1),
                            pattern=[[P, NT], [-CS, NCMP]], channel_multiplier=1).then_inc(sem["masks_ready"], 1)
            link(g.memset(valid[:], 1.0))
            g.affine_select(out=valid[:], in_=valid[:], compare_op=ALU.is_ge, fill=0.0, base=-(CL - 1),
                            pattern=[[P, NT]], channel_multiplier=1).then_inc(sem["masks_ready"], 1)
            pool.wait_ge(sem["ident_ready"], 2)
            g.tensor_copy(identb[:], ident[:]).then_inc(sem["masks_ready"], 1)
            pool.wait_ge(sem["masks_ready"], 2)

            def rstd(l):
                for i in range(NT):
                    pool.wait_ge(sem["msq_done"], NT * l + i + 1)
                    g.tensor_tensor(rsx[:, i:i + 1], msx[:, i:i + 1], neghalf[:, 0:1], ALU.pow).then_inc(sem["rstd_ready"], 1)

            def residual(l):
                for i in range(NT):
                    pool.wait_ge(sem["out_msq"], NT * l + i + 1)
                    g.tensor_tensor(rso[:, i:i + 1], mso[:, i:i + 1], neghalf[:, 0:1], ALU.pow).then_inc(sem["out_rstd"], 1)
                    pool.wait_ge(sem["out_gpg"], NT * l + i + 1)
                    if l == 0 and i == 0:
                        pool.wait_ge(sem["x_loaded"], 32)
                    g.tensor_tensor(xr[:, i, :], xr[:, i, :], (otmp, otmp1)[l][:, i % 2, :], ALU.add).then_inc(sem["out_res"], 1)

            rstd(0)
            pool.wait_ge(sem["stT_done"], 4)
            g.memset(TP, 0.0).then_inc(sem["T_zero"], 1)
            pool.wait_ge(sem["cq_msq"], 1)
            g.tensor_tensor(rst_c, msq_c, neghalf[:], ALU.pow).then_inc(sem["cq_rstd"], 1)
            pool.wait_ge(sem["cq_rstd"], 1)
            for i in range(NT):
                g.tensor_scalar(cqt[:, i, 0:QR], cqt[:, i, 0:QR], rst_c[:, i:i + 1], MSCALE, ALU.mult, ALU.mult).then_inc(sem["cq_scaled"], 1)
                g.tensor_scalar(cqt[:, i, QR:D], cqt[:, i, QR:D], rst_c[:, 4 + i:5 + i], None, ALU.mult).then_inc(sem["cq_scaled"], 1)

            def silu2(z, tanh, n, first, f0=0):
                for f in range(f0, f0 + n):
                    pool.wait_ge(sem["th_act"], first + f - f0 + 1)
                    link(g.tensor_scalar(tanh[:, f % 2, :], tanh[:, f % 2, :], 1.0, None, ALU.add))
                    g.tensor_tensor(z[:, f, :], z[:, f, :], tanh[:, f % 2, :], ALU.mult).then_inc(sem["z_pool"], 1)

            silu2(zaT, th, 4, 0)
            silu2(zbT, th, 4, 4)
            residual(0)
            rstd(1)
            silu2(zT, th1, 4, 8)
            g.memset(vc, 0.0).then_inc(sem["pad_ready"], 1)
            pool.wait_ge(sem["hid_done"], 2)
            g.memset(PcT.rearrange("p h n -> p (h n)"), 0.0).then_inc(sem["pad_ready"], 1)
            silu2(zT, th1, 4, 12, 4)
            residual(1)

        @block.scalar
        def _(act):
            a = nc.scalar
            chain = [0]

            def link(ins):
                chain[0] += 1
                ins.then_inc(sem["act_chain"], 1)
                act.wait_ge(sem["act_chain"], chain[0])

            vec = [(V_C, t["c"].rearrange("o (k p) -> (o k) p", p=P)),
                   (V_PRE, t["pre_norm_g"].rearrange("l (k p) -> (l k) p", p=P)),
                   (V_BADA, t["b_ada"].rearrange("l (k p) -> (l k) p", p=P)),
                   (V_POST, t["post_norm_g"].rearrange("l (k p) -> (l k) p", p=P)),
                   (V_QN, t["ev_q_norm_g"].rearrange("l (k p) -> (l k) p", p=P)),
                   (V_KVN, t["ev_kv_norm_g"].rearrange("l (k p) -> (l k) p", p=P)),
                   (V_BGLU, t["ev_b_glu"].rearrange("l (k p) -> (l k) p", p=P)),
                   (V_DSK, t["ev_d_skip"][0].rearrange("(k a) h -> k (a h)", k=4))]
            for r, src in vec:
                act.dma_start(rows[r:r + src.shape[0], :], src).then_inc(sem["vec_loaded"], 16)
            for b in range(2):
                act.dma_start(perows[CL * b:CL * b + CL, :], t[("od_cmp_k_pe", "od_cmp_v_pe")[b]][0]).then_inc(sem["vec_loaded"], 16)
            act.dma_start(small[0:32, NPW, :], t["ev_lam_re"][0]).then_inc(sem["lam_loaded"], 16)
            act.dma_start(small[0:32, NPW + 1, :], t["ev_lam_im"][0]).then_inc(sem["lam_loaded"], 16)
            act.dma_start(dtc, t["ev_log_dt"].rearrange("o g -> g o")).then_inc(sem["lam_loaded"], 16)
            act.dma_start(cst[:], t["cst"]).then_inc(sem["const_loaded"], 16)
            act.dma_start(posi, t["positions"].to_broadcast([P, S])).then_inc(sem["pos_loaded"], 16)
            act.dma_start(BA[0:64], t["ev_b_re"][0].rearrange("g p h -> p g h")).then_inc(sem["s5_loaded"], 16)
            act.dma_start(BA[64:128], t["ev_b_im"][0].rearrange("g p h -> p g h")).then_inc(sem["s5_loaded"], 16)
            act.dma_start(CN[:, :, 0:64], t["ev_c_re"][0].rearrange("(f a) h p -> (a h) f p", f=4)).then_inc(sem["s5_loaded"], 16)
            act.dma_start(CN[:, :, 64:128], t["ev_c_im"][0].rearrange("(f a) h p -> (a h) f p", f=4)).then_inc(sem["s5_loaded"], 16)
            for e in range(2):
                act.dma_start(wkpe[:, :, 64 * e:64 * e + 64], cols(ev_in, 0, KD, EV_KPE, EV_KPE + RO)).then_inc(sem["small_w_loaded"], 16)
            act.dma_start(wgate[:], cols(od_in, 0, KD, OD_GATE, OD_GATE + 3 * HN)).then_inc(sem["small_w_loaded"], 16)
            for b in range(2):
                act.dma_start(w2[:, b], cols(t[("od_cmp_k_w2", "od_cmp_v_w2")[b]][0], 0, 2, 0, DN)).then_inc(sem["small_w_loaded"], 16)

            X = lambda n: small[0:32, NPW + n, :]
            act.wait_ge(sem["lam_loaded"], 48)
            a.activation(dtc, dtc, ACT.Exp).then_inc(sem["lam_exp"], 1)
            act.wait_ge(sem["lam_red"], 1)
            a.activation(X(9), X(2), ACT.Exp).then_inc(sem["lam_exp"], 1)
            a.activation(small[0:32, iX + 2, :], X(2), ACT.Exp, scale=float(L)).then_inc(sem["lam_exp"], 1)
            act.wait_ge(sem["col_ready"], 1)
            a.activation(sct[:], col[:, V_C:V_C + KD], ACT.Tanh, scale=0.5).then_inc(sem["sc_ready"], 1)
            a.mul(hbg[:], col[:, V_BGLU:V_BGLU + 4], 0.5)

            def squares(l):
                for i in range(NT):
                    if l == 0 and i == 0:
                        act.wait_ge(sem["x_loaded"], 16)
                    if l == 1:
                        act.wait_ge(sem["out_res"], i + 1)
                        act.wait_ge(sem["out_sq"], 2 * NT)
                        if i:
                            act.wait_ge(sem["ssq_done"], NT + i)
                    a.activation((hT[:, 2 * i:2 * i + 2, :] if l == 0 else sqj).rearrange("p k n -> p (k n)"), xr[:, i, :], ACT.Square, accum_out=ssx[:, i:i + 1]).then_inc(sem["ssq_done"], 1)

            def sines(n, sin_out, cos_out, sgn, r_ap, abs_ap):
                act.wait_ge(sem["tab_abs"], n + 1)
                a.activation(sin_out, r_ap, ACT.Sin, scale=sgn).then_inc(sem["tab_sin"], 1)
                a.activation(cos_out, abs_ap, ACT.Sin, scale=-1.0, bias=cst_half_pi()).then_inc(sem["tab_cos"], 1)

            def cst_half_pi(rows_=P):
                return halfpi[0:rows_, :]

            squares(0)
            act.wait_ge(sem["const_loaded"], 16)
            act.wait_ge(sem["masks_ready"], 7)
            act.wait_ge(sem["lam_red"], 2)
            a.activation(X(7), X(5), ACT.Sin).then_inc(sem["lam_sin"], 1)
            a.activation(X(8), X(6), ACT.Sin, scale=-1.0, bias=cst_half_pi(32)).then_inc(sem["lam_sin"], 1)
            sines(0, tabM[:, 1, :], tabM[:, 0, :], cst[:, 3:4], ra, rk)

            def mod_rows(d0, d1):
                for d in range(d0, d1):
                    act.wait_ge(sem["mod_done"], 2 * d + 2)
                    if d >= 2:
                        act.wait_ge(sem["mcol_done"], d - 1)
                    a.copy(mrow[0:1, d % 2, :], bank[7 * (d % 2)][0:1, :]).then_inc(sem["mrow_act"], 1)

            mod_rows(0, 3)
            for b in range(4):
                n = min(16, NPW - 16 * b)
                act.wait_ge(sem["stT_done"], b + 1)
                src = bank[2 + b][0:64, 0:32 * n].rearrange("p (a g) -> p a g", g=NG)
                a.copy(st[0:64, 16 * b:16 * b + n, :], src).then_inc(sem["st_act"], 1)
                a.copy(st[64:128, 16 * b:16 * b + n, :], src).then_inc(sem["st_act"], 1)
            act.wait_ge(sem["CT_done"], 1)
            c1 = C1.rearrange("p g h -> p (g h)")
            a.copy(c1[0:64, :], bank[6][0:64, :]).then_inc(sem["C_act"], 1)
            a.mul(c1[64:128, :], bank[6][64:128, :], -1.0).then_inc(sem["C_act"], 1)
            act.wait_ge(sem["BB_done"], 1)
            a.copy(BB.rearrange("p g h -> p (g h)"), bank[2][:, :]).then_inc(sem["B_ready"], 1)
            act.wait_ge(sem["CT_done"], 2)
            a.mul(C2.rearrange("p g h -> p (g h)"), bank[3][:, :], -1.0).then_inc(sem["C_act"], 1)
            mod_rows(3, 6)
            for j in range(2):
                act.wait_ge(sem["gpg_done"], j + 1)
                a.copy(gpg[:, 512 * j:512 * j + 512], bank[6 + j][:, :]).then_inc(sem["gpg_ready"], 1)

            def hT_tiles(l):
                act.wait_ge(sem["mod_ready"], 3 + 2 * l)
                for k in range(0, KD, 2):
                    act.wait_ge(sem["xT_done"], KD * l + k + 1)
                    a.activation((hT, hlo1)[l][:, k, :], bank[k % 4][:, :], ACT.Identity, bias=mod[:, l, k:k + 1],
                                 scale=pre[:, l, k:k + 1]).then_inc(sem["hT_act"], 1)
                    if l == 1:
                        act.wait_ge(sem["hT_act"], 4 + k // 2 + 1)
                        a.copy(hTr[:, k, :], hlo1[:, k, :]).then_inc(sem["h_hi"], 1)
                        act.wait_ge(sem["hT_dve"], 4 + k // 2 + 1)
                        a.copy(hTr[:, k + 1, :], hlo1[:, k + 1, :]).then_inc(sem["h_hi"], 1)

            hT_tiles(0)

            def pj_wait(n):
                act.wait_ge(sem["pj_done"], n + 1)

            def z_tile(n, b, z, tanh, f, zn):
                pj_wait(n)
                if zn >= 2:
                    act.wait_ge(sem["z_pool"], zn - 1)
                link(a.copy(z[:, f, :], b[:, :]))
                a.activation(tanh[:, zn % 2, :], b[:, :], ACT.Tanh, scale=0.5).then_inc(sem["th_act"], 1)

            thj = th[:, 0, 0:256]

            def G_transposed(b0):
                for b in range(b0, b0 + 4):
                    act.wait_ge(sem["GT_done"], b + 1)
                    a.copy(GT[:, 4 * b:4 * b + 4, :].rearrange("p g n -> p (g n)"), bank[4 + b % 4][:, :]).then_inc(sem["GT_act"], 1)

            def K_blocks(hh):
                for b in range(4 * hh, 4 * hh + 4):
                    act.wait_ge(sem["Kc_done"], b + 1)
                    if b == 0:
                        act.wait_ge(sem["tab_cos"], 1)
                    if b == 4:
                        act.wait_ge(sem["T_stored"], 16 * L)
                    a.copy(Kh[0:NH, 4 * (b % 4):4 * (b % 4) + 4, :].rearrange("p g n -> p (g n)"),
                           bank[4 + b % 4][0:NH, :]).then_inc(sem["Kc_act"], 1)
                act.wait_ge(sem["T_zero"], 1)
                act.wait_ge(sem["Kc_act"], 4 * (hh + 1))
                for s in range(L):
                    act.dma_start(TP[NH * s:NH * s + NH, 16 * hh:16 * hh + 16, NH * s:P],
                                  Kh[0:NH, :, 0:P - NH * s]).then_inc(sem["T_stored"], 16)
            for n, tile in enumerate(PJ0):
                if tile[0] == "u":
                    pj_wait(n)
                    f = tile[1]
                    a.copy(uTp[:, f, :].rearrange("p (s c) -> p c s", s=L),
                           bank[n % 4][:, :].rearrange("p (c s) -> p c s", s=L)).then_inc(sem["pj_act"], 1)
                    act.wait_ge(sem["pj_act"], n + 1)
                    act.dma_start(scr_u[8 * f:8 * f + 8].rearrange("g h s c -> (g h) (s c)"), uTp[:, f, :]).then_inc(sem["u_stored"], 16)
                elif tile[0] == "cq":
                    pj_wait(n)
                    if n == 4:
                        act.wait_ge(sem["xT_done"], KD)
                    j, i = tile[1:]
                    link(a.activation(thj, bank[n % 4][:, 0:256], ACT.Square, accum_out=ssq_c[:, 4 * j + i:4 * j + i + 1]))
                    a.copy(cqt[:, i, 256 * j:256 * j + 256], bank[n % 4][:, 0:256]).then_inc(sem["pj_act"], 1)
                    if i == NT - 1 and j < 2:
                        G_transposed(4 * j)
                    elif i == NT - 1:
                        K_blocks(j - 2)
                elif tile[0] == "kpe":
                    pj_wait(n)
                    a.copy(kpT, bank[n % 4][:, :]).then_inc(sem["pj_act"], 1)
                    act.wait_ge(sem["u_stored"], 64)
                    act.wait_ge(sem["r8_ready"], 1)
                    for s in range(L):
                        act.dma_start(U[NH * s:NH * s + NH, :, :], scr_u[:, :, s, :].rearrange("g h c -> h g c")).then_inc(sem["u_back"], 16)
                elif tile[0] == "za":
                    if tile[1] == 0:
                        act.wait_ge(sem["T_stored"], 32 * L)
                    z_tile(n, bank[n % 4], zaT, th, tile[1], tile[1])
                    if tile[1] == 3:
                        for b in range(4):
                            act.wait_ge(sem["Y_done"], b + 1)
                            a.copy(Yb[:, 8 * b:8 * b + 8, :].rearrange("p g n -> p (g n)"), bank[4 + b][:, :]).then_inc(sem["Y_act"], 1)
                        act.wait_ge(sem["Y_act"], 4)
                        for s in range(L):
                            act.dma_start(scr_y[:, :, s, :].rearrange("g h c -> h g c"), Yb[NH * s:NH * s + NH, :, :]).then_inc(sem["y_stored"], 16)
                        act.wait_ge(sem["y_stored"], 16 * L)
                        act.dma_start(yT, scr_y.rearrange("(f a) h s c -> (a h) f (s c)", f=4)).then_inc(sem["y_back"], 16)
                else:
                    z_tile(n, bank[n % 4], zbT, th, tile[1], 4 + tile[1])

            for f in range(8):
                act.wait_ge(sem["cqT_done"], f + 1)
                dst = cqT[:, f, :] if f < 6 else ckvT[:, f - 6, :]
                a.activation(dst, bank[4 + f % 4][:, :], ACT.Copy, scale=col[:, V_QN + f:V_QN + f + 1]).then_inc(sem["cqT_act"], 1)
            act.wait_ge(sem["y_skip"], 4)
            a.activation(y2.rearrange("p f n -> p (f n)"), yT.rearrange("p f n -> p (f n)"), ACT.Square).then_inc(sem["y_sq"], 1)
            act.wait_ge(sem["y_arg"], 1)
            a.activation(y2.rearrange("p f n -> p (f n)"), y2.rearrange("p f n -> p (f n)"), ACT.Tanh, scale=C_GELU).then_inc(sem["y_tanh"], 1)
            for n in range(6):
                if n % 3 < 2:
                    act.wait_ge(sem["q_done"], n + 1)
                    a.copy(qnT[:, 2 * (n // 3) + n % 3, :], bank[n % 4][:, :]).then_inc(sem["q_act"], 1)
            for n in range(8):
                act.wait_ge(sem["kv_done"], n + 1)
                dst = knT[:, n, :] if n < 4 else vM[:, n - 4, :]
                a.copy(dst, bank[4 + n % 4][:, :]).then_inc(sem["kv_act"], 1)

            for f in range(4):
                act.wait_ge(sem["glu_done"], f + 1)
                a.activation(y2[:, f, :], bank[f][:, :], ACT.Tanh, scale=0.25, bias=hbg[:, f:f + 1]).then_inc(sem["glu_act"], 1)

            def mix_high(l, f, mix):
                if l == 0 and f < 4:
                    act.wait_ge(sem["ya_ready"], f + 1)
                else:
                    act.wait_ge(sem["o_dve"], f - 3 if l == 0 else MH + f + 1)
                a.copy(hTr[:, f, :], mix[:, f, :]).then_inc(sem["mix_hi"], 1)

            def attend(l, units, n0, Pb, PTb, nP, mix):
                N, per = len(units), len(units) // (MH, HN)[l]
                for n in range(N + 6):
                    if l == 0 and 2 <= n < 6:
                        mix_high(0, n - 2, mix)
                    if n >= 6 and (n - 5) % per == 0:
                        mix_high(l, (n - 5) // per - 1 + (4, 0)[l], mix)
                    if n < N:
                        h, i, b = units[n]
                        w = P * (i + 1)
                        act.wait_ge(sem["s_max"], n0 + n + 1)
                        if n >= nP:
                            act.wait_ge(sem["pt_done"], n0 + n - nP + 1)
                        a.activation(Pb[:, n % nP, 0:w], bank[SB[n % 3]][:, 0:w], ACT.Exp, bias=smax[:, n % 4:n % 4 + 1],
                                     accum_out=ssum[:, n % 4:n % 4 + 1]).then_inc(sem["s_exp"], 1)
                    m = n - 2
                    if 0 <= m < N and m % 2 == 0:
                        w = P * (units[m][1] + 1)
                        act.wait_ge(sem["pt_done"], n0 + m + 1)
                        if m >= 2:
                            act.wait_ge(sem["pv_done"], n0 + m - 1)
                        a.copy(PTb[:, m % 2, 0:w], bank[TB[m % 2]][:, 0:w]).then_inc(sem["pt_act"], 1)

            act.wait_ge(sem["rope_done"], 3)
            split_high(act, a, SPLIT[0])
            act.wait_ge(sem["msum_done"], 6)
            attend(0, U0, 0, Pm, PT, 3, mixT)
            for n in range(1, 5):
                split_high(act, a, SPLIT[n])

            def y_squares(l):
                for i in range(NT):
                    act.wait_ge(sem["out_done"], NT * l + i + 1)
                    for e in range(2):
                        if i:
                            act.wait_ge(sem["out_sq"], 2 * (NT * l + i - 1) + e + 1)
                        ins = a.activation(sqj[:, e, :], bank[2 * i + e][:, :], ACT.Square, accum_out=sso[:, 2 * i + e:2 * i + e + 1])
                        ins.then_inc(sem["out_sq"], 1)

            y_squares(0)

            squares(1)
            for j in range(2):
                act.wait_ge(sem["gpg_done"], 3 + j)
                a.copy(gpg[:, 512 * j:512 * j + 512], bank[6 + j][:, :]).then_inc(sem["gpg_ready"], 1)
            act.wait_ge(sem["xn_ready"], 2 * NT)
            act.dma_start(th1[:, 0, :].bitcast(I32), t["positions"].to_broadcast([P, S])).then_inc(sem["pos_loaded"], 16)
            split_high(act, a, SPLIT[5])
            a.copy(wgate_hi[:], wgate[:]).then_inc(sem["gate_w"], 1)
            hT_tiles(1)
            sines(1, tabN[:, 1, :], tabN[:, 0, :], cst[:, 2:3], rt1[:, 0, :], rt1[:, 1, :])
            n0 = NJ0

            def hidden():
                for b in range(2):
                    src = bank[4 + b][0:NB, 0:CH].rearrange("p (e n) -> p e n", e=2)
                    if b == 1:
                        split_high(act, a, ("z", 0))
                        split_high(act, a, ("z", 1))
                    act.wait_ge(sem["hid_done"], b + 1)
                    a.copy(hid[b][0:NB], src).then_inc(sem["hid_sq"], 1)
                    a.activation(hsq[b][0:NB], src, ACT.Square).then_inc(sem["hid_sq"], 1)
                for b in range(2):
                    act.wait_ge(sem["hid_arg"], b + 1)
                    a.activation(hsq[b][0:NB], hsq[b][0:NB], ACT.Tanh, scale=C_GELU).then_inc(sem["hid_tanh"], 1)

            for n, tile in enumerate(PJ1):
                kind, b = tile[0], bank[n % 4]
                if next_split(n) and tile != ("z", 4):
                    split_high(act, a, next_split(n))
                if tile == ("z", 0):
                    hidden()
                if tile == ("z", 4):
                    for b2 in range(2):
                        act.wait_ge(sem["hidT_done"], b2 + 1)
                        a.copy(hidT[b2], bank[6 + b2][:, 0:P].rearrange("p (e n) -> p e n", e=2)[:, :, 0:NB]).then_inc(sem["hidT_act"], 1)
                    split_high(act, a, next_split(n))
                    act.wait_ge(sem["cmp_done"], 2)
                    act.wait_ge(sem["pad_ready"], 1)
                    a.mul(vc[0:NCMP].rearrange("p g n -> p (g n)"), bank[5][0:NCMP, 0:GN * DN], 0.5).then_inc(sem["cmp_act"], 1)
                if tile == ("z", 6):
                    for g in range(GN):
                        act.wait_ge(sem["cs_sub"], g + 1)
                        pc = Pc[g].rearrange("p a n -> p (a n)")
                        a.activation(pc, pc, ACT.Exp).then_inc(sem["cs_exp"], 1)
                if kind in ("v", "gate", "z"):
                    pj_wait(n0 + n)
                if kind == "v":
                    a.copy((vs, vw)[tile[1]][:, tile[2], :], b[:, 0:256]).then_inc(sem["v_act"], 1)
                elif kind == "gate":
                    a.activation(gT[0:3 * HN], b[0:3 * HN, :], ACT.Tanh, scale=0.5).then_inc(sem["gate_act"], 1)
                elif kind == "z":
                    z_tile(n0 + n, b, zT, th1, tile[1], 8 + tile[1])
            split_high(act, a, ("wout1", 1))
            act.wait_ge(sem["pad_ready"], 2)
            for h in range(HN):
                act.wait_ge(sem["cpt_done"], h + 1)
                a.copy(PcT[0:NCMP, h, :], bank[h % 2][0:NCMP, :]).then_inc(sem["cpt_act"], 1)
            attend(1, U1, N0, Pm1, PT1, 3, mix1)
            for j in range(2, 4):
                split_high(act, a, ("wout1", j))
            y_squares(1)

        @block.vector
        def _(dve):
            v = nc.vector
            chain = [0]

            def link(ins):
                chain[0] += 1
                ins.then_inc(sem["dve_chain"], 1)
                dve.wait_ge(sem["dve_chain"], chain[0])

            X = lambda n: small[0:32, NPW + n, :]
            v.memset(halfpi[:], math.pi / 2).then_inc(sem["masks_ready"], 1)
            v.memset(small[0:32, iP, :], 1.0).then_inc(sem["dve_chain"], 1)
            for r in (iP + TAPS, iF + L, iC + L):
                v.memset(small[0:32, r, :], 0.0).then_inc(sem["dve_chain"], 1)
            for r in (iF, iC):
                v.memset(small[0:32, r, :], 1.0).then_inc(sem["dve_chain"], 1)
            chain[0] += 6

            def reduce_angle(k, r, ang, absr):
                link(v.tensor_scalar(k, ang, 1.0 / TWO_PI, MAGIC, ALU.mult, ALU.add))
                link(v.tensor_scalar(k, k, MAGIC, None, ALU.subtract))
                link(v.scalar_tensor_tensor(r, k, -PI_A, ang, ALU.mult, ALU.add))
                link(v.scalar_tensor_tensor(r, k, -PI_B, r, ALU.mult, ALU.add))
                link(v.scalar_tensor_tensor(r, k, -PI_C, r, ALU.mult, ALU.add))
                link(v.tensor_scalar(r, r, PI_SAFE, -PI_SAFE, ALU.min, ALU.max))
                return v.scalar_tensor_tensor(absr, r, -1.0, r, ALU.mult, ALU.max)

            dve.wait_ge(sem["lam_exp"], 1)
            v.tensor_scalar(X(2), X(0), dtc, None, ALU.mult).then_inc(sem["lam_red"], 1)
            link(v.tensor_scalar(X(3), X(1), dtc, None, ALU.mult))
            reduce_angle(X(4), X(5), X(3), X(6)).then_inc(sem["lam_red"], 1)
            dve.wait_ge(sem["colT_done"], 2)
            v.tensor_copy(col[:], bank[0][:, 0:V_N]).then_inc(sem["col_ready"], 1)
            v.tensor_copy(peT[:], bank[0][:, 128:192]).then_inc(sem["col_ready"], 1)
            dve.wait_ge(sem["pos_loaded"], 16)
            dve.wait_ge(sem["const_loaded"], 16)
            link(v.tensor_copy(rk, posi))
            link(v.tensor_scalar(posb, rk, cst[:, 1:2], None, ALU.mult))
            reduce_angle(rk, ra, posb, rk).then_inc(sem["tab_abs"], 1)
            dve.wait_ge(sem["sc_ready"], 1)
            dve.wait_ge(sem["col_ready"], 2)
            link(v.scalar_tensor_tensor(sc[:], sct[:], 1.0, col[:, V_C:V_C + KD], ALU.add, ALU.mult))
            v.tensor_scalar(sc[:], sc[:], 0.5, None, ALU.mult).then_inc(sem["sc_ready"], 1)

            def mean_squares(l):
                for i in range(NT):
                    dve.wait_ge(sem["ssq_done"], NT * l + i + 1)
                    v.tensor_scalar(msx[:, i:i + 1], ssx[:, i:i + 1], 1.0 / D, EPS, ALU.mult, ALU.add).then_inc(sem["msq_done"], 1)

            def normalise(l, dst):
                for i in range(NT):
                    dve.wait_ge(sem["rstd_ready"], NT * l + i + 1)
                    v.tensor_scalar(dst[:, i, :], xr[:, i, :], rsx[:, i:i + 1], None, ALU.mult).then_inc(sem["xn_ready"], 1)

            mean_squares(0)
            normalise(0, xr)

            tt = [at(oD + 2048 + 256 * q, 4, NP_) for q in range(4)]

            def cmul(o_re, o_im, a_re, a_im, b_re, b_im, n, last=False):
                T0, T1, T2, T3 = (q[0:32, 0:n, :] for q in tt)
                v.tensor_tensor(T0, a_re, b_re, ALU.mult).then_inc(sem["dve_chain"], 1)
                v.tensor_tensor(T1, a_im, b_im, ALU.mult).then_inc(sem["dve_chain"], 1)
                v.tensor_tensor(T2, a_re, b_im, ALU.mult).then_inc(sem["dve_chain"], 1)
                chain[0] += 3
                link(v.tensor_tensor(T3, a_im, b_re, ALU.mult))
                v.tensor_tensor(o_re, T0, T1, ALU.subtract).then_inc(sem["dve_chain"], 1)
                chain[0] += 1
                ins = v.tensor_tensor(o_im, T2, T3, ALU.add)
                if last:
                    ins.then_inc(sem["pw_ready"], 1)
                else:
                    link(ins)

            def sm(a0, n):
                return small[0:32, a0:a0 + n, :]

            def one(a0, n):
                return small[0:32, a0:a0 + 1, :].to_broadcast([32, n, NP_])

            dve.wait_ge(sem["lam_exp"], 3)
            dve.wait_ge(sem["lam_sin"], 2)
            v.tensor_tensor(sm(iP + 1, 1), sm(NPW + 9, 1), sm(NPW + 8, 1), ALU.mult).then_inc(sem["dve_chain"], 1)
            chain[0] += 1
            link(v.tensor_tensor(sm(iP + TAPS + 1, 1), sm(NPW + 9, 1), sm(NPW + 7, 1), ALU.mult))
            link(v.tensor_tensor(X(10), X(0), X(0), ALU.mult))
            link(v.tensor_tensor(X(11), X(1), X(1), ALU.mult))
            link(v.tensor_tensor(X(10), X(10), X(11), ALU.add))
            link(v.reciprocal(X(10), X(10)))
            link(v.tensor_scalar(X(11), small[0:32, iP + 1, :], 1.0, None, ALU.subtract))
            ni = small[0:32, iP + TAPS + 1, :]
            link(v.tensor_tensor(X(12), X(11), X(0), ALU.mult))
            link(v.tensor_tensor(X(13), ni, X(1), ALU.mult))
            link(v.tensor_tensor(X(12), X(12), X(13), ALU.add))
            link(v.tensor_tensor(small[0:32, iX, :], X(12), X(10), ALU.mult))
            link(v.tensor_tensor(X(12), ni, X(0), ALU.mult))
            link(v.tensor_tensor(X(13), X(11), X(1), ALU.mult))
            link(v.tensor_tensor(X(12), X(12), X(13), ALU.subtract))
            link(v.tensor_tensor(small[0:32, iX + 1, :], X(12), X(10), ALU.mult))
            p, q = iP, iP + TAPS
            cmul(sm(p + 2, 1), sm(q + 2, 1), sm(p + 1, 1), sm(q + 1, 1), sm(p + 1, 1), sm(q + 1, 1), 1)
            cmul(sm(p + 3, 2), sm(q + 3, 2), sm(p + 1, 2), sm(q + 1, 2), one(p + 2, 2), one(q + 2, 2), 2)
            cmul(sm(p + 5, 4), sm(q + 5, 4), sm(p + 1, 4), sm(q + 1, 4), one(p + 4, 4), one(q + 4, 4), 4)
            cmul(sm(NPW + 14, 1), sm(NPW + 15, 1), sm(NPW + 8, 1), sm(NPW + 7, 1), sm(NPW + 8, 1), sm(NPW + 7, 1), 1)
            w_re, w_im = NPW + 14, NPW + 15

            def square():
                cmul(sm(w_re, 1), sm(w_im, 1), sm(w_re, 1), sm(w_im, 1), sm(w_re, 1), sm(w_im, 1), 1)

            square()
            square()
            for base in (iF, iC):
                p, q = base, base + L
                for n in (1, 2, 4):
                    end = base == iC and n == 4
                    cmul(sm(p + n, n), sm(q + n, n), sm(p, n), sm(q, n), one(w_re, n), one(w_im, n), n, last=end)
                    if not end:
                        square()

            def scales(l):
                v.scalar_tensor_tensor(pre[:, l, :], mod[:, l, KD:2 * KD], 1.0, col[:, V_PRE + KD * l:V_PRE + KD * l + KD], ALU.add, ALU.mult).then_inc(sem["mod_ready"], 1)
                v.tensor_tensor(gcol[:, l, :], mod[:, l, 2 * KD:], col[:, V_POST + KD * l:V_POST + KD * l + KD], ALU.mult).then_inc(sem["mod_ready"], 1)

            def modulation0():
                dve.wait_ge(sem["mcol_done"], 6)
                v.tensor_tensor(mod[:, 0, :], bank[1][:, 0:24], col[:, V_BADA:V_BADA + 24], ALU.add).then_inc(sem["mod_ready"], 1)
                dve.wait_ge(sem["mod_ready"], 1)
                scales(0)

            def modulation1_sums(j0, j1):
                for j in range(j0, j1):
                    key = ("ada", 1, j)
                    w_ready(dve, key)
                    link(v.tensor_scalar(macc[j], slot(key)[:, 0, :], sc[:, 0:1], None, ALU.mult))
                    for k in range(1, KD):
                        ins = v.scalar_tensor_tensor(macc[j], slot(key)[:, k, :], sc[:, k:k + 1], macc[j], ALU.mult, ALU.add)
                        if k < KD - 1:
                            link(ins)
                    ins.then_inc(sem["macc_done"], 1)

            def modulation1(d0):
                for d in range(d0, d0 + 3):
                    dve.wait_ge(sem["msum_done"], d + 1)
                    v.tensor_tensor(mod[:, 1, 4 * d:4 * d + 4], bank[MB[d // 3][d % 3]][:, 0:512:P], col[:, V_BADA + 24 + 4 * d:V_BADA + 28 + 4 * d], ALU.add).then_inc(sem["mod1_ready"], 1)
                if d0 == 3:
                    dve.wait_ge(sem["mod1_ready"], 6)
                    scales(1)

            modulation0()

            def hT_tiles(l):
                dve.wait_ge(sem["mod_ready"], 3 + 2 * l)
                for k in range(1, KD, 2):
                    dve.wait_ge(sem["xT_done"], KD * l + k + 1)
                    v.tensor_scalar((hT, hlo1)[l][:, k, :], bank[k % 4][:, :], pre[:, l, k:k + 1], mod[:, l, k:k + 1], ALU.mult, ALU.add).then_inc(sem["hT_dve"], 1)
                    if l == 1:
                        for k2 in (k - 1, k):
                            h_low(k2)

            def h_low(k):
                dve.wait_ge(sem["h_hi"], k + 1)
                v.tensor_tensor(hlo1r[:, k, :], hlo1[:, k, :], hTr[:, k, :].bitcast(F32), ALU.subtract).then_inc(sem["h_lo"], 1)

            hT_tiles(0)

            dve.wait_ge(sem["st_act"], 8)
            dve.wait_ge(sem["B_ready"], 1)
            fr = st[:, iX, :].unsqueeze(2).to_broadcast([P, NG, NH])
            fi = st[:, iX + 1, :].unsqueeze(2).to_broadcast([P, NG, NH])
            tb = at(oD + 2048, NG, NH)
            link(v.tensor_tensor(Bb, BA, fr, ALU.mult))
            link(v.tensor_tensor(tb, BB, fi, ALU.mult))
            link(v.tensor_tensor(Bb, Bb, tb, ALU.add))
            link(v.tensor_tensor(iBb, BB, fr, ALU.mult))
            link(v.tensor_tensor(tb, BA, fi, ALU.mult))
            link(v.tensor_tensor(iBb, iBb, tb, ALU.subtract))
            dve.wait_ge(sem["CT_done"], 1)
            def powers(base, n, qq, rev):
                a_ = st[:, base:base + n, 8 * qq:8 * qq + 8]
                if rev:
                    a_ = a_[:, ::-1, :]
                return a_.rearrange("p t g -> p g t").unsqueeze(3).to_broadcast([P, 8, n, NH])

            def per_tap(m, n, qq):
                return m[:, 8 * qq:8 * qq + 8, :].unsqueeze(2).to_broadcast([P, 8, n, NH])

            for qq in range(4):
                if qq >= 2:
                    dve.wait_ge(sem["GT_done"], 2 * (qq - 1))
                G4 = Gc[qq % 2].rearrange("p g (s h) -> p g s h", s=L)
                T4 = tmpG[:, :, 0:L * NH].rearrange("p g (s h) -> p g s h", s=L)
                link(v.tensor_tensor(G4, powers(iP, L, qq, True), per_tap(Bb, L, qq), ALU.mult))
                link(v.tensor_tensor(T4, powers(iP + TAPS, L, qq, True), per_tap(iBb, L, qq), ALU.mult))
                v.tensor_tensor(G4, G4, T4, ALU.add).then_inc(sem["G_ready"], 1)
            dve.wait_ge(sem["C_act"], 3)
            for qq in range(4):
                W4 = W1[:, 8 * qq:8 * qq + 8, :].rearrange("p g (s h) -> p g s h", s=TAPS)
                T4 = tmpG.rearrange("p g (s h) -> p g s h", s=TAPS)
                dve.wait_ge(sem["G_ready"], 4)
                link(v.tensor_tensor(W4, powers(iP, TAPS, qq, False), per_tap(C1, TAPS, qq), ALU.mult))
                link(v.tensor_tensor(T4, powers(iP + TAPS, TAPS, qq, False), per_tap(C2, TAPS, qq), ALU.mult))
                v.tensor_tensor(W4, W4, T4, ALU.add).then_inc(sem["W1_ready"], 1)
            for qq in range(2):
                gs = slice(16 * qq, 16 * qq + 16)

                def co(base):
                    return st[:, base:base + L, gs].rearrange("p a g -> p g a").unsqueeze(3).to_broadcast([P, 16, L, L])

                def fi_(base):
                    return st[:, base:base + L, gs].rearrange("p b g -> p g b").unsqueeze(2).to_broadcast([P, 16, L, L])

                c4 = rotc[:, gs, :].rearrange("p g (a b) -> p g a b", a=L)
                s4 = rots[:, gs, :].rearrange("p g (a b) -> p g a b", a=L)
                t4 = at(oD + 2048, 16, L, L)
                link(v.tensor_tensor(c4, co(iC), fi_(iF), ALU.mult))
                link(v.tensor_tensor(t4, co(iC + L), fi_(iF + L), ALU.mult))
                link(v.tensor_tensor(c4, c4, t4, ALU.subtract))
                link(v.tensor_tensor(s4, co(iC), fi_(iF + L), ALU.mult))
                link(v.tensor_tensor(t4, co(iC + L), fi_(iF), ALU.mult))
                link(v.tensor_tensor(s4, s4, t4, ALU.add))
            v.tensor_scalar(rots[0:64], rots[0:64], -1.0, None, ALU.mult).then_inc(sem["rot_ready"], 1)
            dve.wait_ge(sem["GT_done"], 8)
            link(v.tensor_copy(r8b, st[:, iX + 2, :].unsqueeze(2).to_broadcast([P, NG, NC])))
            v.memset(Xs[:, :, 0:1], 0.0).then_inc(sem["zero_ready"], 1)
            v.memset(r8b[:, :, 0:1], 0.0).then_inc(sem["r8_ready"], 1)
            dve.wait_ge(sem["r8_ready"], 1)
            dve.wait_ge(sem["rot_ready"], 1)

            dve.wait_ge(sem["pj_act"], 20)
            link(v.tensor_tensor(msq_c[:, 0:4], ssq_c[:, 0:4], ssq_c[:, 4:8], ALU.add))
            link(v.tensor_tensor(msq_c[:, 0:4], msq_c[:, 0:4], ssq_c[:, 8:12], ALU.add))
            link(v.tensor_scalar(msq_c[:, 4:8], ssq_c[:, 12:16], 1.0 / KVR, EPS, ALU.mult, ALU.add))
            v.tensor_scalar(msq_c[:, 0:4], msq_c[:, 0:4], 1.0 / QR, EPS, ALU.mult, ALU.add).then_inc(sem["cq_msq"], 1)

            for hh in range(2):
                if hh == 1:
                    dve.wait_ge(sem["Xs_ready"], 1)
                zv, tv = zb5.rearrange("p g c -> p (g c)"), tb5.rearrange("p g c -> p (g c)")
                rc = rotc[:, 16 * hh:16 * hh + 16, :].rearrange("p g c -> p (g c)")
                rs = rots[:, 16 * hh:16 * hh + 16, :].rearrange("p g c -> p (g c)")
                for b in range(2):
                    dve.wait_ge(sem["V_done"], 2 * hh + b + 1)
                    vb, cs = bank[4 + 2 * hh + b], slice(512 * b, 512 * b + 512)
                    v.tensor_tensor(tv[0:64, cs], vb[64:128, :], rs[64:128, cs], ALU.mult).then_inc(sem["dve_chain"], 1)
                    v.tensor_tensor(tv[64:128, cs], vb[0:64, :], rs[0:64, cs], ALU.mult).then_inc(sem["dve_chain"], 1)
                    v.tensor_tensor(zv[:, cs], vb[:, :], rc[:, cs], ALU.mult).then_inc(sem["z_dve"], 1)
                    chain[0] += 2
                dve.wait_ge(sem["dve_chain"], chain[0])
                dve.wait_ge(sem["z_dve"], 2 * hh + 2)
                link(v.tensor_tensor(zv, zv, tv, ALU.add))
                link(v.tensor_tensor_scan(tv, r8b[:, 16 * hh:16 * hh + 16, :].rearrange("p g c -> p (g c)"), zv, 0.0, ALU.mult, ALU.add))
                link(v.tensor_tensor(zv[0:64], tv[64:128], rs[64:128], ALU.mult))
                link(v.tensor_tensor(zv[64:128], tv[0:64], rs[0:64], ALU.mult))
                link(v.tensor_tensor(tv, tv, rc, ALU.mult))
                if hh == 1:
                    dve.wait_ge(sem["Y_done"], 2)
                v.tensor_tensor(Xs[:, :, 1:], tb5, zb5, ALU.subtract).then_inc(sem["Xs_ready"], 1)

            dve.wait_ge(sem["Y_done"], 4)
            modulation1_sums(0, 6)

            dve.wait_ge(sem["y_back"], 16)
            for f in range(4):
                v.scalar_tensor_tensor(yT[:, f, :], uTp[:, f, :], col[:, V_DSK + f:V_DSK + f + 1], yT[:, f, :], ALU.mult, ALU.add).then_inc(sem["y_skip"], 1)
            dve.wait_ge(sem["y_sq"], 1)
            yv, sv = yT.rearrange("p f n -> p (f n)"), y2.rearrange("p f n -> p (f n)")
            link(v.tensor_scalar(sv, sv, 0.044715, 1.0, ALU.mult, ALU.add))
            v.tensor_tensor(sv, sv, yv, ALU.mult).then_inc(sem["y_arg"], 1)
            dve.wait_ge(sem["y_tanh"], 1)
            v.scalar_tensor_tensor(yv, sv, 1.0, yv, ALU.add, ALU.mult).then_inc(sem["y_gelu"], 1)
            dve.wait_ge(sem["y_gelu"], 1)

            def rope(dst, x, cos, sin, q, tmp, scalar=1.0):
                A, B = tmp
                link(v.scalar_tensor_tensor(A, x, scalar, cos, ALU.mult, ALU.mult))
                for b0 in range(0, P, 2 * q):
                    lo, hi = slice(b0, b0 + q), slice(b0 + q, b0 + 2 * q)
                    link(v.scalar_tensor_tensor(B[lo], x[hi], scalar, sin[hi], ALU.mult, ALU.mult))
                    link(v.scalar_tensor_tensor(B[hi], x[lo], scalar, sin[lo], ALU.mult, ALU.mult))
                return v.tensor_tensor(dst, A, B, ALU.add)

            dve.wait_ge(sem["tab_cos"], 1)
            rt = (rtmp[:, 0, :], rtmp[:, 1, :])
            rope(kpT, kpT, tabM[:, 0, :], tabM[:, 1, :], 32, rt).then_inc(sem["rope_done"], 1)
            dve.wait_ge(sem["rope_done"], 1)
            v.tensor_copy(kz[64:128], kpT[64:128]).then_inc(sem["kz_ready"], 1)
            v.memset(kz[0:64], 0.0).then_inc(sem["kz_ready"], 1)
            dve.wait_ge(sem["kz_ready"], 1)
            v.memset(kpT[64:128], 0.0).then_inc(sem["kz_ready"], 1)
            for j in range(2):
                dve.wait_ge(sem["q_done"], 3 * j + 3)
                dve.wait_ge(sem["rope_done"], j + 1)
                rope(qpT[:, j, :], bank[(3 * j + 2) % 4][:, :], tabM[:, 0, :], tabM[:, 1, :], 32, rt).then_inc(sem["rope_done"], 1)
                if j == 0:
                    dve.wait_ge(sem["pj_done"], NJ0)
                    modulation1_sums(6, 8)
            modulation1(0)
            modulation1_sums(8, 12)
            dve.wait_ge(sem["z_pool"], 4)
            for f in range(4):
                dve.wait_ge(sem["glu_act"], f + 1)
                link(v.scalar_tensor_tensor(y2[:, f, :], y2[:, f, :], 1.0, yT[:, f, :], ALU.add, ALU.mult))
                v.scalar_tensor_tensor(mixT[:, f, :].rearrange("p (c s) -> p s c", s=L), y2[:, f, :].rearrange("p (s c) -> p s c", s=L),
                                       0.125, zaT[:, f, :].rearrange("p (c s) -> p s c", s=L), ALU.mult, ALU.mult).then_inc(sem["ya_ready"], 1)

            def mix_low(l, f, mix):
                dve.wait_ge(sem["mix_hi"], 8 * l + f + 1)
                v.tensor_tensor(mixr[l][:, f, :], mix[:, f, :], hTr[:, f, :].bitcast(F32), ALU.subtract).then_inc(sem["mix_lo"], 1)

            def attend(l, units, n0, Pb, PTb, nP, heads, mix, z, gated):
                N, per = len(units), len(units) // heads
                f0 = (4, 0)[l]
                for n in range(N + 6):
                    if l == 0 and 4 <= n < 8:
                        mix_low(0, n - 4, mix)
                    if n >= 7 and (n - 6) % per == 0:
                        mix_low(l, (n - 6) // per - 1 + f0, mix)
                    if n < N:
                        w = P * (units[n][1] + 1)
                        dve.wait_ge(sem["s_done"], n0 + n + 1)
                        v.reduce_max(smax[:, n % 4:n % 4 + 1], bank[SB[n % 3]][:, 0:w], AX.X, negate=True).then_inc(sem["s_max"], 1)
                    m = n - 1
                    if 0 <= m < N:
                        h, i, b = units[m]
                        w = P * (i + 1)
                        dve.wait_ge(sem["s_exp"], n0 + m + 1)
                        link(v.reciprocal(srec[:, m % 4:m % 4 + 1], ssum[:, m % 4:m % 4 + 1]))
                        pb = Pb[:, m % nP, 0:w]
                        if gated:
                            v.tensor_scalar(pb, pb, srec[:, m % 4:m % 4 + 1], gates[:, i, 3 * h + b + 1:3 * h + b + 2], ALU.mult, ALU.mult).then_inc(sem["s_scaled"], 1)
                        else:
                            v.tensor_scalar(pb, pb, srec[:, m % 4:m % 4 + 1], None, ALU.mult).then_inc(sem["s_scaled"], 1)
                    m = n - 2
                    if 0 <= m < N and m % 2 == 1:
                        w = P * (units[m][1] + 1)
                        dve.wait_ge(sem["pt_done"], n0 + m + 1)
                        if m >= 2:
                            dve.wait_ge(sem["pv_done"], n0 + m - 1)
                        v.tensor_copy(PTb[:, m % 2, 0:w], bank[TB[m % 2]][:, 0:w]).then_inc(sem["pt_dve"], 1)
                    m = n - 4
                    if 0 <= m < N and (m + 1) % per == 0:
                        h = m // per
                        dve.wait_ge(sem["pv_done"], n0 + m + 1)
                        v.scalar_tensor_tensor(mix[:, f0 + h, :], bank[OB[h % 2]][:, :], 0.5, z[:, h, :], ALU.mult, ALU.mult).then_inc(sem["o_dve"], 1)

            modulation1(3)
            dve.wait_ge(sem["z_pool"], 8)
            split_low(dve, v, SPLIT[0])
            attend(0, U0, 0, Pm, PT, 3, MH, mixT, zbT, False)
            mix_low(0, 7, mixT)
            for n in range(1, 5):
                split_low(dve, v, SPLIT[n])

            def output(l, tmp):
                for i in range(NT):
                    dve.wait_ge(sem["out_sq"], 2 * (NT * l + i + 1))
                    link(v.tensor_tensor(mso[:, i:i + 1], sso[:, 2 * i:2 * i + 1], sso[:, 2 * i + 1:2 * i + 2], ALU.add))
                    v.tensor_scalar(mso[:, i:i + 1], mso[:, i:i + 1], 1.0 / D, EPS, ALU.mult, ALU.add).then_inc(sem["out_msq"], 1)
                    dve.wait_ge(sem["gpg_ready"], 2 * (l + 1))
                    dve.wait_ge(sem["out_rstd"], NT * l + i + 1)
                    if i >= 2:
                        dve.wait_ge(sem["out_res"], NT * l + i - 1)
                    link(v.scalar_tensor_tensor(tmp[:, i % 2, 0:512], bank[2 * i][:, :], rso[:, i:i + 1], gpg[:, 0:512], ALU.mult, ALU.mult))
                    v.scalar_tensor_tensor(tmp[:, i % 2, 512:], bank[2 * i + 1][:, :], rso[:, i:i + 1], gpg[:, 512:], ALU.mult, ALU.mult).then_inc(sem["out_gpg"], 1)

            output(0, otmp)
            mean_squares(1)
            normalise(1, xn1)
            split_low(dve, v, SPLIT[5])
            hT_tiles(1)
            dve.wait_ge(sem["gate_w"], 1)
            v.tensor_tensor(wgater[:], wgate[:], wgate_hi[:].bitcast(F32), ALU.subtract).then_inc(sem["gate_w"], 1)
            dve.wait_ge(sem["pos_loaded"], 32)
            ang = th1[:, 0, :]
            link(v.tensor_copy(rt1[:, 1, :], ang.bitcast(I32)))
            link(v.tensor_scalar(ang, rt1[:, 1, :], cst[:, 0:1], None, ALU.mult))
            reduce_angle(rt1[:, 1, :], rt1[:, 0, :], ang, rt1[:, 1, :]).then_inc(sem["tab_abs"], 1)
            dve.wait_ge(sem["tab_cos"], 2)
            link(v.tensor_scalar(tabN[:, 2:4, :].rearrange("p a n -> p (a n)"), tabN[:, 0:2, :].rearrange("p a n -> p (a n)"), NSCALE, None, ALU.mult))
            n0 = len(PJ0)
            rt = (rt1[:, 0, :], rt1[:, 1, :])
            for n, tile in enumerate(PJ1):
                kind, b = tile[0], bank[n % 4]
                if kind != "z" and next_split(n):
                    split_low(dve, v, next_split(n))
                if kind in ("cmp", "k", "q"):
                    dve.wait_ge(sem["pj_done"], n0 + n + 1)
                if kind == "cmp":
                    kv, gg = tile[1:]
                    for e in range(2):
                        ins = v.tensor_tensor(R[kv][:, CS * e:CS * e + CS, gg, :],
                                              b[:, CS * e:CS * e + CS * NCMP].rearrange("p (n l) -> p l n", l=CS),
                                              peT[:, CL * kv + CS * e:CL * kv + CS * e + CS].unsqueeze(2).to_broadcast([P, CS, NCMP]), ALU.add)
                        ins.then_inc(sem["kc_ready"], 1)
                elif kind == "k":
                    rope((ksT, kwT)[tile[1]][:, tile[2], :], b[:, :], tabN[:, 2, :], tabN[:, 3, :], 64, rt).then_inc(sem["rope1"], 1)
                    dve.wait_ge(sem["rope1"], sum(x[0] in ("k", "q") for x in PJ1[:n + 1]))
                elif kind == "q":
                    rope(qT[:, tile[1], :], b[:, :], tabN[:, 0, :], tabN[:, 1, :], 64, rt).then_inc(sem["rope1"], 1)
                    dve.wait_ge(sem["rope1"], sum(x[0] in ("k", "q") for x in PJ1[:n + 1]))
            dve.wait_ge(sem["gT_done"], 1)
            v.tensor_scalar(gates.rearrange("p i n -> p (i n)"), bank[6][:, 0:NT * 3 * HN], 0.5, 0.5, ALU.mult, ALU.add).then_inc(sem["gate_ready"], 1)
            split_low(dve, v, ("z", 0))
            for b in range(2):
                dve.wait_ge(sem["hid_sq"], 2 * (b + 1))
                hv, qv = hid[b][0:NB], hsq[b][0:NB]
                link(v.tensor_scalar(qv, qv, 0.044715, 1.0, ALU.mult, ALU.add))
                v.tensor_tensor(qv, qv, hv, ALU.mult).then_inc(sem["hid_arg"], 1)
            for b in range(2):
                hv, qv = hid[b][0:NB], hsq[b][0:NB]
                dve.wait_ge(sem["hid_tanh"], b + 1)
                v.scalar_tensor_tensor(hv, qv, 1.0, hv, ALU.add, ALU.mult).then_inc(sem["hid_ready"], 1)
            split_low(dve, v, ("z", 1))
            split_low(dve, v, ("z", 2))
            dve.wait_ge(sem["cmp_done"], 1)
            ends = lambda j: tabN[:, j, CL - 1:CL - 1 + CS * (NCMP - 1) + 1:CS].unsqueeze(1).to_broadcast([P, GN, NCMP])
            kx = bank[4][:, 0:62].rearrange("p (g n) -> p g n", g=GN)
            rope(kcT, kx, ends(2), ends(3), 64, tuple(kct[:, j, :].rearrange("p (g n) -> p g n", g=GN) for j in range(2)), 0.5).then_inc(sem["cmp_rope"], 1)
            split_low(dve, v, ("z", 3))
            split_low(dve, v, ("wout1", 0))
            dve.wait_ge(sem["gate_ready"], 1)
            for b in range(GN):
                pc4 = Pc[b].rearrange("p (r i) n -> p r i n", r=REP)
                ng, sm_, rr = cstat[:, 0, :], cstat[:, 1, :], cstat[:, 2, :]
                dve.wait_ge(sem["cs_done"], b + 1)
                link(v.tensor_tensor(pc4, bank[6 + b][:, 0:496].rearrange("p (r i n) -> p r i n", r=REP, i=NT),
                                     cmpmask[:].unsqueeze(1).to_broadcast([P, REP, NT, NCMP]), ALU.add))
                link(v.reduce_max(ng, Pc[b], AX.X, negate=True))
                v.tensor_tensor(Pc[b], Pc[b], ng.unsqueeze(2).to_broadcast([P, 16, NCMP]), ALU.add).then_inc(sem["cs_sub"], 1)
                dve.wait_ge(sem["cs_exp"], b + 1)
                link(v.reduce_sum(sm_, Pc[b], AX.X))
                link(v.tensor_scalar(sm_, sm_, TINY, None, ALU.max))
                link(v.reciprocal(rr, sm_))
                r4 = rr.rearrange("p (r i) -> p r i", r=REP)
                link(v.tensor_tensor(r4, r4, valid[:].unsqueeze(1).to_broadcast([P, REP, NT]), ALU.mult))
                gt = gates[:, :, 3 * REP * b:3 * REP * (b + 1):3].rearrange("p i r -> p r i")
                link(v.tensor_tensor(r4, r4, gt, ALU.mult))
                v.tensor_tensor(Pc[b], Pc[b], rr.unsqueeze(2).to_broadcast([P, 16, NCMP]), ALU.mult).then_inc(sem["cs_scaled"], 1)
            dve.wait_ge(sem["z_pool"], 16)
            split_low(dve, v, ("wout1", 1))
            attend(1, U1, N0, Pm1, PT1, 3, HN, mix1, zT, True)
            mix_low(1, 7, mix1)
            for j in range(2, 4):
                split_low(dve, v, ("wout1", j))
            output(1, otmp1)

        @block.tensor
        def _(pe):
            m = nc.tensor
            pe.wait_ge(sem["ident_ready"], 2)
            pe.wait_ge(sem["vec_loaded"], 160)
            m.transpose(bank[0][:, 0:V_N], rows[0:V_N, :], ident[0:V_N, 0:V_N]).then_inc(sem["colT_done"], 1)
            m.transpose(bank[0][:, 128:192], perows[:, :], ident[0:64, 0:64]).then_inc(sem["colT_done"], 1)

            def mod_row(d):
                if d >= 2:
                    pe.wait_ge(sem["mrow_act"], d - 1)
                for j in (2 * d, 2 * d + 1):
                    key = ("ada", 0, j)
                    w_ready(pe, key)
                    for k in range(KD):
                        ins = m.matmul(bank[7 * (d % 2)][0:1, 256 * (j % 2):256 * (j % 2) + 256], sc[:, k:k + 1], slot(key)[:, k, :],
                                       start=k == 0, stop=k == KD - 1)
                    ins.then_inc(sem["mod_done"], 1)

            def mod_cols(d):
                pe.wait_ge(sem["mrow_act"], d + 1)
                for f in range(4):
                    ins = m.transpose(bank[1][:, 4 * d + f:4 * d + f + 1], mrow[0:1, d % 2, P * f:P * f + P], ident[0:1, 0:1])
                ins.then_inc(sem["mcol_done"], 1)

            pe.wait_ge(sem["sc_ready"], 2)
            pe.wait_ge(sem["col_ready"], 2)
            mod_row(0)
            mod_row(1)
            mod_cols(0)
            mod_row(2)
            mod_cols(1)
            pe.wait_ge(sem["pw_ready"], 1)
            for j in range(NPW):
                ins = m.transpose(bank[2 + j // 16][0:64, 32 * (j % 16):32 * (j % 16) + 32], small[0:32, j, :], ident[0:32, 0:32])
                if j % 16 == 15 or j == NPW - 1:
                    ins.then_inc(sem["stT_done"], 1)
            pe.wait_ge(sem["s5_loaded"], 64)
            for f in range(4):
                ins = m.transpose(bank[6][:, P * f:P * f + P], CN[:, f, :], ident[:])
            ins.then_inc(sem["CT_done"], 1)
            pe.wait_ge(sem["st_act"], 4)
            m.matmul(bank[2][:, :], swap[:], BA.rearrange("p g h -> p (g h)"), start=True, stop=True).then_inc(sem["BB_done"], 1)
            pe.wait_ge(sem["C_act"], 2)
            m.matmul(bank[3][:, :], swap[:], C1.rearrange("p g h -> p (g h)"), start=True, stop=True).then_inc(sem["CT_done"], 1)
            for d in range(3, 6):
                mod_row(d)
                mod_cols(d - 1)
            mod_cols(5)

            def gate_rows(l):
                pe.wait_ge(sem["mod_ready"], 3 + 2 * l)
                if l == 0:
                    pe.wait_ge(sem["C_act"], 3)
                else:
                    pe.wait_ge(sem["out_gpg"], NT)
                for k in range(KD):
                    ins = m.matmul(bank[6 + k // 4][:, P * (k % 4):P * (k % 4) + P], gcol[:, l, k:k + 1].to_broadcast([P, P]), ident[:], start=True, stop=True)
                    if k % 4 == 3:
                        ins.then_inc(sem["gpg_done"], 1)

            def x_transposes(l, src):
                for k in range(KD):
                    if l == 0 and k == 0:
                        pe.wait_ge(sem["B_ready"], 1)
                        pe.wait_ge(sem["st_act"], 4)
                    if l == 0 and k == 1:
                        pe.wait_ge(sem["mod_ready"], 1)
                    if l == 1 and k == 0:
                        pe.wait_ge(sem["out_gpg"], 2)
                    if k >= 4 and k % 2 == 0:
                        pe.wait_ge(sem["hT_act"], 4 * l + (k - 4) // 2 + 1)
                    if k >= 4 and k % 2 == 1:
                        pe.wait_ge(sem["hT_dve"], 4 * l + (k - 5) // 2 + 1)
                    for i in range(NT):
                        if k == 0:
                            pe.wait_ge(sem["xn_ready"], NT * l + i + 1)
                        ins = m.transpose(bank[k % 4][:, P * i:P * i + P], src[:, i, P * k:P * k + P], ident[:])
                    ins.then_inc(sem["xT_done"], 1)

            def h_ready(l):
                pe.wait_ge(sem["hT_act"], 4 * (l + 1))
                pe.wait_ge(sem["hT_dve"], 4 * (l + 1))

            gate_rows(0)
            x_transposes(0, xr)
            h_ready(0)

            def f_tile(b, w, c0, rhs=hT, nk=KD):
                for k in range(nk):
                    ins = m.matmul(b[:, :], w[:, k, c0:c0 + P], rhs[:, k, :], start=k == 0, stop=k == nk - 1)
                return ins

            def t_tile(b, w, i, n):
                for k in range(KD):
                    ins = m.matmul(b, hT[:, k, P * i:P * i + P], w[:, k, 0:n], start=k == 0, stop=k == KD - 1)
                return ins

            def s5_transposes(b0):
                for b in range(b0, b0 + 4):
                    if b % 2 == 0:
                        pe.wait_ge(sem["G_ready"], b // 2 + 1)
                    if b == 0:
                        pe.wait_ge(sem["st_act"], 8)
                        pe.wait_ge(sem["gpg_ready"], 2)
                    if b >= 4:
                        pe.wait_ge(sem["GT_act"], b - 3)
                    for g in range(4):
                        ins = m.transpose(bank[4 + b % 4][:, P * g:P * g + P], Gc[(b // 2) % 2][:, 4 * (b % 2) + g, :], ident[:])
                    ins.then_inc(sem["GT_done"], 1)

            def s5_kernels(b0):
                for b in range(b0, b0 + 4):
                    pe.wait_ge(sem["W1_ready"], b // 2 + 1)
                    pe.wait_ge(sem["GT_act"], min(8, b + 5))
                    if b >= 4:
                        pe.wait_ge(sem["Kc_act"], b - 3)
                    for g in range(4):
                        ins = m.matmul(bank[4 + b % 4][0:NH, P * g:P * g + P], Bb[:, 4 * b + g, :], W1[:, 4 * b + g, 0:L * NH], start=True, stop=True)
                    ins.then_inc(sem["Kc_done"], 1)

            def s5_states():
                pe.wait_ge(sem["u_back"], 16 * L)
                pe.wait_ge(sem["GT_act"], 8)
                pe.wait_ge(sem["Kc_act"], 8)
                for b in range(4):
                    for g in range(8):
                        ins = m.matmul(bank[4 + b][:, NC * g:NC * g + NC], GT[:, 8 * b + g, :], U[:, 8 * b + g, :], start=True, stop=True)
                    ins.then_inc(sem["V_done"], 1)

            def s5_outputs():
                pe.wait_ge(sem["T_stored"], 32 * L)
                pe.wait_ge(sem["zero_ready"], 1)
                for b in range(4):
                    pe.wait_ge(sem["Xs_ready"], b // 2 + 1)
                    for g in range(8):
                        gg = 8 * b + g
                        dst = bank[4 + b][:, NC * g:NC * g + NC]
                        m.matmul(dst, W1[:, gg, NH:], Xs[:, gg % 16, 0:NC], start=True, stop=False)
                        ins = m.matmul(dst, TP[:, gg, :], U[:, gg, :], start=False, stop=True)
                    ins.then_inc(sem["Y_done"], 1)

            def pj_free(n):
                if n >= 4:
                    kinds = [x[0] for x in PJ0[:n - 3]]
                    nz = sum(x in ("za", "zb") for x in kinds)
                    last = PJ0[n - 4][0]
                    if last in ("za", "zb"):
                        pe.wait_ge(sem["th_act"], nz)
                    else:
                        pe.wait_ge(sem["pj_act"], n - 3 - nz)

            for n, tile in enumerate(PJ0):
                pj_free(n)
                b = bank[n % 4]
                if tile[0] == "u":
                    f = tile[1]
                    w_ready(pe, ("u", f // 2))
                    ins = f_tile(b, slot(("u", f // 2)), P * (f % 2))
                elif tile[0] == "cq":
                    j, i = tile[1:]
                    w_ready(pe, ("cq", j))
                    ins = t_tile(b[:, 0:256], slot(("cq", j)), i, 256)
                elif tile[0] == "kpe":
                    pe.wait_ge(sem["small_w_loaded"], 80)
                    ins = f_tile(b, wkpe, 0)
                else:
                    f = tile[1]
                    w_ready(pe, (tile[0], f // 2))
                    ins = f_tile(b, slot((tile[0], f // 2)), P * (f % 2))
                ins.then_inc(sem["pj_done"], 1)
                if tile[0] == "cq" and tile[2] == NT - 1:
                    (s5_transposes, s5_kernels)[tile[1] // 2](4 * (tile[1] % 2))
                if tile == ("za", 1):
                    s5_states()
                if tile == ("za", 3):
                    s5_outputs()

            pe.wait_ge(sem["cq_scaled"], 2 * NT)
            pe.wait_ge(sem["Y_act"], 4)
            for f in range(8):
                if f >= 4:
                    pe.wait_ge(sem["cqT_act"], f - 3)
                for i in range(NT):
                    ins = m.transpose(bank[4 + f % 4][:, P * i:P * i + P], cqt[:, i, P * f:P * f + P], ident[:])
                ins.then_inc(sem["cqT_done"], 1)
            pe.wait_ge(sem["th_act"], 8)
            pe.wait_ge(sem["cqT_act"], 8)
            for n, key in enumerate(QT):
                if n >= 4:
                    pe.wait_ge(sem["q_act"], n - 3)
                w_ready(pe, key)
                f_tile(bank[n % 4], slot(key), 0, cqT, 6).then_inc(sem["q_done"], 1)
            def mod_sums(d0, banks):
                for d in range(d0, d0 + 3):
                    pe.wait_ge(sem["macc_done"], 2 * d + 2)
                    for f in range(4):
                        ins = m.matmul(bank[banks[d - d0]][:, P * f:P * f + P], macc[2 * d + f // 2][:, P * (f % 2):P * (f % 2) + P], ones[:], start=True, stop=True)
                    ins.then_inc(sem["msum_done"], 1)

            mod_sums(0, MB[0])
            key = ("ukv", 0)
            w_ready(pe, key)
            pe.wait_ge(sem["mod1_ready"], 3)
            for n in range(8):
                if n >= 4:
                    pe.wait_ge(sem["kv_act"], n - 3)
                for k in range(2):
                    if n < 4:
                        ins = m.matmul(bank[4 + n % 4][:, :], slot(key)[:, k, 256 * n:256 * n + P], ckvT[:, k, :], start=k == 0, stop=k == 1)
                    else:
                        wv = slot(key)[:, k, :].rearrange("p (h x) -> p h x", h=MH)[:, :, NOPE:]
                        ins = m.matmul(bank[4 + n % 4][:, :], ckvT[:, k, P * (n - 4):P * (n - 4) + P], wv, start=k == 0, stop=k == 1)
                ins.then_inc(sem["kv_done"], 1)

            pe.wait_ge(sem["q_act"], 4)
            pe.wait_ge(sem["rope_done"], 3)
            pe.wait_ge(sem["y_gelu"], 1)
            for f in range(4):
                w_ready(pe, ("glu", f // 2))
                f_tile(bank[f], slot(("glu", f // 2)), P * (f % 2), yT, 4).then_inc(sem["glu_done"], 1)
            def attend(units, n0, scores, Pb, PTb, heads, h0, values, extra):
                N, per = len(units), len(units) // heads

                def evacuated(m_):
                    pe.wait_ge(sem[("pt_act", "pt_dve")[m_ % 2]], n0 // 2 + m_ // 2 + 1)

                for n in range(N + 3):
                    if n < N:
                        h, i, b = units[n]
                        if n >= 3:
                            pe.wait_ge(sem["s_exp"], n0 + n - 2)
                        w = P * (i + 1)
                        sb_ = bank[SB[n % 3]]
                        scores(sb_, h, i, b, w)
                        m.matmul(sb_[:, P * i:w], identb[:], cmaskb[:], start=False, stop=True).then_inc(sem["s_done"], 1)
                    u = n - 2
                    if 0 <= u < N:
                        pe.wait_ge(sem["s_scaled"], n0 + u + 1)
                        if u >= 2:
                            evacuated(u - 2)
                        for j in range(units[u][1] + 1):
                            ins = m.transpose(bank[TB[u % 2]][:, P * j:P * j + P], Pb[:, u % 3, P * j:P * j + P], ident[:])
                        ins.then_inc(sem["pt_done"], 1)
                    u = n - 3
                    if u >= 0:
                        h, i, b = units[u]
                        evacuated(u)
                        if u % per == 0 and h >= 2:
                            pe.wait_ge(sem["o_dve"], h0 + h - 1)
                        dst = bank[OB[h % 2]][:, P * i:P * i + P]
                        first = b == 0
                        if extra is not None and b == 0:
                            extra(dst, h, i)
                            first = False
                        last_b = extra is None or b == 1
                        for j in range(i + 1):
                            ins = m.matmul(dst, values(h, b, j), PTb[:, u % 2, P * j:P * j + P], start=first and j == 0, stop=last_b and j == i)
                        ins.then_inc(sem["pv_done"], 1)

            def scores0(dst, h, i, b, w):
                m.matmul(dst[:, 0:w], qnT[:, h, P * i:P * i + P], knT[:, h, 0:w], start=True, stop=False)
                m.matmul(dst[:, 0:w], qpT[:, h // 2, P * i:P * i + P], (kpT, kz)[h % 2][:, 0:w], start=False, stop=False)

            pe.wait_ge(sem["masks_ready"], 7)
            pe.wait_ge(sem["q_act"], 4)
            pe.wait_ge(sem["kv_act"], 8)
            pe.wait_ge(sem["rope_done"], 3)
            pe.wait_ge(sem["kz_ready"], 3)
            pe.wait_ge(sem["glu_act"], 4)
            mod_sums(3, MB[1])
            pe.wait_ge(sem["mod1_ready"], 6)
            attend(U0, 0, scores0, Pm, PT, MH, 0, lambda h, b, j: vM[:, j, P * h:P * h + P], None)

            def three(dst, ah, al, bh, bl, start, stop):
                m.matmul(dst, ah, bh, start=start, stop=False)
                m.matmul(dst, ah, bl, start=False, stop=False)
                return m.matmul(dst, al, bh, start=False, stop=stop)

            def output(l):
                for j in range(4):
                    key = (f"wout{l}", j)
                    pe.wait_ge(sem["w_lo"], sorder[key] + 1)
                    for ks in ([range(KD - 1), range(KD - 1, KD)] if j == 0 else [range(KD)]):
                        if j == 0:
                            pe.wait_ge(sem["mix_lo"], 8 * l + ks[-1] + 1)
                        if j == 0 and ks[0] == 0:
                            pe.wait_ge(sem["o_dve"], (MH, MH + HN)[l])
                        for i in range(NT):
                            for k in ks:
                                ts = slice(P * i, P * i + P)
                                ins = three(bank[2 * i + j // 2][:, 256 * (j % 2):256 * (j % 2) + 256], hTr[:, k, ts], mixr[l][:, k, ts],
                                            hi(key)[:, k, :], lo(key)[:, k, :], k == 0, k == KD - 1)
                            if j == 3:
                                ins.then_inc(sem["out_done"], 1)
                    if j < 3:
                        ins.then_inc(sem["wo_used"], 1)

            output(0)

            gate_rows(1)
            x_transposes(1, xn1)

            def pj1_free(n):
                if n < 4:
                    pe.wait_ge(sem[("hT_act", "hT_dve")[n % 2]], 4 + n // 2 + 3)
                    return
                done = PJ1[:n - 3]
                kind = PJ1[n - 4][0]
                count = sum(x[0] == kind for x in done)
                if kind == "cmp":
                    pe.wait_ge(sem["kc_ready"], 2 * count)
                elif kind in ("k", "q"):
                    pe.wait_ge(sem["rope1"], sum(x[0] in ("k", "q") for x in done))
                elif kind == "v":
                    pe.wait_ge(sem["v_act"], count)
                elif kind == "gate":
                    pe.wait_ge(sem["gate_act"], 1)
                else:
                    pe.wait_ge(sem["th_act"], 8 + count)

            def hidden():
                pe.wait_ge(sem["kc_ready"], 8)
                for b in range(2):
                    for j in range(4):
                        key = ("w1", b, j)
                        w_ready(pe, key)
                        for l in range(8):
                            ins = m.matmul(bank[4 + b][0:NB, 0:CH], R[b][:, 8 * j + l, :, :].rearrange("p g n -> p (g n)"),
                                           slot(key)[:, l, :], start=j + l == 0, stop=j == 3 and l == 7)
                        if j < 3:
                            ins.then_inc(sem["w1_used"], 1)
                    ins.then_inc(sem["hid_done"], 1)

            def compressed():
                pe.wait_ge(sem["small_w_loaded"], 80)
                for b in range(2):
                    pe.wait_ge(sem["hid_ready"], b + 1)
                    for e in range(2):
                        ins = m.transpose(bank[6 + b][:, 64 * e:64 * e + NB], hid[b][0:NB, e, :], ident[0:NB, 0:NB])
                    ins.then_inc(sem["hidT_done"], 1)
                pe.wait_ge(sem["hidT_act"], 2)
                for e in range(2):
                    ins = m.matmul(bank[4][:, 0:NB], w2[:, 0, e, :], hidT[0][:, e, :], start=e == 0, stop=e == 1)
                ins.then_inc(sem["cmp_done"], 1)
                for g in range(GN):
                    for e in range(2):
                        ins = m.matmul(bank[5][0:NCMP, DN * g:DN * g + DN], hidT[1][:, e, NCMP * g:NCMP * g + NCMP], w2[:, 1, e, :],
                                       start=e == 0, stop=e == 1)
                ins.then_inc(sem["cmp_done"], 1)

            def compressed_scores():
                pe.wait_ge(sem["cmp_rope"], 1)
                pe.wait_ge(sem["rope1"], 12)
                for g in range(GN):
                    for r in range(REP):
                        for i in range(NT):
                            c0 = NCMP * (NT * r + i)
                            ins = m.matmul(bank[6 + g][:, c0:c0 + NCMP], qT[:, REP * g + r, P * i:P * i + P], kcT[:, g, :], start=True, stop=True)
                    ins.then_inc(sem["cs_done"], 1)

            for n, tile in enumerate(PJ1):
                if tile == ("z", 0):
                    hidden()
                    pe.wait_ge(sem["gate_act"], 1)
                    for i in range(NT):
                        ins = m.transpose(bank[6][:, 24 * i:24 * i + 24], gT[0:24, P * i:P * i + P], ident[0:24, 0:24])
                    ins.then_inc(sem["gT_done"], 1)
                if tile == ("z", 4):
                    pe.wait_ge(sem["gate_ready"], 1)
                    compressed()
                if tile == ("z", 6):
                    compressed_scores()
                pj1_free(n)
                kind, b = tile[0], bank[n % 4]
                if kind == "gate":
                    pe.wait_ge(sem["gate_w"], 2)
                else:
                    key = weights1(tile)
                    pe.wait_ge(sem["w_lo"], sorder[key] + 1)
                for k in range(KD):
                    if n == 0:
                        pe.wait_ge(sem["h_lo"], k + 1)
                    first, last = k == 0, k == KD - 1
                    if kind == "gate":
                        ins = three(b[0:3 * HN, :], wgate_hi[:, k, :], wgater[:, k, :], hTr[:, k, :], hlo1r[:, k, :], first, last)
                    elif kind == "v":
                        ts = slice(P * tile[2], P * tile[2] + P)
                        ins = three(b[:, 0:256], hTr[:, k, ts], hlo1r[:, k, ts], hi(key)[:, k, :], lo(key)[:, k, :], first, last)
                    else:
                        fs = slice(P * (tile[-1] % 2), P * (tile[-1] % 2) + P)
                        ins = three(b[:, :], hi(key)[:, k, fs], lo(key)[:, k, fs], hTr[:, k, :], hlo1r[:, k, :], first, last)
                ins.then_inc(sem["pj_done"], 1)
            pe.wait_ge(sem["th_act"], 16)
            for h in range(HN):
                if h % REP == 0:
                    pe.wait_ge(sem["cs_scaled"], h // REP + 1)
                if h >= 2:
                    pe.wait_ge(sem["cpt_act"], h - 1)
                for i in range(NT):
                    ins = m.transpose(bank[h % 2][0:NCMP, P * i:P * i + P], Pc[h // REP][:, NT * (h % REP) + i, :], ident[:])
                ins.then_inc(sem["cpt_done"], 1)

            def scores1(dst, h, i, b, w):
                m.matmul(dst[:, 0:w], qT[:, h, P * i:P * i + P], (ksT, kwT)[b][:, h // REP, 0:w], start=True, stop=False)

            def extra(dst, h, i):
                m.matmul(dst, vc[:, h // REP, :], PcT[:, h, P * i:P * i + P], start=True, stop=False)

            pe.wait_ge(sem["v_act"], 8)
            pe.wait_ge(sem["cmp_act"], 1)
            pe.wait_ge(sem["cpt_act"], HN)
            attend(U1, N0, scores1, Pm1, PT1, HN, MH, lambda h, b, j: (vs, vw)[b][:, j, DN * (h // REP):DN * (h // REP) + DN], extra)
            output(1)


_INS = ['x', 'c', 'positions', 'pre_norm_g', 'post_norm_g', 'w_ada', 'b_ada', 'ev_w_in', 'ev_lam_re', 'ev_lam_im', 'ev_log_dt',
        'ev_b_re', 'ev_b_im', 'ev_c_re', 'ev_c_im', 'ev_d_skip', 'ev_w_glu', 'ev_b_glu', 'ev_q_norm_g', 'ev_kv_norm_g', 'ev_w_uq',
        'ev_w_ukv', 'ev_w_out', 'od_w_in', 'od_cmp_k_pe', 'od_cmp_k_w1', 'od_cmp_k_w2', 'od_cmp_v_pe', 'od_cmp_v_w1', 'od_cmp_v_w2',
        'od_w_out']


def _constants():
    f = np.float32
    half_n, half_m = DN // 2, RO // 2
    inv = lambda half: (f(10000.0) ** (-np.arange(half, dtype=f) / f(half))).astype(f)
    p = np.arange(P)
    return np.stack([inv(half_n)[p % half_n], inv(half_m)[p % half_m], np.where(p < half_n, f(1), f(-1)),
                     np.where(p % RO < half_m, f(1), f(-1))], axis=1).astype(f)


def kernel(**inputs):
    import numpy as _np
    import concourse.bacc as _bacc
    from concourse import mybir as _mybir
    from concourse.bass_utils import run_bass_kernel_spmd as _run

    nc = _bacc.Bacc("TRN2", target_bir_lowering=False, num_devices=1)
    arrays, t = {}, {}
    for name in _INS:
        a = _np.ascontiguousarray(inputs[name])
        arrays[f"in_{name}"] = a
        t[name] = nc.dram_tensor(f"in_{name}", a.shape, _mybir.dt.from_np(a.dtype), kind="ExternalInput").ap()
    arrays["in_cst"] = _constants()
    t["cst"] = nc.dram_tensor("in_cst", (P, 4), F32, kind="ExternalInput").ap()
    t["out"] = nc.dram_tensor("out_0", (1, S, D), F32, kind="ExternalOutput").ap()
    build_trunk(nc, t)
    r = _run(nc, [arrays], core_ids=[0])
    return r.results[0]["out_0"]
```

```python
import concourse.bass as bass
from concourse import mybir
from contextlib import ExitStack
import math
import numpy as np

F32 = mybir.dt.float32
F32R = mybir.dt.float32r
I32 = mybir.dt.int32
ALU = mybir.AluOpType
ACT = mybir.ActivationFunctionType
AX = mybir.AxisListType

P = 128
S = 512
NT = S // P
D = 1024
KD = D // P
EPS = 1e-6
TINY = 1e-30
NEG = -1e30
W5 = 512
NG, NH, NP_ = 32, 16, 64
L = 8
NC = S // L
TAPS = L + 1
MH, NOPE, RO, MV = 4, 128, 64, 128
QR, KVR = 768, 256
EV_CQ, EV_KPE, EV_ZB = 2 * W5, 2 * W5 + QR + KVR, 2 * W5 + QR + KVR + RO
MSCALE = (NOPE + RO) ** -0.5
HN, GN, REP, DN = 8, 2, 4, 128
NW = HN * DN
OD_KC, OD_VC, OD_KS, OD_VS, OD_KW, OD_VW = (NW + i * GN * DN for i in range(6))
OD_GATE = NW + 6 * GN * DN
OD_Z = OD_GATE + 3 * HN
NSCALE = DN ** -0.5
CL, CS, CH = 32, 16, 256
NCMP = (S - CL) // CS + 1
SLOT = 2048
RING = 4
R0 = 4
C_GELU = math.sqrt(2.0 / math.pi)
PI_SAFE = 3.1415925
MAGIC = 12582912.0
TWO_PI = 2 * math.pi
PI_A = 6.28125
PI_B = float(np.float32(TWO_PI - 6.28125))
PI_C = TWO_PI - PI_A - PI_B

V_C, V_PRE, V_BADA, V_POST, V_QN, V_KVN, V_BGLU, V_DSK, V_N = 0, 8, 24, 72, 88, 94, 96, 100, 104

SEMS = """c_loaded half_ready out_half w_loaded0 w_loaded1 w_loaded2 w_loaded3 vec_loaded const_loaded pos_loaded
x_loaded lam_loaded s5_loaded small_w_loaded ident_ready masks_ready pool_chain dve_chain act_chain colT_done
col_ready sc_ready mod_done mod_ready ssq_done msq_done rstd_ready xn_ready xT_done hT_act tab_abs tab_sin
tab_cos lam_exp lam_red lam_sin pw_ready stT_done st_act CT_done C_act BB_done B_ready GT_done GT_act Kc_done
Kc_act T_zero T_stored W1_ready G_ready pj_done pj_act th_act z_pool u_stored u_back V_done z_dve zero_ready
Xs_ready Y_done Y_act YT_done y_skip y_sq y_arg y_tanh y_gelu glu_done glu_act ya_ready cq_msq cq_rstd
cq_scaled cqT_done cqT_act q_done q_act kv_done kv_act rope_done s_done s_max s_exp s_scaled pt_done pt_act
pt_dve o_dve out_done out_sq out_msq out_rstd out_gpg gpg_done gpg_ready out_res kc_ready hid_done hid_tanh
hid_sq hid_arg hid_ready cmp_done cmp_act cmp_rope cs_done cs_sub cs_exp cs_scaled cpt_done cpt_act gate_act
gate_ready stored v_act rope1 hT_dve pv_done mrow_act mcol_done macc_done kz_ready hidT_done hidT_act gT_done
pad_ready rot_ready r8_ready wo_used w1_used w_hi w_lo R_hi R_lo mw_hi mw_lo cq_lo y_hi y_lo mix_hi mix_lo h_hi h_lo
gate_w""".split()


def build_trunk(nc, t):
    with ExitStack() as ctx:
        def sb(name, shape, dt=F32):
            return ctx.enter_context(nc.sbuf_tensor(name, shape, dt))

        sem = {n: ctx.enter_context(nc.semaphore(n)) for n in SEMS}
        bank = [ctx.enter_context(nc.psum_tensor(f"bank{i}", [P, 512], F32)) for i in range(8)]

        ident = sb("ident", [P, P])
        swap = sb("swap", [P, P])
        identb = sb("identb", [P, P], mybir.dt.bfloat16)
        cmaskb = sb("cmaskb", [P, P], mybir.dt.bfloat16)
        cmpmask = sb("cmpmask", [P, NT, NCMP])
        valid = sb("valid", [P, NT])
        rows = sb("rows", [P, P])
        perows = sb("perows", [2 * CL, DN])
        peT = sb("peT", [P, 2 * CL])
        col = sb("col", [P, V_N])
        cst = sb("cst", [P, 4])
        mod = sb("mod", [P, 2, 24])
        pre = sb("pre", [P, 2, KD])
        gcol = sb("gcol", [P, 2, KD])
        sc = sb("sc", [P, KD])
        sct = sb("sct", [P, KD])
        hbg = sb("hbg", [P, 4])
        st1 = sb("st1", [P, 64])
        smax, ssum, srec = sb("smax", [P, 4]), sb("ssum", [P, 4]), sb("srec", [P, 4])
        halfpi = sb("halfpi", [P, 1])
        ones = sb("ones", [P, P])
        neghalf = sb("neghalf", [P, 8])
        gpg = sb("gpg", [P, D])
        xr = sb("xr", [P, NT, D])
        def sb_split(name, shape):
            full = sb(name, shape)
            return full, nc.alloc_sbuf_tensor_at(name + "_r", shape, F32R, offset=nc.sbuf_base - 4 * int(np.prod(shape[1:])))

        hT, hTr = sb_split("hT", [P, KD, S])
        ring, ringr = sb_split("ring", [P, RING, SLOT])
        wgate, wgater = sb_split("wgate", [P, KD, 3 * HN])
        m1raw = sb("m1raw", [P, 24])
        wgate_hi = sb("wgate_hi", [P, KD, 3 * HN], F32R)
        l0s, l0sr = sb_split("l0s", [P, SLOT])
        wkpe = l0s[:, 0:KD * P].rearrange("p (k n) -> p k n", k=KD)
        tabM = l0s[:, KD * P:].rearrange("p (a n) -> p a n", a=2)
        w2 = sb("w2", [P, 2, 2, DN])
        oW1, oGT = 0, 4608
        oROT = oGT + 4096
        oD = oROT + 4096
        oT = oD + 3200
        oH = oT + 4608
        oU = oH + 4768
        oMA = oU + 5632
        ARENA = oMA + 512
        arena = sb("arena", [P, ARENA])
        arena0 = nc.sbuf_base - 4 * ARENA

        def at_r(name, off, *shape):
            return nc.alloc_sbuf_tensor_at(name, [P, *shape], F32R, offset=arena0 + 4 * off)

        def at(off, *shape):
            n = int(np.prod(shape))
            assert off + n <= ARENA, (off + n, ARENA)
            v = arena[:, off:off + n]
            if len(shape) == 2:
                v = v.rearrange("p (a b) -> p a b", a=shape[0])
            if len(shape) == 3:
                v = v.rearrange("p (a b c) -> p a b c", a=shape[0], b=shape[1])
            return v

        W1 = at(oW1, NG, TAPS * NH)
        GT = at(oGT, NG, P)
        rotc, rots = at(oROT, NG, NC), at(oROT + 2048, NG, NC)
        Gc = [at(oD, 8, P), at(oD + 1024, 8, P)]
        tmpG = at(oD + 2048, 8, TAPS * NH)
        TP = at(oT, NG, P)
        NPW = 2 * TAPS + 2 * L + 2 * L + 3
        small = at(oT, NPW + 18, NP_)
        iP, iF, iC, iX = 0, 2 * TAPS, 2 * TAPS + 2 * L, 2 * TAPS + 4 * L
        st = at(oH, NPW, NG)
        BA, BB = at(oH + 1696, NG, NH), at(oH + 2208, NG, NH)
        Bb, iBb = at(oH + 2720, NG, NH), at(oH + 3232, NG, NH)
        C1, C2 = at(oH + 3744, NG, NH), at(oH + 4256, NG, NH)
        CN = Gc[0].rearrange("p a b -> p (a b)")[:, 0:512].rearrange("p (a b) -> p a b", a=4)
        U = at(oH, NG, NC)
        zb5, tb5 = at(oH + 2048, 16, NC), at(oH + 3072, 16, NC)
        Xs = at(oD, 16, NC + 1)
        r8b = at(oD + 1040, NG, NC)
        Kh = at(oU + 2048, 16, P)
        uTp = at(oU, 4, S)
        zaT = at(oU + 2048, 4, S)
        th = at(oU + 4096, 2, S)
        mrow = th
        macc = [at(o, 2, 256) for o in (oU + 3584, oU + 4608, oMA, oMA, oMA, oT)]
        kz = at(oD + 1024 + 1536, S)
        kpT = at(oU + 5120, S)
        Yc = at(oGT, L, NG * NH)[0:NC]
        yT, y2 = at(oROT, 4, S), at(oGT + 2048, 4, S)
        cqt = xr
        cqr = at_r("cq_r", 0, KD, S)
        qnT = at(oROT + 2048, 4, S)
        qpT = at(oD, 2, S)
        knT, vM = at(oT, 4, S), at(oT + 2048, NT, 4 * MV)
        zbT = at(oH, 4, S)
        mixT = at(oGT, KD, S)
        Pm, PT = at(oD + 1024, 3, S), at(oH + 2048, 2, S)
        rtmp = at(oH + 3072, 2, S)
        ra, rk = at(oU + 2048, S), at(oU + 2560, S)
        posb = at(oU + 3072, S)
        posi = posb.bitcast(I32)
        otmp = at(0, 2, D)
        tabN = at(0, 4, S)
        qT, ksT, kwT = at(2048, HN, S), at(6144, GN, S), at(7168, GN, S)
        vs, vw = at(8192, NT, GN * DN), at(9216, NT, GN * DN)
        R = [at(10240, CL, GN, NCMP), at(10240 + 1984, CL, GN, NCMP)]
        PcT = at(10240, HN, S)
        zT = at(14336, HN, S)
        Pc = [at(18432, 16, NCMP), at(18928, 16, NCMP)]
        NB = GN * NCMP
        hidT = [at(19424, 2, NB), at(19548, 2, NB)]
        kcT, kct = at(19920, GN, NCMP), at(19982, 2, NB)
        hid, hsq = [at(20592 + 256 * b, 2, P) for b in range(2)], [at(21104 + 256 * b, 2, P) for b in range(2)]
        vc = at(20106, GN, DN)
        gates = at(20362, NT, 3 * HN)
        cstat = at(20458, 4, 16)
        gT = at(21616, S)
        Pm1, PT1 = at(20592, 3, S), at(22128, 2, S)
        rt1, th1 = at(23152, 2, S), at(24176, 2, S)
        mix1 = at(25200, KD, S)
        xn1 = at(14336, NT, D)
        hlo1, hlo1r = mix1, at_r("hlo1_r", 25200, KD, S)
        mixr = [at_r("mix0_r", oGT, KD, S), hlo1r]
        w_high = [l0sr, at_r("w_high_r", 29296, SLOT)]
        Rr = at_r("R_r", 10240, 2, CL * NB)
        R_high = at_r("R_high", 14336, 2, CL * NB)
        mla_high = [l0sr[:, 0:KD * P], at_r("mla_high1_r", oD + 1024, KD * P)[:, :],
                    at_r("mla_high2_r", oH + 2048, KD * P)[:, :]]
        sqj, ysj = at(oROT, 2, S), at(oROT + 1024, S)
        otmp1 = at(2048, 2, D)

        def cols(w, r0, nk, c0, c1):
            return w[r0:r0 + nk * P, c0:c1].rearrange("(k p) n -> p k n", p=P)

        ev_in, od_in = t["ev_w_in"][0], t["od_w_in"][0]
        loads = []

        def use(key, pieces, shape):
            loads.append((key, pieces, shape))

        def ada(l, j0, j1):
            for j in range(j0, j1):
                use(("ada", l, j), [(slice(0, 256), cols(t["w_ada"][l], 0, KD, 256 * j, 256 * j + 256))], (KD, 256))

        def colchunks(key, w, c0, n, r0=0, nk=KD, j0=0):
            for j in range(n // 256):
                use((key, j0 + j), [(slice(0, 256), cols(w, r0, nk, c0 + 256 * j, c0 + 256 * j + 256))], (nk, 256))

        ada(0, 0, 12)
        colchunks("u", ev_in, 0, 512)
        for j in range(4):
            if j < 3:
                ada(1, 2 * j, 2 * j + 2)
            colchunks("cq", ev_in, EV_CQ + 256 * j, 256, j0=j)
        for j in range(2):
            colchunks("za", ev_in, W5 + 256 * j, 256, j0=j)
            ada(1, 6 + 2 * j, 8 + 2 * j)
        colchunks("zb", ev_in, EV_ZB, 256)
        ada(1, 10, 12)
        colchunks("zb", ev_in, EV_ZB + 256, 256, j0=1)
        uq = t["ev_w_uq"][0]
        for h in range(0, MH, 2):
            for e in range(2):
                use(("uqn", h + e), [(slice(0, P), cols(uq, 0, 6, (h + e) * 192, (h + e) * 192 + P))], (6, P))
            use(("uqp", h // 2), [(slice(64 * e, 64 * e + 64), cols(uq, 0, 6, (h + e) * 192 + P, (h + e) * 192 + 192)) for e in range(2)], (6, P))
        use(("ukv", 0), [(slice(0, 1024), cols(t["ev_w_ukv"][0], 0, 2, 0, 1024))], (2, 1024))
        colchunks("glu", t["ev_w_glu"][0], 0, 512, nk=4)
        colchunks("wout0", t["ev_w_out"][0], 0, 1024)
        colchunks("kc", od_in, OD_KC, 256)
        colchunks("vc", od_in, OD_VC, 256)
        colchunks("ks", od_in, OD_KS, 256)
        colchunks("vs", od_in, OD_VS, 256)
        colchunks("kw", od_in, OD_KW, 256)
        colchunks("vw", od_in, OD_VW, 256)
        colchunks("q", od_in, 0, 1024)
        for b in range(2):
            w1 = t[("od_cmp_k_w1", "od_cmp_v_w1")[b]][0]
            for j in range(4):
                use(("w1", b, j), [(slice(0, CH), cols(w1, 1024 * j, 8, 0, CH))], (8, CH))
        colchunks("z", od_in, OD_Z, 1024)
        colchunks("wout1", t["od_w_out"][0], 0, 1024)
        order = {key: n for n, (key, _, _) in enumerate(loads)}
        npieces = [len(p) for _, p, _ in loads]

        def loaded_count(n):
            return 16 * sum(npieces[m] for m in range(n % RING, n + 1, RING))

        def slot(key):
            n = order[key]
            nk, w = loads[n][2]
            return ring[:, n % RING, 0:nk * w].rearrange("p (k n) -> p k n", k=nk)

        SPLIT = [key for key, _, _ in loads if key[0] in ("wout0", "kc", "vc", "ks", "vs", "kw", "vw", "q", "w1", "z", "wout1")]
        sorder = {key: n for n, key in enumerate(SPLIT)}

        def hi(key):
            nk, w = loads[order[key]][2]
            return w_high[sorder[key] % 2][:, 0:nk * w].rearrange("p (k n) -> p k n", k=nk)

        def lo(key):
            nk, w = loads[order[key]][2]
            return ringr[:, order[key] % RING, 0:nk * w].rearrange("p (k n) -> p k n", k=nk)

        def split_high(act, a, key):
            n = sorder[key]
            w_ready(act, key)
            if n >= 2:
                name, count = last_use(SPLIT[n - 2])
                act.wait_ge(sem[name], count)
            for ks in (slice(0, KD // 2), slice(KD // 2, KD)):
                a.copy(hi(key)[:, ks, :], slot(key)[:, ks, :]).then_inc(sem["w_hi"], 1)

        def split_low(dve, v, key):
            for e, ks in enumerate((slice(0, KD // 2), slice(KD // 2, KD))):
                dve.wait_ge(sem["w_hi"], 2 * sorder[key] + e + 1)
                v.tensor_tensor(lo(key)[:, ks, :], slot(key)[:, ks, :], hi(key)[:, ks, :].bitcast(F32), ALU.subtract).then_inc(sem["w_lo"], 1)

        QT = [("uqn", 0), ("uqn", 1), ("uqp", 0), ("uqn", 2), ("uqn", 3), ("uqp", 1)]
        MSPLIT = [(key, slice(0, 6)) for key in QT] + [(("ukv", 0), slice(k, k + 1)) for k in range(2)] + [(("glu", j), slice(0, 4)) for j in range(2)]

        def mhi(n):
            key, ks = MSPLIT[n]
            nk, w = ks.stop - ks.start, loads[order[key]][2][1]
            return mla_high[n % 3][:, 0:nk * w].rearrange("p (k n) -> p k n", k=nk)

        def mla_split_high(act, a, n):
            key, ks = MSPLIT[n]
            w_ready(act, key)
            if n == 9:
                act.wait_ge(sem["kv_done"], 8)
            elif n >= 3:
                act.wait_ge(sem["q_done"], n - 2)
            a.copy(mhi(n), slot(key)[:, ks, :]).then_inc(sem["mw_hi"], 1)

        def mla_split_low(dve, v, n):
            key, ks = MSPLIT[n]
            dve.wait_ge(sem["mw_hi"], n + 1)
            v.tensor_tensor(lo(key)[:, ks, :], slot(key)[:, ks, :], mhi(n).bitcast(F32), ALU.subtract).then_inc(sem["mw_lo"], 1)

        def next_split(n):
            if n == 0 or PJ1[n] == ("gate",) or PJ1[n][-1] % 2:
                return None
            key = weights1(PJ1[n])
            if PJ1[n - 1] != ("gate",) and weights1(PJ1[n - 1]) == key:
                return None
            return SPLIT[sorder[key] + 1]

        def w_ready(eng, key):
            eng.wait_ge(sem[f"w_loaded{order[key] % RING}"], loaded_count(order[key]))

        scr_u = nc.dram_tensor("scr_u", (NG, NH, L, NC), F32, kind="Internal").ap()
        SB, TB, OB = [3, 4, 5], [6, 7], [1, 2]
        ssx, msx, rsx = st1[:, 0:4], st1[:, 4:8], st1[:, 8:12]
        ssq_c, msq_c, rst_c = st1[:, 12:28], st1[:, 28:36], st1[:, 36:44]
        sso, mso, rso = st1[:, 44:52], st1[:, 52:56], st1[:, 56:60]
        dtc = st1[0:32, 60:61]
        xin = t["x"][0].rearrange("(i p) d -> p i d", p=P)
        out = t["out"][0].rearrange("(i p) d -> i p d", p=P)
        U0 = [(h, i, 0) for h in range(MH) for i in range(NT)]
        U1 = [(h, i, b) for h in range(HN) for i in range(NT) for b in range(2)]
        N0, N1 = len(U0), len(U1)

        PJ0 = ([("u", f) for f in range(4)]
               + [x for j in range(4) for x in [("cq", j, i) for i in range(NT)] + [("ms", j)] * (j < 2)]
               + [("ms", 2), ("kpe",)] + [("za", f) for f in range(4)] + [("ms", 3)] + [("zb", 0), ("zb", 1), ("ms", 4), ("zb", 2), ("zb", 3), ("ms", 5)])
        evac0 = [sum(x[0] not in ("za", "zb") for x in PJ0[:n + 1]) for n in range(len(PJ0))]

        PJ1 = ([("cmp", kv, g) for kv in range(2) for g in range(GN)]
               + [x for br in range(2) for x in [("k", br, g) for g in range(GN)] + [("v", br, i) for i in range(NT)]]
               + [("q", f) for f in range(HN)] + [("gate",)] + [("z", f) for f in range(HN)])
        NJ0 = len(PJ0)

        def weights1(tile):
            kind = tile[0]
            if kind == "cmp":
                return (("kc", "vc")[tile[1]], 0)
            if kind == "k":
                return (("ks", "kw")[tile[1]], 0)
            if kind == "v":
                return (("vs", "vw")[tile[1]], 0)
            return (kind, tile[1] // 2)

        def last_use(key):
            kind = key[0]
            if kind == "ada":
                return ("mod_done", "macc_done")[key[1]], key[2] + 1
            if kind == "cq":
                return "pj_done", PJ0.index(("cq", key[1], NT - 1)) + 1
            if kind in ("u", "za", "zb"):
                return "pj_done", PJ0.index((kind, 2 * key[1] + 1)) + 1
            if kind == "glu":
                return "glu_done", 2 * key[1] + 2
            if kind in ("uqn", "uqp"):
                return "q_done", QT.index(key) + 1
            if kind == "ukv":
                return "kv_done", 8
            if kind in ("wout0", "wout1"):
                l = int(kind[-1])
                return [("wo_used", 2 * l + 1), ("out_half", l + 1), ("wo_used", 2 * l + 2), ("out_done", NT * (l + 1))][key[1]]
            if kind == "w1":
                return ("w1_used", 3 * key[1] + key[2] + 1) if key[2] < 3 else ("hid_done", key[1] + 1)
            return "pj_done", NJ0 + max(n for n, x in enumerate(PJ1) if x != ("gate",) and weights1(x) == key) + 1

        block = ctx.enter_context(nc.Block())

        @block.sync
        def _(sp):
            sp.dma_start(rows[V_C:V_C + KD, :], t["c"].rearrange("o (k p) -> (o k) p", p=P)).then_inc(sem["c_loaded"], 16)
            sp.dma_start(small[0:32, NPW, :], t["ev_lam_re"][0]).then_inc(sem["lam_loaded"], 16)
            sp.dma_start(small[0:32, NPW + 1, :], t["ev_lam_im"][0]).then_inc(sem["lam_loaded"], 16)
            sp.dma_start(dtc, t["ev_log_dt"].rearrange("o g -> g o")).then_inc(sem["lam_loaded"], 16)
            for n, (key, pieces, (nk, w)) in enumerate(loads):
                if n >= RING:
                    name, count = last_use(loads[n - RING][0])
                    sp.wait_ge(sem[name], count)
                for where, src in pieces:
                    sp.dma_start(slot(key)[:, :, where], src).then_inc(sem[f"w_loaded{n % RING}"], 16)
                if n == RING - 1:
                    sp.dma_start(xr[:], xin).then_inc(sem["x_loaded"], 16)
                if key == ("wout0", 3):
                    sp.wait_ge(sem["cqT_done"], 8)
                    sp.dma_start(xr[:], xin).then_inc(sem["x_loaded"], 16)
            for i in range(NT):
                sp.wait_ge(sem["out_res"], 2 * (NT + i + 1))
                sp.dma_start(out[i], xr[:, i, :]).then_inc(sem["stored"], 16)
            sp.wait_ge(sem["stored"], 16 * NT)

        @block.gpsimd
        def _(pool):
            g = nc.gpsimd
            chain = [0]

            def link(ins):
                chain[0] += 1
                ins.then_inc(sem["pool_chain"], 1)
                pool.wait_ge(sem["pool_chain"], chain[0])

            link(g.memset(ident[:], 0.0))
            g.affine_select(out=ident[:], in_=ident[:], compare_op=ALU.not_equal, fill=1.0, base=0,
                            pattern=[[-1, P]], channel_multiplier=1).then_inc(sem["ident_ready"], 1)
            link(g.memset(swap[:], 0.0))
            link(g.affine_select(out=swap[:], in_=swap[:], compare_op=ALU.not_equal, fill=-1.0, base=-64,
                                 pattern=[[-1, P]], channel_multiplier=1))
            g.affine_select(out=swap[:], in_=swap[:], compare_op=ALU.not_equal, fill=1.0, base=64,
                            pattern=[[-1, P]], channel_multiplier=1).then_inc(sem["ident_ready"], 1)
            g.memset(ones[:], 1.0).then_inc(sem["masks_ready"], 1)
            g.memset(neghalf[:], -0.5).then_inc(sem["masks_ready"], 1)
            link(g.memset(cmaskb[:], 0.0))
            g.affine_select(out=cmaskb[:], in_=cmaskb[:], compare_op=ALU.is_ge, fill=NEG, base=0,
                            pattern=[[-1, P]], channel_multiplier=1).then_inc(sem["masks_ready"], 1)
            link(g.memset(cmpmask[:], 0.0))
            g.affine_select(out=cmpmask[:], in_=cmpmask[:], compare_op=ALU.is_ge, fill=NEG, base=-(CL - 1),
                            pattern=[[P, NT], [-CS, NCMP]], channel_multiplier=1).then_inc(sem["masks_ready"], 1)
            link(g.memset(valid[:], 1.0))
            g.affine_select(out=valid[:], in_=valid[:], compare_op=ALU.is_ge, fill=0.0, base=-(CL - 1),
                            pattern=[[P, NT]], channel_multiplier=1).then_inc(sem["masks_ready"], 1)
            pool.wait_ge(sem["ident_ready"], 2)
            g.tensor_copy(identb[:], ident[:]).then_inc(sem["masks_ready"], 1)
            pool.wait_ge(sem["masks_ready"], 2)

            def rstd(l, i):
                pool.wait_ge(sem["msq_done"], NT * l + i + 1)
                g.tensor_tensor(rsx[:, i:i + 1], msx[:, i:i + 1], neghalf[:, 0:1], ALU.pow).then_inc(sem["rstd_ready"], 1)

            def residual(l):
                for i in range(NT):
                    pool.wait_ge(sem["out_msq"], NT * l + i + 1)
                    g.tensor_tensor(rso[:, i:i + 1], mso[:, i:i + 1], neghalf[:, 0:1], ALU.pow).then_inc(sem["out_rstd"], 1)
                    pool.wait_ge(sem["out_gpg"], 2 * (NT * l + i) + 1)
                    if l == 0 and i == 0:
                        pool.wait_ge(sem["x_loaded"], 32)
                    g.tensor_tensor(xr[:, i, 0:512], xr[:, i, 0:512], (otmp, otmp1)[l][:, i % 2, 0:512], ALU.add).then_inc(sem["out_res"], 1)
                    if l == 0 and i >= 2:
                        rstd(1, i - 2)

            for i in range(NT):
                rstd(0, i)
            pool.wait_ge(sem["stT_done"], 4)
            g.memset(TP, 0.0).then_inc(sem["T_zero"], 1)
            pool.wait_ge(sem["cq_msq"], 1)
            g.tensor_tensor(rst_c, msq_c, neghalf[:], ALU.pow).then_inc(sem["cq_rstd"], 1)
            pool.wait_ge(sem["cq_rstd"], 1)
            for i in range(NT):
                g.tensor_scalar(cqt[:, i, 0:QR], cqt[:, i, 0:QR], rst_c[:, i:i + 1], MSCALE, ALU.mult, ALU.mult).then_inc(sem["cq_scaled"], 1)
                g.tensor_scalar(cqt[:, i, QR:D], cqt[:, i, QR:D], rst_c[:, 4 + i:5 + i], None, ALU.mult).then_inc(sem["cq_scaled"], 1)

            def silu2(z, tanh, n, first, f0=0):
                for f in range(f0, f0 + n):
                    pool.wait_ge(sem["th_act"], first + f - f0 + 1)
                    link(g.tensor_scalar(tanh[:, f % 2, :], tanh[:, f % 2, :], 1.0, None, ALU.add))
                    g.tensor_tensor(z[:, f, :], z[:, f, :], tanh[:, f % 2, :], ALU.mult).then_inc(sem["z_pool"], 1)

            silu2(zaT, th, 4, 0)
            silu2(zbT, th, 4, 4)
            residual(0)
            for i in range(2, NT):
                rstd(1, i)
            silu2(zT, th1, 2, 8)
            g.memset(vc, 0.0).then_inc(sem["pad_ready"], 1)
            pool.wait_ge(sem["hid_done"], 2)
            g.memset(PcT.rearrange("p h n -> p (h n)"), 0.0).then_inc(sem["pad_ready"], 1)
            silu2(zT, th1, 6, 10, 2)
            residual(1)

        @block.scalar
        def _(act):
            a = nc.scalar
            chain = [0]

            def link(ins):
                chain[0] += 1
                ins.then_inc(sem["act_chain"], 1)
                act.wait_ge(sem["act_chain"], chain[0])

            X = lambda n: small[0:32, NPW + n, :]
            act.wait_ge(sem["colT_done"], 1)
            a.activation(sct[:], bank[0][:, 0:KD], ACT.Tanh, scale=0.5).then_inc(sem["sc_ready"], 1)
            act.wait_ge(sem["lam_loaded"], 48)
            a.activation(dtc, dtc, ACT.Exp).then_inc(sem["lam_exp"], 1)
            act.wait_ge(sem["lam_red"], 1)
            a.activation(X(9), X(2), ACT.Exp).then_inc(sem["lam_exp"], 1)
            a.activation(small[0:32, iX + 2, :], X(2), ACT.Exp, scale=float(L)).then_inc(sem["lam_exp"], 1)
            act.wait_ge(sem["half_ready"], 1)
            act.wait_ge(sem["lam_red"], 2)
            a.activation(X(7), X(5), ACT.Sin).then_inc(sem["lam_sin"], 1)
            a.activation(X(8), X(6), ACT.Sin, scale=-1.0, bias=halfpi[0:32, :]).then_inc(sem["lam_sin"], 1)

            vec = [(V_PRE, t["pre_norm_g"].rearrange("l (k p) -> (l k) p", p=P)),
                   (V_BADA, t["b_ada"].rearrange("l (k p) -> (l k) p", p=P)),
                   (V_POST, t["post_norm_g"].rearrange("l (k p) -> (l k) p", p=P)),
                   (V_QN, t["ev_q_norm_g"].rearrange("l (k p) -> (l k) p", p=P)),
                   (V_KVN, t["ev_kv_norm_g"].rearrange("l (k p) -> (l k) p", p=P)),
                   (V_BGLU, t["ev_b_glu"].rearrange("l (k p) -> (l k) p", p=P)),
                   (V_DSK, t["ev_d_skip"][0].rearrange("(k a) h -> k (a h)", k=4))]
            for r, src in vec:
                act.dma_start(rows[r:r + src.shape[0], :], src).then_inc(sem["vec_loaded"], 16)
            for b in range(2):
                act.dma_start(perows[CL * b:CL * b + CL, :], t[("od_cmp_k_pe", "od_cmp_v_pe")[b]][0]).then_inc(sem["vec_loaded"], 16)
            act.dma_start(cst[:], t["cst"]).then_inc(sem["const_loaded"], 16)
            act.dma_start(posi, t["positions"].to_broadcast([P, S])).then_inc(sem["pos_loaded"], 16)
            act.dma_start(BA[0:64], t["ev_b_re"][0].rearrange("g p h -> p g h")).then_inc(sem["s5_loaded"], 16)
            act.dma_start(BA[64:128], t["ev_b_im"][0].rearrange("g p h -> p g h")).then_inc(sem["s5_loaded"], 16)
            act.dma_start(CN[:, :, 0:64], t["ev_c_re"][0].rearrange("(f a) h p -> (a h) f p", f=4)).then_inc(sem["s5_loaded"], 16)
            act.dma_start(CN[:, :, 64:128], t["ev_c_im"][0].rearrange("(f a) h p -> (a h) f p", f=4)).then_inc(sem["s5_loaded"], 16)
            for e in range(2):
                act.dma_start(wkpe[:, :, 64 * e:64 * e + 64], cols(ev_in, 0, KD, EV_KPE, EV_KPE + RO)).then_inc(sem["small_w_loaded"], 16)
            act.dma_start(wgate[:], cols(od_in, 0, KD, OD_GATE, OD_GATE + 3 * HN)).then_inc(sem["small_w_loaded"], 16)
            for b in range(2):
                act.dma_start(w2[:, b], cols(t[("od_cmp_k_w2", "od_cmp_v_w2")[b]][0], 0, 2, 0, DN)).then_inc(sem["small_w_loaded"], 16)

            def square(l, i):
                if l == 0 and i == 0:
                    act.wait_ge(sem["x_loaded"], 16)
                if l == 1:
                    act.wait_ge(sem["out_res"], 2 * (i + 1))
                    if i:
                        act.wait_ge(sem["ssq_done"], NT + i)
                a.activation((hT[:, 2 * i:2 * i + 2, :] if l == 0 else sqj).rearrange("p k n -> p (k n)"), xr[:, i, :], ACT.Square, accum_out=ssx[:, i:i + 1]).then_inc(sem["ssq_done"], 1)

            def sines(n, sin_out, cos_out, sgn, r_ap, abs_ap):
                act.wait_ge(sem["tab_abs"], n + 1)
                a.activation(sin_out, r_ap, ACT.Sin, scale=sgn).then_inc(sem["tab_sin"], 1)
                a.activation(cos_out, abs_ap, ACT.Sin, scale=-1.0, bias=halfpi[:]).then_inc(sem["tab_cos"], 1)

            for i in range(NT):
                square(0, i)

            def mod_rows(d0, d1):
                for d in range(d0, d1):
                    act.wait_ge(sem["mod_done"], 2 * d + 2)
                    if d >= 2:
                        act.wait_ge(sem["mcol_done"], d - 1)
                    a.copy(mrow[0:1, d % 2, :], bank[7 * (d % 2)][0:1, :]).then_inc(sem["mrow_act"], 1)

            mod_rows(0, R0)
            act.wait_ge(sem["const_loaded"], 16)
            sines(0, tabM[:, 1, :], tabM[:, 0, :], cst[:, 3:4], ra, rk)

            for b in range(4):
                n = min(16, NPW - 16 * b)
                act.wait_ge(sem["stT_done"], b + 1)
                src = bank[2 + b][0:64, 0:32 * n].rearrange("p (a g) -> p a g", g=NG)
                a.copy(st[0:64, 16 * b:16 * b + n, :], src).then_inc(sem["st_act"], 1)
                a.copy(st[64:128, 16 * b:16 * b + n, :], src).then_inc(sem["st_act"], 1)
            act.wait_ge(sem["CT_done"], 1)
            c1 = C1.rearrange("p g h -> p (g h)")
            a.copy(c1[0:64, :], bank[6][0:64, :]).then_inc(sem["C_act"], 1)
            a.mul(c1[64:128, :], bank[6][64:128, :], -1.0).then_inc(sem["C_act"], 1)
            act.wait_ge(sem["BB_done"], 1)
            a.copy(BB.rearrange("p g h -> p (g h)"), bank[2][:, :]).then_inc(sem["B_ready"], 1)
            act.wait_ge(sem["CT_done"], 2)
            a.mul(C2.rearrange("p g h -> p (g h)"), bank[3][:, :], -1.0).then_inc(sem["C_act"], 1)
            act.wait_ge(sem["col_ready"], 1)
            a.mul(hbg[:], col[:, V_BGLU:V_BGLU + 4], 0.5)
            mod_rows(R0, 6)
            for j in range(2):
                act.wait_ge(sem["gpg_done"], j + 1)
                a.copy(gpg[:, 512 * j:512 * j + 512], bank[6 + j][:, :]).then_inc(sem["gpg_ready"], 1)

            def hT_tiles(l):
                act.wait_ge(sem["mod_ready"], 3 + 3 * l)
                for k in range(0, KD, 2):
                    act.wait_ge(sem["xT_done"], KD * l + k + 1)
                    a.activation((hT, hlo1)[l][:, k, :], bank[k % 4][:, :], ACT.Identity, bias=mod[:, l, k:k + 1],
                                 scale=pre[:, l, k:k + 1]).then_inc(sem["hT_act"], 1)
                    if l == 1:
                        act.wait_ge(sem["hT_act"], 4 + k // 2 + 1)
                        a.copy(hTr[:, k, :], hlo1[:, k, :]).then_inc(sem["h_hi"], 1)
                        act.wait_ge(sem["hT_dve"], 4 + k // 2 + 1)
                        a.copy(hTr[:, k + 1, :], hlo1[:, k + 1, :]).then_inc(sem["h_hi"], 1)

            hT_tiles(0)

            def pj_wait(n):
                act.wait_ge(sem["pj_done"], n + 1)

            def z_tile(n, b, z, tanh, f, zn):
                pj_wait(n)
                if zn >= 2:
                    act.wait_ge(sem["z_pool"], zn - 1)
                link(a.copy(z[:, f, :], b[:, :]))
                a.activation(tanh[:, zn % 2, :], b[:, :], ACT.Tanh, scale=0.5).then_inc(sem["th_act"], 1)

            thj = th[:, 0, 0:256]

            def G_transposed(b0):
                for b in range(b0, b0 + 4):
                    act.wait_ge(sem["GT_done"], b + 1)
                    a.copy(GT[:, 4 * b:4 * b + 4, :].rearrange("p g n -> p (g n)"), bank[4 + b % 4][:, :]).then_inc(sem["GT_act"], 1)

            def K_blocks(hh):
                for b in range(4 * hh, 4 * hh + 4):
                    act.wait_ge(sem["Kc_done"], b + 1)
                    if b == 0:
                        act.wait_ge(sem["tab_cos"], 1)
                    if b == 4:
                        act.wait_ge(sem["T_stored"], 16 * L)
                    a.copy(Kh[0:NH, 4 * (b % 4):4 * (b % 4) + 4, :].rearrange("p g n -> p (g n)"),
                           bank[4 + b % 4][0:NH, :]).then_inc(sem["Kc_act"], 1)
                act.wait_ge(sem["T_zero"], 1)
                act.wait_ge(sem["Kc_act"], 4 * (hh + 1))
                for s in range(L):
                    act.dma_start(TP[NH * s:NH * s + NH, 16 * hh:16 * hh + 16, NH * s:P],
                                  Kh[0:NH, :, 0:P - NH * s]).then_inc(sem["T_stored"], 16)
            for n, tile in enumerate(PJ0):
                if tile == ("zb", 2):
                    act.wait_ge(sem["y_skip"], 4)
                    a.activation(y2.rearrange("p f n -> p (f n)"), yT.rearrange("p f n -> p (f n)"), ACT.Square).then_inc(sem["y_sq"], 1)
                if tile == ("zb", 3):
                    for j in range(3):
                        mla_split_high(act, a, j)
                    act.wait_ge(sem["y_arg"], 1)
                    a.activation(y2.rearrange("p f n -> p (f n)"), y2.rearrange("p f n -> p (f n)"), ACT.Tanh, scale=C_GELU).then_inc(sem["y_tanh"], 1)
                if tile[0] == "u":
                    pj_wait(n)
                    f = tile[1]
                    a.copy(uTp[:, f, :].rearrange("p (s c) -> p c s", s=L),
                           bank[n % 4][:, :].rearrange("p (c s) -> p c s", s=L)).then_inc(sem["pj_act"], 1)
                    act.wait_ge(sem["pj_act"], n + 1)
                    act.dma_start(scr_u[8 * f:8 * f + 8].rearrange("g h s c -> (g h) (s c)"), uTp[:, f, :]).then_inc(sem["u_stored"], 16)
                elif tile[0] == "cq":
                    pj_wait(n)
                    if n == 4:
                        act.wait_ge(sem["xT_done"], KD)
                    j, i = tile[1:]
                    link(a.activation(thj, bank[n % 4][:, 0:256], ACT.Square, accum_out=ssq_c[:, 4 * j + i:4 * j + i + 1]))
                    a.copy(cqt[:, i, 256 * j:256 * j + 256], bank[n % 4][:, 0:256]).then_inc(sem["pj_act"], 1)
                    if i == NT - 1 and j < 2:
                        G_transposed(4 * j)
                    elif i == NT - 1:
                        K_blocks(j - 2)
                elif tile[0] == "ms":
                    pj_wait(n)
                    d = tile[1]
                    a.copy(m1raw[:, 4 * d:4 * d + 4], bank[n % 4][:, 0:512:P]).then_inc(sem["pj_act"], 1)
                elif tile[0] == "kpe":
                    pj_wait(n)
                    a.copy(kpT, bank[n % 4][:, :]).then_inc(sem["pj_act"], 1)
                    act.wait_ge(sem["u_stored"], 64)
                    act.wait_ge(sem["r8_ready"], 1)
                    for s in range(L):
                        act.dma_start(U[NH * s:NH * s + NH, :, :], scr_u[:, :, s, :].rearrange("g h c -> h g c")).then_inc(sem["u_back"], 16)
                elif tile[0] == "za":
                    if tile[1] == 0:
                        act.wait_ge(sem["T_stored"], 32 * L)
                    z_tile(n, bank[n % 4], zaT, th, tile[1], tile[1])
                    if tile[1] == 3:
                        for b in range(8):
                            act.wait_ge(sem["Y_done"], b + 1)
                            a.copy(Yc[:, :, 64 * b:64 * b + 64].rearrange("c s (g h) -> c g s h", g=4),
                                   bank[4 + 2 * (b // 4) + b % 2][0:NC, :].rearrange("c (g s h) -> c g s h", g=4, s=L)).then_inc(sem["Y_act"], 1)
                else:
                    z_tile(n, bank[n % 4], zbT, th, tile[1], 4 + tile[1])

            for f in range(8):
                act.wait_ge(sem["cqT_done"], f + 1)
                a.activation(hTr[:, f, :], bank[4 + f % 4][:, :], ACT.Copy, scale=col[:, V_QN + f:V_QN + f + 1]).then_inc(sem["cqT_act"], 1)
            for n in range(6):
                act.wait_ge(sem["q_done"], n + 1)
                if n < 5:
                    mla_split_high(act, a, n + 3)
                if n % 3 < 2:
                    a.copy(qnT[:, 2 * (n // 3) + n % 3, :], bank[n % 4][:, :]).then_inc(sem["q_act"], 1)
            for n in range(8):
                act.wait_ge(sem["kv_done"], n + 1)
                dst = knT[:, n, :] if n < 4 else vM[:, n - 4, :]
                a.copy(dst, bank[4 + n % 4][:, :]).then_inc(sem["kv_act"], 1)
                if n < 4:
                    act.wait_ge(sem["y_gelu"], 1)
                    a.copy(hTr[:, n, :], yT[:, n, :]).then_inc(sem["y_hi"], 1)
                if n in (4, 7):
                    mla_split_high(act, a, 8 + n // 7)

            for f in range(4):
                act.wait_ge(sem["glu_done"], f + 1)
                a.activation(y2[:, f, :], bank[f][:, :], ACT.Tanh, scale=0.25, bias=hbg[:, f:f + 1]).then_inc(sem["glu_act"], 1)

            def mix_high(l, f, mix):
                if l == 0 and f < 4:
                    act.wait_ge(sem["ya_ready"], f + 1)
                else:
                    act.wait_ge(sem["o_dve"], f - 3 if l == 0 else MH + f + 1)
                a.copy(hTr[:, f, :], mix[:, f, :]).then_inc(sem["mix_hi"], 1)

            def attend(l, units, n0, Pb, PTb, nP, mix):
                N, per = len(units), len(units) // (MH, HN)[l]
                for n in range(N + 6):
                    if l == 0 and 2 <= n < 6:
                        mix_high(0, n - 2, mix)
                    if l == 0 and n == 7:
                        act.wait_ge(sem["rope_done"], 3)
                        split_high(act, a, SPLIT[0])
                    if n >= 6 and (n - 5) % per == 0:
                        mix_high(l, (n - 5) // per - 1 + (4, 0)[l], mix)
                    if n < N:
                        h, i, b = units[n]
                        w = P * (i + 1)
                        act.wait_ge(sem["s_max"], n0 + n + 1)
                        if n >= nP:
                            act.wait_ge(sem["pt_done"], n0 + n - nP + 1)
                        a.activation(Pb[:, n % nP, 0:w], bank[SB[n % 3]][:, 0:w], ACT.Exp, bias=smax[:, n % 4:n % 4 + 1],
                                     accum_out=ssum[:, n % 4:n % 4 + 1]).then_inc(sem["s_exp"], 1)
                    m = n - 2
                    if 0 <= m < N and m % 2 == 0:
                        w = P * (units[m][1] + 1)
                        act.wait_ge(sem["pt_done"], n0 + m + 1)
                        if m >= 2:
                            act.wait_ge(sem["pv_done"], n0 + m - 1)
                        a.copy(PTb[:, m % 2, 0:w], bank[TB[m % 2]][:, 0:w]).then_inc(sem["pt_act"], 1)

            attend(0, U0, 0, Pm, PT, 3, mixT)
            for n in range(1, 5):
                split_high(act, a, SPLIT[n])

            def y_squares(l):
                for e in range(2):
                    for i in range(NT):
                        if e == 0:
                            act.wait_ge(sem["out_half"], l + 1)
                        else:
                            act.wait_ge(sem["out_done"], NT * l + i + 1)
                        n = NT * e + i
                        if n:
                            act.wait_ge(sem["out_sq"], 2 * NT * l + n)
                        a.activation(ysj, bank[2 * i + e][:, :], ACT.Square, accum_out=sso[:, n:n + 1]).then_inc(sem["out_sq"], 1)
                        if l == 0 and e == 1 and i >= 2:
                            square(1, i - 2)

            y_squares(0)

            for i in range(2, NT):
                square(1, i)
            for j in range(2):
                act.wait_ge(sem["gpg_done"], 3 + j)
                a.copy(gpg[:, 512 * j:512 * j + 512], bank[6 + j][:, :]).then_inc(sem["gpg_ready"], 1)
            act.wait_ge(sem["xn_ready"], 2 * NT)
            act.dma_start(th1[:, 0, :].bitcast(I32), t["positions"].to_broadcast([P, S])).then_inc(sem["pos_loaded"], 16)
            hT_tiles(1)
            split_high(act, a, SPLIT[5])
            a.copy(wgate_hi[:], wgate[:]).then_inc(sem["gate_w"], 1)
            sines(1, tabN[:, 1, :], tabN[:, 0, :], cst[:, 2:3], rt1[:, 0, :], rt1[:, 1, :])
            n0 = NJ0

            def hidden():
                for b in range(2):
                    src = bank[4 + b][0:NB, 0:CH].rearrange("p (e n) -> p e n", e=2)
                    for key in [("w1", b, j) for j in range(1, 4)] + [("w1", 1, 0) if b == 0 else ("z", 0)]:
                        split_high(act, a, key)
                    act.wait_ge(sem["hid_done"], b + 1)
                    a.copy(hid[b][0:NB], src).then_inc(sem["hid_sq"], 1)
                    a.activation(hsq[b][0:NB], src, ACT.Square).then_inc(sem["hid_sq"], 1)
                for b in range(2):
                    act.wait_ge(sem["hid_arg"], b + 1)
                    a.activation(hsq[b][0:NB], hsq[b][0:NB], ACT.Tanh, scale=C_GELU).then_inc(sem["hid_tanh"], 1)

            for n, tile in enumerate(PJ1):
                kind, b = tile[0], bank[n % 4]
                if tile == ("z", 0):
                    hidden()
                if next_split(n) and tile != ("z", 6):
                    split_high(act, a, next_split(n))
                if tile == ("q", 0):
                    for b2 in range(2):
                        act.wait_ge(sem["kc_ready"], 4 * b2 + 4)
                        a.copy(R_high[:, b2, :], R[b2].rearrange("p l g n -> p (l g n)")).then_inc(sem["R_hi"], 1)
                if tile == ("z", 3):
                    for b2 in range(2):
                        act.wait_ge(sem["hidT_done"], b2 + 1)
                        a.copy(hidT[b2], bank[6 + b2][:, 0:P].rearrange("p (e n) -> p e n", e=2)[:, :, 0:NB]).then_inc(sem["hidT_act"], 1)
                    act.wait_ge(sem["cmp_done"], 2)
                    act.wait_ge(sem["pad_ready"], 1)
                    a.mul(vc[0:NCMP].rearrange("p g n -> p (g n)"), bank[5][0:NCMP, 0:GN * DN], 0.5).then_inc(sem["cmp_act"], 1)
                if tile == ("z", 5):
                    for g in range(GN):
                        act.wait_ge(sem["cs_sub"], g + 1)
                        pc = Pc[g].rearrange("p a n -> p (a n)")
                        a.activation(pc, pc, ACT.Exp).then_inc(sem["cs_exp"], 1)
                if tile in (("z", 6), ("z", 7)):
                    act.wait_ge(sem["pad_ready"], 2)
                    for h in range(REP * (tile[1] - 6), REP * (tile[1] - 5)):
                        act.wait_ge(sem["cpt_done"], h + 1)
                        a.copy(PcT[0:NCMP, h, :], bank[4 + h % 2][0:NCMP, :]).then_inc(sem["cpt_act"], 1)
                if tile == ("z", 6):
                    split_high(act, a, next_split(n))
                if kind in ("v", "gate", "z"):
                    pj_wait(n0 + n)
                if kind == "v":
                    a.copy((vs, vw)[tile[1]][:, tile[2], :], b[:, 0:256]).then_inc(sem["v_act"], 1)
                elif kind == "gate":
                    a.activation(gT[0:3 * HN], b[0:3 * HN, :], ACT.Tanh, scale=0.5).then_inc(sem["gate_act"], 1)
                elif kind == "z":
                    z_tile(n0 + n, b, zT, th1, tile[1], 8 + tile[1])
            attend(1, U1, N0, Pm1, PT1, 3, mix1)
            for j in range(1, 4):
                split_high(act, a, ("wout1", j))
            y_squares(1)

        @block.vector
        def _(dve):
            v = nc.vector
            chain = [0]

            def link(ins):
                chain[0] += 1
                ins.then_inc(sem["dve_chain"], 1)
                dve.wait_ge(sem["dve_chain"], chain[0])

            X = lambda n: small[0:32, NPW + n, :]
            v.memset(halfpi[:], math.pi / 2).then_inc(sem["half_ready"], 1)
            v.memset(small[0:32, iP, :], 1.0).then_inc(sem["dve_chain"], 1)
            for r in (iP + TAPS, iF + L, iC + L):
                v.memset(small[0:32, r, :], 0.0).then_inc(sem["dve_chain"], 1)
            for r in (iF, iC):
                v.memset(small[0:32, r, :], 1.0).then_inc(sem["dve_chain"], 1)
            chain[0] += 6

            def reduce_angle(k, r, ang, absr):
                link(v.tensor_scalar(k, ang, 1.0 / TWO_PI, MAGIC, ALU.mult, ALU.add))
                link(v.tensor_scalar(k, k, MAGIC, None, ALU.subtract))
                link(v.scalar_tensor_tensor(r, k, -PI_A, ang, ALU.mult, ALU.add))
                link(v.scalar_tensor_tensor(r, k, -PI_B, r, ALU.mult, ALU.add))
                link(v.scalar_tensor_tensor(r, k, -PI_C, r, ALU.mult, ALU.add))
                link(v.tensor_scalar(r, r, PI_SAFE, -PI_SAFE, ALU.min, ALU.max))
                return v.scalar_tensor_tensor(absr, r, -1.0, r, ALU.mult, ALU.max)

            dve.wait_ge(sem["sc_ready"], 1)
            link(v.scalar_tensor_tensor(sc[:], sct[:], 1.0, bank[0][:, 0:KD], ALU.add, ALU.mult))
            v.tensor_scalar(sc[:], sc[:], 0.5, None, ALU.mult).then_inc(sem["sc_ready"], 1)
            dve.wait_ge(sem["lam_exp"], 1)
            v.tensor_scalar(X(2), X(0), dtc, None, ALU.mult).then_inc(sem["lam_red"], 1)
            link(v.tensor_scalar(X(3), X(1), dtc, None, ALU.mult))
            reduce_angle(X(4), X(5), X(3), X(6)).then_inc(sem["lam_red"], 1)
            def mean_square(l, i):
                dve.wait_ge(sem["ssq_done"], NT * l + i + 1)
                v.tensor_scalar(msx[:, i:i + 1], ssx[:, i:i + 1], 1.0 / D, EPS, ALU.mult, ALU.add).then_inc(sem["msq_done"], 1)

            def normalise(l, i, dst):
                dve.wait_ge(sem["rstd_ready"], NT * l + i + 1)
                v.tensor_scalar(dst[:, i, :], xr[:, i, :], rsx[:, i:i + 1], None, ALU.mult).then_inc(sem["xn_ready"], 1)

            tt = [at(oD + 2048 + 256 * q, 4, NP_) for q in range(4)]

            def cmul(o_re, o_im, a_re, a_im, b_re, b_im, n, last=False):
                T0, T1, T2, T3 = (q[0:32, 0:n, :] for q in tt)
                v.tensor_tensor(T0, a_re, b_re, ALU.mult).then_inc(sem["dve_chain"], 1)
                v.tensor_tensor(T1, a_im, b_im, ALU.mult).then_inc(sem["dve_chain"], 1)
                v.tensor_tensor(T2, a_re, b_im, ALU.mult).then_inc(sem["dve_chain"], 1)
                chain[0] += 3
                link(v.tensor_tensor(T3, a_im, b_re, ALU.mult))
                v.tensor_tensor(o_re, T0, T1, ALU.subtract).then_inc(sem["dve_chain"], 1)
                chain[0] += 1
                ins = v.tensor_tensor(o_im, T2, T3, ALU.add)
                if last:
                    ins.then_inc(sem["pw_ready"], 1)
                else:
                    link(ins)

            def sm(a0, n):
                return small[0:32, a0:a0 + n, :]

            def one(a0, n):
                return small[0:32, a0:a0 + 1, :].to_broadcast([32, n, NP_])

            dve.wait_ge(sem["lam_exp"], 3)
            dve.wait_ge(sem["lam_sin"], 2)
            v.tensor_tensor(sm(iP + 1, 1), sm(NPW + 9, 1), sm(NPW + 8, 1), ALU.mult).then_inc(sem["dve_chain"], 1)
            chain[0] += 1
            link(v.tensor_tensor(sm(iP + TAPS + 1, 1), sm(NPW + 9, 1), sm(NPW + 7, 1), ALU.mult))
            link(v.tensor_tensor(X(10), X(0), X(0), ALU.mult))
            link(v.tensor_tensor(X(11), X(1), X(1), ALU.mult))
            link(v.tensor_tensor(X(10), X(10), X(11), ALU.add))
            link(v.reciprocal(X(10), X(10)))
            link(v.tensor_scalar(X(11), small[0:32, iP + 1, :], 1.0, None, ALU.subtract))
            ni = small[0:32, iP + TAPS + 1, :]
            link(v.tensor_tensor(X(12), X(11), X(0), ALU.mult))
            link(v.tensor_tensor(X(13), ni, X(1), ALU.mult))
            link(v.tensor_tensor(X(12), X(12), X(13), ALU.add))
            link(v.tensor_tensor(small[0:32, iX, :], X(12), X(10), ALU.mult))
            link(v.tensor_tensor(X(12), ni, X(0), ALU.mult))
            link(v.tensor_tensor(X(13), X(11), X(1), ALU.mult))
            link(v.tensor_tensor(X(12), X(12), X(13), ALU.subtract))
            link(v.tensor_tensor(small[0:32, iX + 1, :], X(12), X(10), ALU.mult))
            p, q = iP, iP + TAPS
            cmul(sm(p + 2, 1), sm(q + 2, 1), sm(p + 1, 1), sm(q + 1, 1), sm(p + 1, 1), sm(q + 1, 1), 1)
            cmul(sm(p + 3, 2), sm(q + 3, 2), sm(p + 1, 2), sm(q + 1, 2), one(p + 2, 2), one(q + 2, 2), 2)
            cmul(sm(p + 5, 4), sm(q + 5, 4), sm(p + 1, 4), sm(q + 1, 4), one(p + 4, 4), one(q + 4, 4), 4)
            cmul(sm(NPW + 14, 1), sm(NPW + 15, 1), sm(NPW + 8, 1), sm(NPW + 7, 1), sm(NPW + 8, 1), sm(NPW + 7, 1), 1)
            w_re, w_im = NPW + 14, NPW + 15

            def square():
                cmul(sm(w_re, 1), sm(w_im, 1), sm(w_re, 1), sm(w_im, 1), sm(w_re, 1), sm(w_im, 1), 1)

            square()
            square()
            for base in (iF, iC):
                p, q = base, base + L
                for n in (1, 2, 4):
                    end = base == iC and n == 4
                    cmul(sm(p + n, n), sm(q + n, n), sm(p, n), sm(q, n), one(w_re, n), one(w_im, n), n, last=end)
                    if not end:
                        square()

            dve.wait_ge(sem["colT_done"], 3)
            v.tensor_copy(col[:], bank[6][:, 0:V_N]).then_inc(sem["col_ready"], 1)
            v.tensor_copy(peT[:], bank[6][:, 128:192]).then_inc(sem["col_ready"], 1)
            dve.wait_ge(sem["col_ready"], 2)
            dve.wait_ge(sem["pos_loaded"], 16)
            dve.wait_ge(sem["const_loaded"], 16)
            link(v.tensor_copy(rk, posi))
            link(v.tensor_scalar(posb, rk, cst[:, 1:2], None, ALU.mult))
            reduce_angle(rk, ra, posb, rk).then_inc(sem["tab_abs"], 1)
            for i in range(NT):
                mean_square(0, i)
            for i in range(NT):
                normalise(0, i, xr)

            def scales(l):
                v.scalar_tensor_tensor(pre[:, l, :], mod[:, l, KD:2 * KD], 1.0, col[:, V_PRE + KD * l:V_PRE + KD * l + KD], ALU.add, ALU.mult).then_inc(sem["mod_ready"], 1)
                v.tensor_tensor(gcol[:, l, :], mod[:, l, 2 * KD:], col[:, V_POST + KD * l:V_POST + KD * l + KD], ALU.mult).then_inc(sem["mod_ready"], 1)

            def modulation0():
                dve.wait_ge(sem["mcol_done"], 6)
                v.tensor_tensor(mod[:, 0, :], bank[1][:, 0:24], col[:, V_BADA:V_BADA + 24], ALU.add).then_inc(sem["mod_ready"], 1)
                dve.wait_ge(sem["mod_ready"], 1)
                scales(0)

            def modulation1_sums(d):
                if d in (3, 4):
                    dve.wait_ge(sem["pj_done"], PJ0.index(("ms", d - 1)) + 1)
                if d == 5:
                    dve.wait_ge(sem["Y_done"], 8)
                for e in range(2):
                    key, dst = ("ada", 1, 2 * d + e), macc[d][:, e, :]
                    w_ready(dve, key)
                    link(v.tensor_scalar(dst, slot(key)[:, 0, :], sc[:, 0:1], None, ALU.mult))
                    for k in range(1, KD):
                        ins = v.scalar_tensor_tensor(dst, slot(key)[:, k, :], sc[:, k:k + 1], dst, ALU.mult, ALU.add)
                        if k < KD - 1:
                            link(ins)
                    ins.then_inc(sem["macc_done"], 1)

            def modulation1():
                dve.wait_ge(sem["pj_act"], evac0[-1])
                v.tensor_tensor(mod[:, 1, :], m1raw[:], col[:, V_BADA + 24:V_BADA + 48], ALU.add).then_inc(sem["mod_ready"], 1)
                dve.wait_ge(sem["mod_ready"], 4)
                scales(1)

            modulation0()

            def hT_tiles(l):
                dve.wait_ge(sem["mod_ready"], 3 + 3 * l)
                for k in range(1, KD, 2):
                    dve.wait_ge(sem["xT_done"], KD * l + k + 1)
                    v.tensor_scalar((hT, hlo1)[l][:, k, :], bank[k % 4][:, :], pre[:, l, k:k + 1], mod[:, l, k:k + 1], ALU.mult, ALU.add).then_inc(sem["hT_dve"], 1)
                    if l == 1:
                        for k2 in (k - 1, k):
                            h_low(k2)

            def h_low(k):
                dve.wait_ge(sem["h_hi"], k + 1)
                v.tensor_tensor(hlo1r[:, k, :], hlo1[:, k, :], hTr[:, k, :].bitcast(F32), ALU.subtract).then_inc(sem["h_lo"], 1)

            hT_tiles(0)

            dve.wait_ge(sem["st_act"], 8)
            dve.wait_ge(sem["B_ready"], 1)
            fr = st[:, iX, :].unsqueeze(2).to_broadcast([P, NG, NH])
            fi = st[:, iX + 1, :].unsqueeze(2).to_broadcast([P, NG, NH])
            tb = at(oD + 2048, NG, NH)
            link(v.tensor_tensor(Bb, BA, fr, ALU.mult))
            link(v.tensor_tensor(tb, BB, fi, ALU.mult))
            link(v.tensor_tensor(Bb, Bb, tb, ALU.add))
            link(v.tensor_tensor(iBb, BB, fr, ALU.mult))
            link(v.tensor_tensor(tb, BA, fi, ALU.mult))
            link(v.tensor_tensor(iBb, iBb, tb, ALU.subtract))
            dve.wait_ge(sem["CT_done"], 1)
            def powers(base, n, qq, rev):
                a_ = st[:, base:base + n, 8 * qq:8 * qq + 8]
                if rev:
                    a_ = a_[:, ::-1, :]
                return a_.rearrange("p t g -> p g t").unsqueeze(3).to_broadcast([P, 8, n, NH])

            def per_tap(m, n, qq):
                return m[:, 8 * qq:8 * qq + 8, :].unsqueeze(2).to_broadcast([P, 8, n, NH])

            for qq in range(4):
                if qq == 2:
                    modulation1_sums(0)
                    modulation1_sums(1)
                if qq >= 2:
                    dve.wait_ge(sem["GT_done"], 2 * (qq - 1))
                G4 = Gc[qq % 2].rearrange("p g (s h) -> p g s h", s=L)
                T4 = tmpG[:, :, 0:L * NH].rearrange("p g (s h) -> p g s h", s=L)
                link(v.tensor_tensor(G4, powers(iP, L, qq, True), per_tap(Bb, L, qq), ALU.mult))
                link(v.tensor_tensor(T4, powers(iP + TAPS, L, qq, True), per_tap(iBb, L, qq), ALU.mult))
                v.tensor_tensor(G4, G4, T4, ALU.add).then_inc(sem["G_ready"], 1)
            dve.wait_ge(sem["C_act"], 3)
            for qq in range(4):
                W4 = W1[:, 8 * qq:8 * qq + 8, :].rearrange("p g (s h) -> p g s h", s=TAPS)
                T4 = tmpG.rearrange("p g (s h) -> p g s h", s=TAPS)
                dve.wait_ge(sem["G_ready"], 4)
                link(v.tensor_tensor(W4, powers(iP, TAPS, qq, False), per_tap(C1, TAPS, qq), ALU.mult))
                link(v.tensor_tensor(T4, powers(iP + TAPS, TAPS, qq, False), per_tap(C2, TAPS, qq), ALU.mult))
                v.tensor_tensor(W4, W4, T4, ALU.add).then_inc(sem["W1_ready"], 1)
            modulation1_sums(2)
            for qq in range(2):
                gs = slice(16 * qq, 16 * qq + 16)

                def co(base):
                    return st[:, base:base + L, gs].rearrange("p a g -> p g a").unsqueeze(3).to_broadcast([P, 16, L, L])

                def fi_(base):
                    return st[:, base:base + L, gs].rearrange("p b g -> p g b").unsqueeze(2).to_broadcast([P, 16, L, L])

                c4 = rotc[:, gs, :].rearrange("p g (a b) -> p g a b", a=L)
                s4 = rots[:, gs, :].rearrange("p g (a b) -> p g a b", a=L)
                t4 = at(oD + 2048, 16, L, L)
                link(v.tensor_tensor(c4, co(iC), fi_(iF), ALU.mult))
                link(v.tensor_tensor(t4, co(iC + L), fi_(iF + L), ALU.mult))
                link(v.tensor_tensor(c4, c4, t4, ALU.subtract))
                link(v.tensor_tensor(s4, co(iC), fi_(iF + L), ALU.mult))
                link(v.tensor_tensor(t4, co(iC + L), fi_(iF), ALU.mult))
                link(v.tensor_tensor(s4, s4, t4, ALU.add))
            v.tensor_scalar(rots[0:64], rots[0:64], -1.0, None, ALU.mult).then_inc(sem["rot_ready"], 1)
            dve.wait_ge(sem["GT_done"], 8)
            link(v.tensor_copy(r8b, st[:, iX + 2, :].unsqueeze(2).to_broadcast([P, NG, NC])))
            v.memset(Xs[:, :, 0:1], 0.0).then_inc(sem["zero_ready"], 1)
            v.memset(r8b[:, :, 0:1], 0.0).then_inc(sem["r8_ready"], 1)
            dve.wait_ge(sem["r8_ready"], 1)
            dve.wait_ge(sem["rot_ready"], 1)

            dve.wait_ge(sem["pj_act"], evac0[PJ0.index(("cq", 3, NT - 1))])
            link(v.tensor_tensor(msq_c[:, 0:4], ssq_c[:, 0:4], ssq_c[:, 4:8], ALU.add))
            link(v.tensor_tensor(msq_c[:, 0:4], msq_c[:, 0:4], ssq_c[:, 8:12], ALU.add))
            link(v.tensor_scalar(msq_c[:, 4:8], ssq_c[:, 12:16], 1.0 / KVR, EPS, ALU.mult, ALU.add))
            v.tensor_scalar(msq_c[:, 0:4], msq_c[:, 0:4], 1.0 / QR, EPS, ALU.mult, ALU.add).then_inc(sem["cq_msq"], 1)

            modulation1_sums(3)
            for hh in range(2):
                if hh == 1:
                    dve.wait_ge(sem["Xs_ready"], 1)
                zv, tv = zb5.rearrange("p g c -> p (g c)"), tb5.rearrange("p g c -> p (g c)")
                rc = rotc[:, 16 * hh:16 * hh + 16, :].rearrange("p g c -> p (g c)")
                rs = rots[:, 16 * hh:16 * hh + 16, :].rearrange("p g c -> p (g c)")
                for b in range(2):
                    dve.wait_ge(sem["V_done"], 2 * hh + b + 1)
                    vb, cs = bank[4 + 2 * hh + b], slice(512 * b, 512 * b + 512)
                    v.tensor_tensor(tv[0:64, cs], vb[64:128, :], rs[64:128, cs], ALU.mult).then_inc(sem["dve_chain"], 1)
                    v.tensor_tensor(tv[64:128, cs], vb[0:64, :], rs[0:64, cs], ALU.mult).then_inc(sem["dve_chain"], 1)
                    v.tensor_tensor(zv[:, cs], vb[:, :], rc[:, cs], ALU.mult).then_inc(sem["z_dve"], 1)
                    chain[0] += 2
                dve.wait_ge(sem["dve_chain"], chain[0])
                dve.wait_ge(sem["z_dve"], 2 * hh + 2)
                link(v.tensor_tensor(zv, zv, tv, ALU.add))
                link(v.tensor_tensor_scan(tv, r8b[:, 16 * hh:16 * hh + 16, :].rearrange("p g c -> p (g c)"), zv, 0.0, ALU.mult, ALU.add))
                link(v.tensor_tensor(zv[0:64], tv[64:128], rs[64:128], ALU.mult))
                link(v.tensor_tensor(zv[64:128], tv[0:64], rs[0:64], ALU.mult))
                link(v.tensor_tensor(tv, tv, rc, ALU.mult))
                if hh == 1:
                    dve.wait_ge(sem["Y_done"], 4)
                v.tensor_tensor(Xs[:, :, 1:], tb5, zb5, ALU.subtract).then_inc(sem["Xs_ready"], 1)

            modulation1_sums(4)
            for f in range(4):
                dve.wait_ge(sem["YT_done"], f + 1)
                v.scalar_tensor_tensor(yT[:, f, :], uTp[:, f, :], col[:, V_DSK + f:V_DSK + f + 1], bank[4 + f][:, :], ALU.mult, ALU.add).then_inc(sem["y_skip"], 1)
            modulation1_sums(5)
            dve.wait_ge(sem["y_sq"], 1)
            yv, sv = yT.rearrange("p f n -> p (f n)"), y2.rearrange("p f n -> p (f n)")
            link(v.tensor_scalar(sv, sv, 0.044715, 1.0, ALU.mult, ALU.add))
            v.tensor_tensor(sv, sv, yv, ALU.mult).then_inc(sem["y_arg"], 1)
            for n in range(3):
                mla_split_low(dve, v, n)
            dve.wait_ge(sem["y_tanh"], 1)
            v.scalar_tensor_tensor(yv, sv, 1.0, yv, ALU.add, ALU.mult).then_inc(sem["y_gelu"], 1)
            dve.wait_ge(sem["y_gelu"], 1)
            for f in range(8):
                dve.wait_ge(sem["cqT_act"], f + 1)
                v.scalar_tensor_tensor(cqr[:, f, :], bank[4 + f % 4][:, :], col[:, V_QN + f:V_QN + f + 1], hTr[:, f, :].bitcast(F32),
                                       ALU.mult, ALU.subtract).then_inc(sem["cq_lo"], 1)

            def rope(dst, x, cos, sin, q, tmp, scalar=1.0):
                A, B = tmp
                link(v.scalar_tensor_tensor(A, x, scalar, cos, ALU.mult, ALU.mult))
                for b0 in range(0, P, 2 * q):
                    lo, hi = slice(b0, b0 + q), slice(b0 + q, b0 + 2 * q)
                    link(v.scalar_tensor_tensor(B[lo], x[hi], scalar, sin[hi], ALU.mult, ALU.mult))
                    link(v.scalar_tensor_tensor(B[hi], x[lo], scalar, sin[lo], ALU.mult, ALU.mult))
                return v.tensor_tensor(dst, A, B, ALU.add)

            mla_split_low(dve, v, 3)
            dve.wait_ge(sem["tab_cos"], 1)
            rt = (rtmp[:, 0, :], rtmp[:, 1, :])
            rope(kpT, kpT, tabM[:, 0, :], tabM[:, 1, :], 32, rt).then_inc(sem["rope_done"], 1)
            dve.wait_ge(sem["rope_done"], 1)
            v.tensor_copy(kz[64:128], kpT[64:128]).then_inc(sem["kz_ready"], 1)
            v.memset(kz[0:64], 0.0).then_inc(sem["kz_ready"], 1)
            dve.wait_ge(sem["kz_ready"], 1)
            v.memset(kpT[64:128], 0.0).then_inc(sem["kz_ready"], 1)
            mla_split_low(dve, v, 4)
            mla_split_low(dve, v, 5)
            for j in range(2):
                if j == 1:
                    for n in range(6, 8):
                        mla_split_low(dve, v, n)
                dve.wait_ge(sem["q_done"], 3 * j + 3)
                dve.wait_ge(sem["rope_done"], j + 1)
                rope(qpT[:, j, :], bank[(3 * j + 2) % 4][:, :], tabM[:, 0, :], tabM[:, 1, :], 32, rt).then_inc(sem["rope_done"], 1)
            modulation1()
            for f in range(4):
                dve.wait_ge(sem["y_hi"], f + 1)
                v.tensor_tensor(cqr[:, f, :], yT[:, f, :], hTr[:, f, :].bitcast(F32), ALU.subtract).then_inc(sem["y_lo"], 1)
            for n in range(8, 10):
                mla_split_low(dve, v, n)
            dve.wait_ge(sem["z_pool"], 4)
            for f in range(4):
                dve.wait_ge(sem["glu_act"], f + 1)
                link(v.scalar_tensor_tensor(y2[:, f, :], y2[:, f, :], 1.0, yT[:, f, :], ALU.add, ALU.mult))
                v.scalar_tensor_tensor(mixT[:, f, :].rearrange("p (c s) -> p s c", s=L), y2[:, f, :].rearrange("p (s c) -> p s c", s=L),
                                       0.125, zaT[:, f, :].rearrange("p (c s) -> p s c", s=L), ALU.mult, ALU.mult).then_inc(sem["ya_ready"], 1)

            def mix_low(l, f, mix):
                dve.wait_ge(sem["mix_hi"], 8 * l + f + 1)
                v.tensor_tensor(mixr[l][:, f, :], mix[:, f, :], hTr[:, f, :].bitcast(F32), ALU.subtract).then_inc(sem["mix_lo"], 1)

            def attend(l, units, n0, Pb, PTb, nP, heads, mix, z, gated):
                N, per = len(units), len(units) // heads
                f0 = (4, 0)[l]
                for n in range(N + 6):
                    if l == 0 and 4 <= n < 8:
                        mix_low(0, n - 4, mix)
                    if l == 0 and n == 9:
                        split_low(dve, v, SPLIT[0])
                    if n >= 7 and (n - 6) % per == 0:
                        mix_low(l, (n - 6) // per - 1 + f0, mix)
                    if n < N:
                        w = P * (units[n][1] + 1)
                        dve.wait_ge(sem["s_done"], n0 + n + 1)
                        v.reduce_max(smax[:, n % 4:n % 4 + 1], bank[SB[n % 3]][:, 0:w], AX.X, negate=True).then_inc(sem["s_max"], 1)
                    m = n - 1
                    if 0 <= m < N:
                        h, i, b = units[m]
                        w = P * (i + 1)
                        dve.wait_ge(sem["s_exp"], n0 + m + 1)
                        link(v.reciprocal(srec[:, m % 4:m % 4 + 1], ssum[:, m % 4:m % 4 + 1]))
                        pb = Pb[:, m % nP, 0:w]
                        if gated:
                            v.tensor_scalar(pb, pb, srec[:, m % 4:m % 4 + 1], gates[:, i, 3 * h + b + 1:3 * h + b + 2], ALU.mult, ALU.mult).then_inc(sem["s_scaled"], 1)
                        else:
                            v.tensor_scalar(pb, pb, srec[:, m % 4:m % 4 + 1], None, ALU.mult).then_inc(sem["s_scaled"], 1)
                    m = n - 2
                    if 0 <= m < N and m % 2 == 1:
                        w = P * (units[m][1] + 1)
                        dve.wait_ge(sem["pt_done"], n0 + m + 1)
                        if m >= 2:
                            dve.wait_ge(sem["pv_done"], n0 + m - 1)
                        v.tensor_copy(PTb[:, m % 2, 0:w], bank[TB[m % 2]][:, 0:w]).then_inc(sem["pt_dve"], 1)
                    m = n - 4
                    if 0 <= m < N and (m + 1) % per == 0:
                        h = m // per
                        if h == 0:
                            dve.wait_ge(sem["z_pool"], 8 * (l + 1))
                        dve.wait_ge(sem["pv_done"], n0 + m + 1)
                        v.scalar_tensor_tensor(mix[:, f0 + h, :], bank[OB[h % 2]][:, :], 0.5, z[:, h, :], ALU.mult, ALU.mult).then_inc(sem["o_dve"], 1)

            attend(0, U0, 0, Pm, PT, 3, MH, mixT, zbT, False)
            mix_low(0, 7, mixT)
            for n in range(1, 5):
                split_low(dve, v, SPLIT[n])

            def output(l, tmp):
                for i in range(NT):
                    dve.wait_ge(sem["out_sq"], 2 * NT * l + NT + i + 1)
                    link(v.tensor_tensor(mso[:, i:i + 1], sso[:, i:i + 1], sso[:, NT + i:NT + i + 1], ALU.add))
                    v.tensor_scalar(mso[:, i:i + 1], mso[:, i:i + 1], 1.0 / D, EPS, ALU.mult, ALU.add).then_inc(sem["out_msq"], 1)
                    dve.wait_ge(sem["gpg_ready"], 2 * (l + 1))
                    dve.wait_ge(sem["out_rstd"], NT * l + i + 1)
                    if i >= 2:
                        dve.wait_ge(sem["out_res"], 2 * (NT * l + i - 1))
                    v.scalar_tensor_tensor(tmp[:, i % 2, 0:512], bank[2 * i][:, :], rso[:, i:i + 1], gpg[:, 0:512], ALU.mult, ALU.mult).then_inc(sem["out_gpg"], 1)
                    v.scalar_tensor_tensor(tmp[:, i % 2, 512:], bank[2 * i + 1][:, :], rso[:, i:i + 1], gpg[:, 512:], ALU.mult, ALU.mult).then_inc(sem["out_gpg"], 1)
                    dve.wait_ge(sem["out_gpg"], 2 * (NT * l + i + 1))
                    if l == 0 and i == 0:
                        dve.wait_ge(sem["x_loaded"], 32)
                    v.tensor_tensor(xr[:, i, 512:], xr[:, i, 512:], tmp[:, i % 2, 512:], ALU.add).then_inc(sem["out_res"], 1)
                    if l == 0 and i >= 2:
                        mean_square(1, i - 2)

            output(0, otmp)
            normalise(1, 0, xn1)
            mean_square(1, 2)
            normalise(1, 1, xn1)
            mean_square(1, 3)
            normalise(1, 2, xn1)
            normalise(1, 3, xn1)
            hT_tiles(1)
            split_low(dve, v, SPLIT[5])
            dve.wait_ge(sem["gate_w"], 1)
            v.tensor_tensor(wgater[:], wgate[:], wgate_hi[:].bitcast(F32), ALU.subtract).then_inc(sem["gate_w"], 1)
            dve.wait_ge(sem["pos_loaded"], 32)
            ang = th1[:, 0, :]
            link(v.tensor_copy(rt1[:, 1, :], ang.bitcast(I32)))
            link(v.tensor_scalar(ang, rt1[:, 1, :], cst[:, 0:1], None, ALU.mult))
            reduce_angle(rt1[:, 1, :], rt1[:, 0, :], ang, rt1[:, 1, :]).then_inc(sem["tab_abs"], 1)
            dve.wait_ge(sem["tab_cos"], 2)
            link(v.tensor_scalar(tabN[:, 2:4, :].rearrange("p a n -> p (a n)"), tabN[:, 0:2, :].rearrange("p a n -> p (a n)"), NSCALE, None, ALU.mult))
            n0 = len(PJ0)
            rt = (rt1[:, 0, :], rt1[:, 1, :])
            for n, tile in enumerate(PJ1):
                kind, b = tile[0], bank[n % 4]
                if kind != "z" and next_split(n):
                    split_low(dve, v, next_split(n))
                if tile[0] == "q" and tile[1] in (1, 2):
                    b2 = tile[1] - 1
                    dve.wait_ge(sem["R_hi"], b2 + 1)
                    v.tensor_tensor(Rr[:, b2, :], R[b2].rearrange("p l g n -> p (l g n)"), R_high[:, b2, :].bitcast(F32), ALU.subtract).then_inc(sem["R_lo"], 1)
                if kind in ("cmp", "k", "q"):
                    dve.wait_ge(sem["pj_done"], n0 + n + 1)
                if kind == "cmp":
                    kv, gg = tile[1:]
                    for e in range(2):
                        ins = v.tensor_tensor(R[kv][:, CS * e:CS * e + CS, gg, :],
                                              b[:, CS * e:CS * e + CS * NCMP].rearrange("p (n l) -> p l n", l=CS),
                                              peT[:, CL * kv + CS * e:CL * kv + CS * e + CS].unsqueeze(2).to_broadcast([P, CS, NCMP]), ALU.add)
                        ins.then_inc(sem["kc_ready"], 1)
                elif kind == "k":
                    rope((ksT, kwT)[tile[1]][:, tile[2], :], b[:, :], tabN[:, 2, :], tabN[:, 3, :], 64, rt).then_inc(sem["rope1"], 1)
                    dve.wait_ge(sem["rope1"], sum(x[0] in ("k", "q") for x in PJ1[:n + 1]))
                elif kind == "q":
                    rope(qT[:, tile[1], :], b[:, :], tabN[:, 0, :], tabN[:, 1, :], 64, rt).then_inc(sem["rope1"], 1)
                    dve.wait_ge(sem["rope1"], sum(x[0] in ("k", "q") for x in PJ1[:n + 1]))
            for key in SPLIT[sorder[("w1", 0, 1)]:sorder[("z", 0)] + 1]:
                split_low(dve, v, key)
            dve.wait_ge(sem["gT_done"], 1)
            v.tensor_scalar(gates.rearrange("p i n -> p (i n)"), bank[6][:, 0:NT * 3 * HN], 0.5, 0.5, ALU.mult, ALU.add).then_inc(sem["gate_ready"], 1)
            for b in range(2):
                dve.wait_ge(sem["hid_sq"], 2 * (b + 1))
                hv, qv = hid[b][0:NB], hsq[b][0:NB]
                link(v.tensor_scalar(qv, qv, 0.044715, 1.0, ALU.mult, ALU.add))
                v.tensor_tensor(qv, qv, hv, ALU.mult).then_inc(sem["hid_arg"], 1)
            for b in range(2):
                hv, qv = hid[b][0:NB], hsq[b][0:NB]
                dve.wait_ge(sem["hid_tanh"], b + 1)
                v.scalar_tensor_tensor(hv, qv, 1.0, hv, ALU.add, ALU.mult).then_inc(sem["hid_ready"], 1)
            split_low(dve, v, ("z", 1))
            split_low(dve, v, ("z", 2))
            dve.wait_ge(sem["cmp_done"], 1)
            ends = lambda j: tabN[:, j, CL - 1:CL - 1 + CS * (NCMP - 1) + 1:CS].unsqueeze(1).to_broadcast([P, GN, NCMP])
            kx = bank[4][:, 0:62].rearrange("p (g n) -> p g n", g=GN)
            rope(kcT, kx, ends(2), ends(3), 64, tuple(kct[:, j, :].rearrange("p (g n) -> p g n", g=GN) for j in range(2)), 0.5).then_inc(sem["cmp_rope"], 1)
            split_low(dve, v, ("z", 3))
            dve.wait_ge(sem["gate_ready"], 1)
            for b in range(GN):
                pc4 = Pc[b].rearrange("p (r i) n -> p r i n", r=REP)
                ng, sm_, rr = cstat[:, 0, :], cstat[:, 1, :], cstat[:, 2, :]
                dve.wait_ge(sem["cs_done"], b + 1)
                link(v.tensor_tensor(pc4, bank[6 + b][:, 0:496].rearrange("p (r i n) -> p r i n", r=REP, i=NT),
                                     cmpmask[:].unsqueeze(1).to_broadcast([P, REP, NT, NCMP]), ALU.add))
                link(v.reduce_max(ng, Pc[b], AX.X, negate=True))
                v.tensor_tensor(Pc[b], Pc[b], ng.unsqueeze(2).to_broadcast([P, 16, NCMP]), ALU.add).then_inc(sem["cs_sub"], 1)
                dve.wait_ge(sem["cs_exp"], b + 1)
                link(v.reduce_sum(sm_, Pc[b], AX.X))
                link(v.tensor_scalar(sm_, sm_, TINY, None, ALU.max))
                link(v.reciprocal(rr, sm_))
                r4 = rr.rearrange("p (r i) -> p r i", r=REP)
                link(v.tensor_tensor(r4, r4, valid[:].unsqueeze(1).to_broadcast([P, REP, NT]), ALU.mult))
                gt = gates[:, :, 3 * REP * b:3 * REP * (b + 1):3].rearrange("p i r -> p r i")
                link(v.tensor_tensor(r4, r4, gt, ALU.mult))
                v.tensor_tensor(Pc[b], Pc[b], rr.unsqueeze(2).to_broadcast([P, 16, NCMP]), ALU.mult).then_inc(sem["cs_scaled"], 1)
            split_low(dve, v, ("wout1", 0))
            attend(1, U1, N0, Pm1, PT1, 3, HN, mix1, zT, True)
            mix_low(1, 7, mix1)
            for j in range(1, 4):
                split_low(dve, v, ("wout1", j))
            output(1, otmp1)

        @block.tensor
        def _(pe):
            m = nc.tensor
            pe.wait_ge(sem["ident_ready"], 2)
            pe.wait_ge(sem["c_loaded"], 16)
            m.transpose(bank[0][:, 0:KD], rows[0:KD, :], ident[0:KD, 0:KD]).then_inc(sem["colT_done"], 1)

            def mod_row(d):
                if d >= 2:
                    pe.wait_ge(sem["mrow_act"], d - 1)
                for j in (2 * d, 2 * d + 1):
                    key = ("ada", 0, j)
                    w_ready(pe, key)
                    for k in range(KD):
                        ins = m.matmul(bank[7 * (d % 2)][0:1, 256 * (j % 2):256 * (j % 2) + 256], sc[:, k:k + 1], slot(key)[:, k, :],
                                       start=k == 0, stop=k == KD - 1)
                    ins.then_inc(sem["mod_done"], 1)

            def mod_cols(d):
                pe.wait_ge(sem["mrow_act"], d + 1)
                for f in range(4):
                    ins = m.transpose(bank[1][:, 4 * d + f:4 * d + f + 1], mrow[0:1, d % 2, P * f:P * f + P], ident[0:1, 0:1])
                ins.then_inc(sem["mcol_done"], 1)

            pe.wait_ge(sem["sc_ready"], 2)
            mod_row(0)
            for d in range(1, R0):
                mod_row(d)
                mod_cols(d - 1)
                if d == 1:
                    pe.wait_ge(sem["vec_loaded"], 144)
                    m.transpose(bank[6][:, 0:V_N], rows[0:V_N, :], ident[0:V_N, 0:V_N]).then_inc(sem["colT_done"], 1)
                    m.transpose(bank[6][:, 128:192], perows[:, :], ident[0:64, 0:64]).then_inc(sem["colT_done"], 1)
            pe.wait_ge(sem["pw_ready"], 1)
            for j in range(NPW):
                ins = m.transpose(bank[2 + j // 16][0:64, 32 * (j % 16):32 * (j % 16) + 32], small[0:32, j, :], ident[0:32, 0:32])
                if j % 16 == 15 or j == NPW - 1:
                    ins.then_inc(sem["stT_done"], 1)
            pe.wait_ge(sem["s5_loaded"], 64)
            pe.wait_ge(sem["col_ready"], 2)
            for f in range(4):
                ins = m.transpose(bank[6][:, P * f:P * f + P], CN[:, f, :], ident[:])
            ins.then_inc(sem["CT_done"], 1)
            pe.wait_ge(sem["st_act"], 4)
            m.matmul(bank[2][:, :], swap[:], BA.rearrange("p g h -> p (g h)"), start=True, stop=True).then_inc(sem["BB_done"], 1)
            pe.wait_ge(sem["C_act"], 2)
            m.matmul(bank[3][:, :], swap[:], C1.rearrange("p g h -> p (g h)"), start=True, stop=True).then_inc(sem["CT_done"], 1)
            for d in range(R0, 6):
                mod_row(d)
                mod_cols(d - 1)
            mod_cols(5)

            def gate_rows(l):
                pe.wait_ge(sem["mod_ready"], 3 + 3 * l)
                if l == 0:
                    pe.wait_ge(sem["C_act"], 3)
                else:
                    pe.wait_ge(sem["out_gpg"], 2 * NT)
                for k in range(KD):
                    ins = m.matmul(bank[6 + k // 4][:, P * (k % 4):P * (k % 4) + P], gcol[:, l, k:k + 1].to_broadcast([P, P]), ident[:], start=True, stop=True)
                    if k % 4 == 3:
                        ins.then_inc(sem["gpg_done"], 1)

            def x_transposes(l, src):
                for k in range(KD):
                    if l == 0 and k == 0:
                        pe.wait_ge(sem["B_ready"], 1)
                        pe.wait_ge(sem["st_act"], 4)
                    if l == 0 and k == 1:
                        pe.wait_ge(sem["mod_ready"], 1)
                    if l == 1 and k == 0:
                        pe.wait_ge(sem["out_gpg"], 4)
                    if k >= 4 and k % 2 == 0:
                        pe.wait_ge(sem["hT_act"], 4 * l + (k - 4) // 2 + 1)
                    if k >= 4 and k % 2 == 1:
                        pe.wait_ge(sem["hT_dve"], 4 * l + (k - 5) // 2 + 1)
                    for i in range(NT):
                        if k == 0:
                            pe.wait_ge(sem["xn_ready"], NT * l + i + 1)
                        ins = m.transpose(bank[k % 4][:, P * i:P * i + P], src[:, i, P * k:P * k + P], ident[:])
                    ins.then_inc(sem["xT_done"], 1)

            def h_ready(l):
                pe.wait_ge(sem["hT_act"], 4 * (l + 1))
                pe.wait_ge(sem["hT_dve"], 4 * (l + 1))

            gate_rows(0)
            x_transposes(0, xr)
            h_ready(0)

            def f_tile(b, w, c0, rhs=hT, nk=KD):
                for k in range(nk):
                    ins = m.matmul(b[:, :], w[:, k, c0:c0 + P], rhs[:, k, :], start=k == 0, stop=k == nk - 1)
                return ins

            def t_tile(b, w, i, n):
                for k in range(KD):
                    ins = m.matmul(b, hT[:, k, P * i:P * i + P], w[:, k, 0:n], start=k == 0, stop=k == KD - 1)
                return ins

            def three(dst, ah, al, bh, bl, start, stop):
                m.matmul(dst, ah, bh, start=start, stop=False)
                m.matmul(dst, ah, bl, start=False, stop=False)
                return m.matmul(dst, al, bh, start=False, stop=stop)

            def s5_transposes(b0):
                for b in range(b0, b0 + 4):
                    if b % 2 == 0:
                        pe.wait_ge(sem["G_ready"], b // 2 + 1)
                    if b == 0:
                        pe.wait_ge(sem["st_act"], 8)
                        pe.wait_ge(sem["gpg_ready"], 2)
                    if b >= 4:
                        pe.wait_ge(sem["GT_act"], b - 3)
                    for g in range(4):
                        ins = m.transpose(bank[4 + b % 4][:, P * g:P * g + P], Gc[(b // 2) % 2][:, 4 * (b % 2) + g, :], ident[:])
                    ins.then_inc(sem["GT_done"], 1)

            def s5_kernels(b0):
                for b in range(b0, b0 + 4):
                    pe.wait_ge(sem["W1_ready"], b // 2 + 1)
                    pe.wait_ge(sem["GT_act"], min(8, b + 5))
                    if b >= 4:
                        pe.wait_ge(sem["Kc_act"], b - 3)
                    for g in range(4):
                        ins = m.matmul(bank[4 + b % 4][0:NH, P * g:P * g + P], Bb[:, 4 * b + g, :], W1[:, 4 * b + g, 0:L * NH], start=True, stop=True)
                    ins.then_inc(sem["Kc_done"], 1)

            def s5_states():
                pe.wait_ge(sem["u_back"], 16 * L)
                pe.wait_ge(sem["GT_act"], 8)
                pe.wait_ge(sem["Kc_act"], 8)
                for b in range(4):
                    for g in range(8):
                        ins = m.matmul(bank[4 + b][:, NC * g:NC * g + NC], GT[:, 8 * b + g, :], U[:, 8 * b + g, :], start=True, stop=True)
                    ins.then_inc(sem["V_done"], 1)

            def s5_outputs():
                pe.wait_ge(sem["T_stored"], 32 * L)
                pe.wait_ge(sem["zero_ready"], 1)
                for b in range(8):
                    pe.wait_ge(sem["Xs_ready"], b // 4 + 1)
                    if b % 4 >= 2:
                        pe.wait_ge(sem["Y_act"], b - 1)
                    for g in range(4):
                        gg = 4 * b + g
                        dst = bank[4 + 2 * (b // 4) + b % 2][0:NC, P * g:P * g + P]
                        m.matmul(dst, Xs[:, gg % 16, 0:NC], W1[:, gg, NH:], start=True, stop=False)
                        ins = m.matmul(dst, U[:, gg, :], TP[:, gg, :], start=False, stop=True)
                    ins.then_inc(sem["Y_done"], 1)

            def s5_features():
                pe.wait_ge(sem["Y_act"], 8)
                for f in range(4):
                    for s in range(L):
                        ins = m.transpose(bank[4 + f][:, NC * s:NC * s + NC], Yc[:, s, P * f:P * f + P], ident[0:NC, 0:NC])
                    ins.then_inc(sem["YT_done"], 1)

            def pj_free(n):
                if n >= 4:
                    kinds = [x[0] for x in PJ0[:n - 3]]
                    nz = sum(x in ("za", "zb") for x in kinds)
                    last = PJ0[n - 4][0]
                    if last in ("za", "zb"):
                        pe.wait_ge(sem["th_act"], nz)
                    else:
                        pe.wait_ge(sem["pj_act"], evac0[n - 4])

            for n, tile in enumerate(PJ0):
                pj_free(n)
                b = bank[n % 4]
                if tile[0] == "u":
                    f = tile[1]
                    w_ready(pe, ("u", f // 2))
                    ins = f_tile(b, slot(("u", f // 2)), P * (f % 2))
                elif tile[0] == "cq":
                    j, i = tile[1:]
                    w_ready(pe, ("cq", j))
                    ins = t_tile(b[:, 0:256], slot(("cq", j)), i, 256)
                elif tile[0] == "ms":
                    pe.wait_ge(sem["macc_done"], 2 * tile[1] + 2)
                    for f in range(4):
                        ins = m.matmul(b[:, P * f:P * f + P], macc[tile[1]][:, f // 2, P * (f % 2):P * (f % 2) + P], ones[:], start=True, stop=True)
                elif tile[0] == "kpe":
                    pe.wait_ge(sem["small_w_loaded"], 80)
                    ins = f_tile(b, wkpe, 0)
                else:
                    f = tile[1]
                    w_ready(pe, (tile[0], f // 2))
                    ins = f_tile(b, slot((tile[0], f // 2)), P * (f % 2))
                ins.then_inc(sem["pj_done"], 1)
                if tile[0] == "cq" and tile[2] == NT - 1:
                    (s5_transposes, s5_kernels)[tile[1] // 2](4 * (tile[1] % 2))
                if tile == ("za", 1):
                    s5_states()
                if tile == ("za", 3):
                    s5_outputs()
                if tile == ("zb", 0):
                    s5_features()

            pe.wait_ge(sem["cq_scaled"], 2 * NT)
            pe.wait_ge(sem["y_skip"], 4)
            for f in range(8):
                if f >= 4:
                    pe.wait_ge(sem["cq_lo"], f - 3)
                for i in range(NT):
                    ins = m.transpose(bank[4 + f % 4][:, P * i:P * i + P], cqt[:, i, P * f:P * f + P], ident[:])
                ins.then_inc(sem["cqT_done"], 1)
            pe.wait_ge(sem["th_act"], 8)
            for n, key in enumerate(QT):
                if n >= 4:
                    pe.wait_ge(sem["q_act"], n - 3)
                pe.wait_ge(sem["mw_lo"], n + 1)
                for k in range(6):
                    if n == 0:
                        pe.wait_ge(sem["cq_lo"], k + 1)
                    ins = three(bank[n % 4][:, :], mhi(n)[:, k, :], lo(key)[:, k, :], hTr[:, k, :], cqr[:, k, :], k == 0, k == 5)
                ins.then_inc(sem["q_done"], 1)
            pe.wait_ge(sem["mw_lo"], 8)
            pe.wait_ge(sem["cq_lo"], 8)
            for n in range(8):
                if n >= 4:
                    pe.wait_ge(sem["kv_act"], n - 3)
                for k in range(2):
                    wh, wl = mhi(6 + k)[:, 0, :], lo(("ukv", 0))[:, k, :]
                    ch, cl = hTr[:, 6 + k, :], cqr[:, 6 + k, :]
                    if n < 4:
                        fs = slice(256 * n, 256 * n + P)
                        ins = three(bank[4 + n % 4][:, :], wh[:, fs], wl[:, fs], ch, cl, k == 0, k == 1)
                    else:
                        ts = slice(P * (n - 4), P * (n - 4) + P)
                        wvh, wvl = (x.rearrange("p (h x) -> p h x", h=MH)[:, :, NOPE:] for x in (wh, wl))
                        ins = three(bank[4 + n % 4][:, :], ch[:, ts], cl[:, ts], wvh, wvl, k == 0, k == 1)
                ins.then_inc(sem["kv_done"], 1)

            pe.wait_ge(sem["q_act"], 4)
            pe.wait_ge(sem["rope_done"], 3)
            pe.wait_ge(sem["y_lo"], 4)
            for f in range(4):
                n, fs = 8 + f // 2, slice(P * (f % 2), P * (f % 2) + P)
                pe.wait_ge(sem["mw_lo"], n + 1)
                for k in range(4):
                    ins = three(bank[f][:, :], mhi(n)[:, k, fs], lo(("glu", f // 2))[:, k, fs], hTr[:, k, :], cqr[:, k, :], k == 0, k == 3)
                ins.then_inc(sem["glu_done"], 1)

            def attend(units, n0, scores, Pb, PTb, heads, h0, values, extra):
                N, per = len(units), len(units) // heads

                def evacuated(m_):
                    pe.wait_ge(sem[("pt_act", "pt_dve")[m_ % 2]], n0 // 2 + m_ // 2 + 1)

                for n in range(N + 3):
                    if n < N:
                        h, i, b = units[n]
                        if n >= 3:
                            pe.wait_ge(sem["s_exp"], n0 + n - 2)
                        w = P * (i + 1)
                        sb_ = bank[SB[n % 3]]
                        scores(sb_, h, i, b, w)
                        m.matmul(sb_[:, P * i:w], identb[:], cmaskb[:], start=False, stop=True).then_inc(sem["s_done"], 1)
                    u = n - 2
                    if 0 <= u < N:
                        pe.wait_ge(sem["s_scaled"], n0 + u + 1)
                        if u >= 2:
                            evacuated(u - 2)
                        for j in range(units[u][1] + 1):
                            ins = m.transpose(bank[TB[u % 2]][:, P * j:P * j + P], Pb[:, u % 3, P * j:P * j + P], ident[:])
                        ins.then_inc(sem["pt_done"], 1)
                    u = n - 3
                    if u >= 0:
                        h, i, b = units[u]
                        evacuated(u)
                        if u % per == 0 and h >= 2:
                            pe.wait_ge(sem["o_dve"], h0 + h - 1)
                        dst = bank[OB[h % 2]][:, P * i:P * i + P]
                        first = b == 0
                        if extra is not None and b == 0:
                            extra(dst, h, i)
                            first = False
                        last_b = extra is None or b == 1
                        for j in range(i + 1):
                            ins = m.matmul(dst, values(h, b, j), PTb[:, u % 2, P * j:P * j + P], start=first and j == 0, stop=last_b and j == i)
                        ins.then_inc(sem["pv_done"], 1)

            def scores0(dst, h, i, b, w):
                m.matmul(dst[:, 0:w], qnT[:, h, P * i:P * i + P], knT[:, h, 0:w], start=True, stop=False)
                m.matmul(dst[:, 0:w], qpT[:, h // 2, P * i:P * i + P], (kpT, kz)[h % 2][:, 0:w], start=False, stop=False)

            pe.wait_ge(sem["masks_ready"], 6)
            pe.wait_ge(sem["q_act"], 4)
            pe.wait_ge(sem["kv_act"], 8)
            pe.wait_ge(sem["rope_done"], 3)
            pe.wait_ge(sem["kz_ready"], 3)
            pe.wait_ge(sem["glu_act"], 4)
            attend(U0, 0, scores0, Pm, PT, MH, 0, lambda h, b, j: vM[:, j, P * h:P * h + P], None)

            def output(l):
                for j in range(4):
                    key = (f"wout{l}", j)
                    pe.wait_ge(sem["w_lo"], 2 * sorder[key] + 2)
                    for ks in ([range(KD - 1), range(KD - 1, KD)] if j == 0 else [range(KD)]):
                        if j == 0:
                            pe.wait_ge(sem["mix_lo"], 8 * l + ks[-1] + 1)
                        if j == 0 and ks[0] == 0:
                            pe.wait_ge(sem["o_dve"], (MH, MH + HN)[l])
                        for i in range(NT):
                            for k in ks:
                                ts = slice(P * i, P * i + P)
                                ins = three(bank[2 * i + j // 2][:, 256 * (j % 2):256 * (j % 2) + 256], hTr[:, k, ts], mixr[l][:, k, ts],
                                            hi(key)[:, k, :], lo(key)[:, k, :], k == 0, k == KD - 1)
                            if j == 3:
                                ins.then_inc(sem["out_done"], 1)
                            elif j == 1 and i == NT - 1:
                                ins.then_inc(sem["out_half"], 1)
                    if j in (0, 2):
                        ins.then_inc(sem["wo_used"], 1)

            output(0)

            gate_rows(1)
            x_transposes(1, xn1)

            def pj1_free(n):
                if n < 4:
                    pe.wait_ge(sem[("hT_act", "hT_dve")[n % 2]], 4 + n // 2 + 3)
                    return
                done = PJ1[:n - 3]
                kind = PJ1[n - 4][0]
                count = sum(x[0] == kind for x in done)
                if kind == "cmp":
                    pe.wait_ge(sem["kc_ready"], 2 * count)
                elif kind in ("k", "q"):
                    pe.wait_ge(sem["rope1"], sum(x[0] in ("k", "q") for x in done))
                elif kind == "v":
                    pe.wait_ge(sem["v_act"], count)
                elif kind == "gate":
                    pe.wait_ge(sem["gate_act"], 1)
                else:
                    pe.wait_ge(sem["th_act"], 8 + count)

            def hidden():
                for b in range(2):
                    pe.wait_ge(sem["R_lo"], b + 1)
                    for j in range(4):
                        key = ("w1", b, j)
                        pe.wait_ge(sem["w_lo"], 2 * sorder[key] + 2)
                        for l in range(8):
                            ls = slice(NB * (8 * j + l), NB * (8 * j + l) + NB)
                            ins = three(bank[4 + b][0:NB, 0:CH], R_high[:, b, ls], Rr[:, b, ls],
                                        hi(key)[:, l, :], lo(key)[:, l, :], j + l == 0, j == 3 and l == 7)
                        if j < 3:
                            ins.then_inc(sem["w1_used"], 1)
                    ins.then_inc(sem["hid_done"], 1)

            def compressed():
                pe.wait_ge(sem["small_w_loaded"], 80)
                for b in range(2):
                    pe.wait_ge(sem["hid_ready"], b + 1)
                    for e in range(2):
                        ins = m.transpose(bank[6 + b][:, 64 * e:64 * e + NB], hid[b][0:NB, e, :], ident[0:NB, 0:NB])
                    ins.then_inc(sem["hidT_done"], 1)
                pe.wait_ge(sem["hidT_act"], 2)
                for e in range(2):
                    ins = m.matmul(bank[4][:, 0:NB], w2[:, 0, e, :], hidT[0][:, e, :], start=e == 0, stop=e == 1)
                ins.then_inc(sem["cmp_done"], 1)
                for g in range(GN):
                    for e in range(2):
                        ins = m.matmul(bank[5][0:NCMP, DN * g:DN * g + DN], hidT[1][:, e, NCMP * g:NCMP * g + NCMP], w2[:, 1, e, :],
                                       start=e == 0, stop=e == 1)
                ins.then_inc(sem["cmp_done"], 1)

            def compressed_scores():
                pe.wait_ge(sem["cmp_rope"], 1)
                pe.wait_ge(sem["rope1"], 12)
                for g in range(GN):
                    for r in range(REP):
                        for i in range(NT):
                            c0 = NCMP * (NT * r + i)
                            ins = m.matmul(bank[6 + g][:, c0:c0 + NCMP], qT[:, REP * g + r, P * i:P * i + P], kcT[:, g, :], start=True, stop=True)
                    ins.then_inc(sem["cs_done"], 1)

            def compressed_transposes(g):
                pe.wait_ge(sem["cs_scaled"], g + 1)
                pe.wait_ge(sem["cmp_act"], 1)
                for h in range(REP * g, REP * g + REP):
                    if h >= 2:
                        pe.wait_ge(sem["cpt_act"], h - 1)
                    for i in range(NT):
                        ins = m.transpose(bank[4 + h % 2][0:NCMP, P * i:P * i + P], Pc[g][:, NT * (h % REP) + i, :], ident[:])
                    ins.then_inc(sem["cpt_done"], 1)

            for n, tile in enumerate(PJ1):
                if tile in (("z", 6), ("z", 7)):
                    compressed_transposes(tile[1] - 6)
                if tile == ("z", 0):
                    hidden()
                    pe.wait_ge(sem["gate_act"], 1)
                    for i in range(NT):
                        ins = m.transpose(bank[6][:, 24 * i:24 * i + 24], gT[0:24, P * i:P * i + P], ident[0:24, 0:24])
                    ins.then_inc(sem["gT_done"], 1)
                if tile == ("z", 3):
                    pe.wait_ge(sem["gate_ready"], 1)
                    compressed()
                if tile == ("z", 5):
                    compressed_scores()
                pj1_free(n)
                kind, b = tile[0], bank[n % 4]
                if kind == "gate":
                    pe.wait_ge(sem["gate_w"], 2)
                else:
                    key = weights1(tile)
                    pe.wait_ge(sem["w_lo"], 2 * sorder[key] + 2)
                for k in range(KD):
                    if n == 0:
                        pe.wait_ge(sem["h_lo"], k + 1)
                    first, last = k == 0, k == KD - 1
                    if kind == "gate":
                        ins = three(b[0:3 * HN, :], wgate_hi[:, k, :], wgater[:, k, :], hTr[:, k, :], hlo1r[:, k, :], first, last)
                    elif kind == "v":
                        ts = slice(P * tile[2], P * tile[2] + P)
                        ins = three(b[:, 0:256], hTr[:, k, ts], hlo1r[:, k, ts], hi(key)[:, k, :], lo(key)[:, k, :], first, last)
                    else:
                        fs = slice(P * (tile[-1] % 2), P * (tile[-1] % 2) + P)
                        ins = three(b[:, :], hi(key)[:, k, fs], lo(key)[:, k, fs], hTr[:, k, :], hlo1r[:, k, :], first, last)
                ins.then_inc(sem["pj_done"], 1)
            def scores1(dst, h, i, b, w):
                m.matmul(dst[:, 0:w], qT[:, h, P * i:P * i + P], (ksT, kwT)[b][:, h // REP, 0:w], start=True, stop=False)

            def extra(dst, h, i):
                m.matmul(dst, vc[:, h // REP, :], PcT[:, h, P * i:P * i + P], start=True, stop=False)

            pe.wait_ge(sem["v_act"], 8)
            pe.wait_ge(sem["cmp_act"], 1)
            pe.wait_ge(sem["cpt_act"], HN)
            attend(U1, N0, scores1, Pm1, PT1, HN, MH, lambda h, b, j: (vs, vw)[b][:, j, DN * (h // REP):DN * (h // REP) + DN], extra)
            output(1)


_INS = ['x', 'c', 'positions', 'pre_norm_g', 'post_norm_g', 'w_ada', 'b_ada', 'ev_w_in', 'ev_lam_re', 'ev_lam_im', 'ev_log_dt',
        'ev_b_re', 'ev_b_im', 'ev_c_re', 'ev_c_im', 'ev_d_skip', 'ev_w_glu', 'ev_b_glu', 'ev_q_norm_g', 'ev_kv_norm_g', 'ev_w_uq',
        'ev_w_ukv', 'ev_w_out', 'od_w_in', 'od_cmp_k_pe', 'od_cmp_k_w1', 'od_cmp_k_w2', 'od_cmp_v_pe', 'od_cmp_v_w1', 'od_cmp_v_w2',
        'od_w_out']


def _constants():
    f = np.float32
    half_n, half_m = DN // 2, RO // 2
    inv = lambda half: (f(10000.0) ** (-np.arange(half, dtype=f) / f(half))).astype(f)
    p = np.arange(P)
    return np.stack([inv(half_n)[p % half_n], inv(half_m)[p % half_m], np.where(p < half_n, f(1), f(-1)),
                     np.where(p % RO < half_m, f(1), f(-1))], axis=1).astype(f)


def kernel(**inputs):
    import numpy as _np
    import concourse.bacc as _bacc
    from concourse import mybir as _mybir
    from concourse.bass_utils import run_bass_kernel_spmd as _run

    nc = _bacc.Bacc("TRN2", target_bir_lowering=False, num_devices=1)
    arrays, t = {}, {}
    for name in _INS:
        a = _np.ascontiguousarray(inputs[name])
        arrays[f"in_{name}"] = a
        t[name] = nc.dram_tensor(f"in_{name}", a.shape, _mybir.dt.from_np(a.dtype), kind="ExternalInput").ap()
    arrays["in_cst"] = _constants()
    t["cst"] = nc.dram_tensor("in_cst", (P, 4), F32, kind="ExternalInput").ap()
    t["out"] = nc.dram_tensor("out_0", (1, S, D), F32, kind="ExternalOutput").ap()
    build_trunk(nc, t)
    r = _run(nc, [arrays], core_ids=[0])
    return r.results[0]["out_0"]
```
